# Optimizing a Trainium2 kernel written in Bass

```python
import math
import jax, jax.numpy as jnp
from jax import lax
import numpy as np

D_MODEL = 1024
BATCH = 1
SEQ = 256
DEPTH = 2

CTX_LEN = 256
GRID_W = 64
N_MIXERS = 4
ALPHA = (2 * DEPTH) ** 0.25
BETA = (8 * DEPTH) ** -0.25
LN_EPS = 1e-5
ATT_HEADS = 8
ATT_HEAD_DIM = D_MODEL // (2 * ATT_HEADS)
ROPE_THETA = 10000.0
Q_BLOCK = 128
POOL_WINDOWS = (2, 4, 8, 16)
POOL_GROUP = D_MODEL // len(POOL_WINDOWS)
FFT_GROUPS = 4
FFT_GROUP = D_MODEL // FFT_GROUPS
HY_BANDS = 16
HY_EMB = 2 * HY_BANDS + 1
HY_FILTER_HIDDEN = 64
HY_TARGET = 1e-2
HY_FAST = 0.3
HY_SLOW = 1.5
N_EXPERTS = 16
N_GROUPS = 4
EXPERTS_PER_GROUP = N_EXPERTS // N_GROUPS
TOP_K = 2
D_EXPERT = 1024
MOE_BLOCK = 256

kernel_name = "hybrid_diffusion_interleaved_moe_trunk"

def n_layers_of(kind):
    return len(range(kind, DEPTH, N_MIXERS))

def ctx_needed(i):
    return any(j % N_MIXERS == 0 for j in range(i, DEPTH))

def layer_norm(x, g, b):
    xf = x.astype(jnp.float32)
    mu = xf.mean(-1, keepdims=True)
    var = jnp.square(xf - mu).mean(-1, keepdims=True)
    return ((xf - mu) * lax.rsqrt(var + LN_EPS) * g.astype(jnp.float32) + b.astype(jnp.float32)).astype(x.dtype)

def deepnorm_update(x, y, gate, g, b):
    return layer_norm(ALPHA * x + (1.0 + gate) * y, g, b)

def axial_rope_tables(n_tokens):
    rows = n_tokens // GRID_W
    row = jnp.repeat(jnp.arange(rows), GRID_W).astype(jnp.float32)
    col = jnp.tile(jnp.arange(GRID_W), rows).astype(jnp.float32)
    half = ATT_HEAD_DIM // 2
    inv = ROPE_THETA ** (-jnp.arange(0, half, 2, dtype=jnp.float32) / half)
    ar = row[:, None] * inv
    ac = col[:, None] * inv
    ang = jnp.concatenate([ar, ar, ac, ac], axis=-1)
    return jnp.cos(ang), jnp.sin(ang)

def apply_axial_rope(x, cos, sin):
    a, b, c, d = jnp.split(x, 4, axis=-1)
    rot = jnp.concatenate([-b, a, -d, c], axis=-1)
    cos = cos[None, :, None, None, :].astype(x.dtype)
    sin = sin[None, :, None, None, :].astype(x.dtype)
    return x * cos + rot * sin

def attn_qkv(h, wqkv):
    B, L, _ = h.shape
    q, k, v = jnp.split(h @ wqkv, 3, axis=-1)
    q = q.reshape(B, L, ATT_HEADS, 2, ATT_HEAD_DIM)
    k = k.reshape(B, L, ATT_HEADS, 2, ATT_HEAD_DIM)
    v = v.reshape(B, L, ATT_HEADS, 2 * ATT_HEAD_DIM)
    return q, k, v

def diff_attention(q, k, v, lam, subln, wo, lam_init):
    B, Lq = q.shape[0], q.shape[1]
    lf = lam.astype(jnp.float32)
    lam_full = jnp.exp(jnp.sum(lf[0] * lf[1])) - jnp.exp(jnp.sum(lf[2] * lf[3])) + lam_init
    scale = ATT_HEAD_DIM ** -0.5

    def block(qb):
        s = jnp.einsum('bqhnd,bkhnd->nbhqk', qb, k).astype(jnp.float32) * scale
        p = jax.nn.softmax(s, axis=-1)
        a = p[0] - lam_full * p[1]
        return jnp.einsum('bhqk,bkhe->bqhe', a.astype(v.dtype), v)

    nb = Lq // Q_BLOCK
    qb = q.reshape(B, nb, Q_BLOCK, ATT_HEADS, 2, ATT_HEAD_DIM).swapaxes(0, 1)
    o = lax.map(block, qb)
    o = o.swapaxes(0, 1).reshape(B, Lq, ATT_HEADS, 2 * ATT_HEAD_DIM).astype(jnp.float32)
    o = o * lax.rsqrt(jnp.mean(jnp.square(o), axis=-1, keepdims=True) + LN_EPS)
    o = o * subln.astype(jnp.float32) * (1.0 - lam_init)
    return o.reshape(B, Lq, D_MODEL).astype(q.dtype) @ wo

def pool_mixer(h, w, scale):
    B, L, D = h.shape
    hf = h.astype(jnp.float32)
    csum = jnp.concatenate([jnp.zeros((B, 1, D), jnp.float32), jnp.cumsum(hf, axis=1)], axis=1)
    t = jnp.arange(L)
    groups = []
    for g, win in enumerate(POOL_WINDOWS):
        lo = jnp.clip(t - win // 2, 0, L)
        hi = jnp.clip(t - win // 2 + win, 0, L)
        sl = slice(g * POOL_GROUP, (g + 1) * POOL_GROUP)
        cs = csum[:, :, sl]
        mean = (cs[:, hi] - cs[:, lo]) / (hi - lo).astype(jnp.float32)[:, None]
        groups.append(mean - hf[:, :, sl])
    pooled = jnp.stack(groups, axis=2).astype(h.dtype)
    y = jnp.einsum('blgd,gde->blge', pooled, w).reshape(B, L, D)
    return y * scale

def fourier_mixer(h, w, b):
    B, L, D = h.shape
    hg = h.astype(jnp.float32).reshape(B, L, FFT_GROUPS, FFT_GROUP)
    f = jnp.fft.fft2(hg, axes=(1, 3), norm="ortho").real
    return f.reshape(B, L, D).astype(h.dtype) @ w + b

def hyena_filters(L, f1, fb1, f2, fb2, f3, freq):
    f32 = jnp.float32
    pos = jnp.arange(L, dtype=f32)
    t = pos / L
    bands = jnp.linspace(1e-4, HY_BANDS - 1, HY_BANDS, dtype=f32)
    ang = (2.0 * math.pi / L) * pos[:, None] * bands[None, :]
    z = jnp.concatenate([t[:, None], jnp.cos(ang), jnp.sin(ang)], axis=-1)
    fr = freq.astype(f32)
    a = jnp.sin(fr * (z @ f1.astype(f32) + fb1.astype(f32)))
    a = jnp.sin(fr * (a @ f2.astype(f32) + fb2.astype(f32)))
    k = a @ f3.astype(f32)
    deltas = jnp.abs(jnp.linspace(math.log(HY_TARGET) / HY_SLOW, math.log(HY_TARGET) / HY_FAST, D_MODEL, dtype=f32))
    window = jnp.exp(-t[:, None] * deltas[None, :])
    return k[:, :D_MODEL] * window, k[:, D_MODEL:] * window

def hyena_mixer(h, win, bin_, conv_w, conv_b, f1, fb1, f2, fb2, f3, freq, skip, wo, bo):
    B, L, D = h.shape
    z = h @ win + bin_
    zp = jnp.pad(z, ((0, 0), (1, 1), (0, 0)))
    z = zp[:, :-2] * conv_w[0] + zp[:, 1:-1] * conv_w[1] + zp[:, 2:] * conv_w[2] + conv_b
    x0, x1, v = jnp.split(z, 3, axis=-1)
    v = (v * x1).astype(jnp.float32)
    kf, kb = hyena_filters(L, f1, fb1, f2, fb2, f3, freq)
    k_full = jnp.concatenate([kf, jnp.zeros((1, D), jnp.float32), kb[:0:-1]], axis=0)
    n = 2 * L
    y = jnp.fft.irfft(jnp.fft.rfft(v, n=n, axis=1) * jnp.fft.rfft(k_full, n=n, axis=0)[None], n=n, axis=1)[:, :L]
    y = (y + v * skip.astype(jnp.float32)) * x0.astype(jnp.float32)
    return y.astype(h.dtype) @ wo + bo

def route(h, router_w, router_b):
    T = h.shape[0]
    logits = (h @ router_w).astype(jnp.float32) + router_b.astype(jnp.float32)
    probs = jax.nn.softmax(logits, axis=-1).reshape(T, N_GROUPS, EXPERTS_PER_GROUP)
    gscore = lax.top_k(probs, TOP_K)[0].sum(-1)
    g = jnp.argmax(gscore, axis=-1)
    in_g = probs[jnp.arange(T), g]
    vals, idx = lax.top_k(in_g, TOP_K)
    return g[:, None] * EXPERTS_PER_GROUP + idx, vals / vals.sum(-1, keepdims=True)

def moe_ffn(h, router_w, router_b, wg, wu, wd):
    T, D = h.shape
    eidx, ew = route(h, router_w, router_b)
    A = T * TOP_K
    flat_e = eidx.reshape(A)
    flat_w = ew.reshape(A)
    flat_t = jnp.repeat(jnp.arange(T, dtype=jnp.int32), TOP_K)
    order = jnp.argsort(flat_e)
    se, st, sw = flat_e[order], flat_t[order], flat_w[order]
    counts = jnp.bincount(flat_e, length=N_EXPERTS)
    starts = jnp.cumsum(counts) - counts
    padded = (counts + MOE_BLOCK - 1) // MOE_BLOCK * MOE_BLOCK
    pend = jnp.cumsum(padded)
    pstart = pend - padded
    dest = pstart[se] + jnp.arange(A) - starts[se]
    n_blocks = -(-A // MOE_BLOCK) + N_EXPERTS
    P = n_blocks * MOE_BLOCK
    buf_t = jnp.zeros((P,), jnp.int32).at[dest].set(st)
    buf_w = jnp.zeros((P,), jnp.float32).at[dest].set(sw)
    blk_e = jnp.minimum(jnp.searchsorted(pend, jnp.arange(n_blocks) * MOE_BLOCK, side='right'), N_EXPERTS - 1)
    xs = h[buf_t].reshape(n_blocks, MOE_BLOCK, D)

    def expert_block(args):
        xb, e = args
        return (jax.nn.silu(xb @ wg[e]) * (xb @ wu[e])) @ wd[e]

    ys = lax.map(expert_block, (xs, blk_e)).reshape(P, D)
    out = jnp.zeros((T, D), jnp.float32).at[buf_t].add(ys.astype(jnp.float32) * buf_w[:, None])
    return out.astype(h.dtype)

def setup_inputs(seed: int = 0) -> dict:
    key = jax.random.key(seed)
    ks = list(jax.random.split(key, 40))
    f32 = jnp.float32

    def nrm(i, shape, s):
        return jax.random.normal(ks[i], shape, f32) * s

    nA, nB, nC, nD = n_layers_of(0), n_layers_of(1), n_layers_of(2), n_layers_of(3)
    D = D_MODEL
    return {
        "x": nrm(0, (BATCH, SEQ, D), 1.0),
        "c": nrm(1, (BATCH, D), 1.0),
        "ctx": nrm(2, (BATCH, CTX_LEN, D), 1.0),
        "c_ctx": nrm(3, (D,), 1.0),
        "mod_w": nrm(4, (DEPTH, D, 6 * D), 0.3 * D ** -0.5),
        "mod_b": nrm(5, (DEPTH, 6 * D), 0.02),
        "ln_g": 1.0 + nrm(6, (DEPTH, 2, D), 0.02),
        "ln_b": nrm(7, (DEPTH, 2, D), 0.02),
        "attn_wqkv": nrm(8, (nA, D, 3 * D), D ** -0.5),
        "attn_wo": nrm(9, (nA, D, D), BETA * D ** -0.5),
        "attn_lam": nrm(10, (nA, 4, ATT_HEAD_DIM), 0.1),
        "attn_subln": 1.0 + nrm(11, (nA, 2 * ATT_HEAD_DIM), 0.02),
        "pool_w": nrm(12, (nB, len(POOL_WINDOWS), POOL_GROUP, POOL_GROUP), BETA * POOL_GROUP ** -0.5),
        "pool_scale": 1.0 + nrm(13, (nB, D), 0.02),
        "fnet_w": nrm(14, (nC, D, D), BETA * D ** -0.5),
        "fnet_b": nrm(15, (nC, D), 0.02),
        "hy_win": nrm(16, (nD, D, 3 * D), D ** -0.5),
        "hy_bin": nrm(17, (nD, 3 * D), 0.02),
        "hy_conv_w": nrm(18, (nD, 3, 3 * D), 3 ** -0.5),
        "hy_conv_b": nrm(19, (nD, 3 * D), 0.02),
        "hy_f1": nrm(20, (nD, HY_EMB, HY_FILTER_HIDDEN), HY_EMB ** -0.5),
        "hy_fb1": nrm(21, (nD, HY_FILTER_HIDDEN), 0.02),
        "hy_f2": nrm(22, (nD, HY_FILTER_HIDDEN, HY_FILTER_HIDDEN), HY_FILTER_HIDDEN ** -0.5),
        "hy_fb2": nrm(23, (nD, HY_FILTER_HIDDEN), 0.02),
        "hy_f3": nrm(24, (nD, HY_FILTER_HIDDEN, 2 * D), 0.02),
        "hy_freq": 1.0 + nrm(25, (nD, HY_FILTER_HIDDEN), 0.02),
        "hy_skip": nrm(26, (nD, D), 0.1),
        "hy_wo": nrm(27, (nD, D, D), BETA * D ** -0.5),
        "hy_bo": nrm(28, (nD, D), 0.02),
        "router_w": nrm(29, (D, N_EXPERTS), D ** -0.5),
        "router_b": nrm(30, (N_EXPERTS,), 0.01),
        "moe_wg": nrm(31, (DEPTH, N_EXPERTS, D, D_EXPERT), D ** -0.5),
        "moe_wu": nrm(32, (DEPTH, N_EXPERTS, D, D_EXPERT), D ** -0.5),
        "moe_wd": nrm(33, (DEPTH, N_EXPERTS, D_EXPERT, D), BETA * D_EXPERT ** -0.5),
    }

def reference(x, c, ctx, c_ctx, mod_w, mod_b, ln_g, ln_b, attn_wqkv, attn_wo, attn_lam, attn_subln,
              pool_w, pool_scale, fnet_w, fnet_b, hy_win, hy_bin, hy_conv_w, hy_conv_b, hy_f1, hy_fb1,
              hy_f2, hy_fb2, hy_f3, hy_freq, hy_skip, hy_wo, hy_bo, router_w, router_b, moe_wg, moe_wu, moe_wd):
    B, S, D = x.shape
    rope = axial_rope_tables(S)
    xl, xc = x, ctx
    for i in range(DEPTH):
        kind, j = i % N_MIXERS, i // N_MIXERS
        ctx_in, ctx_out = ctx_needed(i), ctx_needed(i + 1)
        ml = (jax.nn.silu(c) @ mod_w[i] + mod_b[i])[:, None, :]
        sh1, sc1, g1, sh2, sc2, g2 = jnp.split(ml, 6, axis=-1)
        hl = xl * (1.0 + sc1) + sh1
        if ctx_in:
            mc = jax.nn.silu(c_ctx) @ mod_w[i] + mod_b[i]
            csh1, csc1, cg1, csh2, csc2, cg2 = jnp.split(mc, 6)
            hc = xc * (1.0 + csc1) + csh1
        yc = None
        if kind == 0:
            lam_init = 0.8 - 0.6 * math.exp(-0.3 * i)
            ql, kl, vl = attn_qkv(hl, attn_wqkv[j])
            ql = apply_axial_rope(ql, *rope)
            kl = apply_axial_rope(kl, *rope)
            qc, kc, vc = attn_qkv(hc, attn_wqkv[j])
            yl = diff_attention(ql, jnp.concatenate([kl, kc], axis=1), jnp.concatenate([vl, vc], axis=1),
                                attn_lam[j], attn_subln[j], attn_wo[j], lam_init)
            if ctx_out:
                yc = diff_attention(qc, kc, vc, attn_lam[j], attn_subln[j], attn_wo[j], lam_init)
        elif kind == 1:
            yl = pool_mixer(hl, pool_w[j], pool_scale[j])
            if ctx_out:
                yc = pool_mixer(hc, pool_w[j], pool_scale[j])
        elif kind == 2:
            yl = fourier_mixer(hl, fnet_w[j], fnet_b[j])
            if ctx_out:
                yc = fourier_mixer(hc, fnet_w[j], fnet_b[j])
        else:
            hp = (hy_win[j], hy_bin[j], hy_conv_w[j], hy_conv_b[j], hy_f1[j], hy_fb1[j], hy_f2[j], hy_fb2[j],
                  hy_f3[j], hy_freq[j], hy_skip[j], hy_wo[j], hy_bo[j])
            yl = hyena_mixer(hl, *hp)
            if ctx_out:
                yc = hyena_mixer(hc, *hp)
        xl = deepnorm_update(xl, yl, g1, ln_g[i, 0], ln_b[i, 0])
        tokens = (xl * (1.0 + sc2) + sh2).reshape(B * S, D)
        if ctx_out:
            xc = deepnorm_update(xc, yc, cg1, ln_g[i, 0], ln_b[i, 0])
            tokens = jnp.concatenate([tokens, (xc * (1.0 + csc2) + csh2).reshape(-1, D)], axis=0)
        y2 = moe_ffn(tokens, router_w, router_b, moe_wg[i], moe_wu[i], moe_wd[i])
        xl = deepnorm_update(xl, y2[:B * S].reshape(B, S, D), g2, ln_g[i, 1], ln_b[i, 1])
        if ctx_out:
            xc = deepnorm_update(xc, y2[B * S:].reshape(B, -1, D), cg2, ln_g[i, 1], ln_b[i, 1])
    return xl


_drawn_inputs = setup_inputs


def setup_inputs(seed=0):
    import zlib

    import numpy as np

    out = dict(_drawn_inputs(seed))
    spreads = {}
    factors = {}
    for name, (base, spread) in spreads.items():
        noise = np.random.default_rng([zlib.crc32(name.encode()), seed]).standard_normal(out[name].shape)
        drawn = base * np.exp(spread * noise) if base else spread * noise
        out[name] = __import__('jax').numpy.asarray(drawn.astype(out[name].dtype))
    for name, factor in factors.items():
        out[name] = (out[name] * factor).astype(out[name].dtype)
    return out
```

```python
import math
from contextlib import ExitStack

import concourse.bass as bass
from concourse import mybir

F32 = mybir.dt.float32
I32 = mybir.dt.int32
ALU = mybir.AluOpType
ACT = mybir.ActivationFunctionType
AX = mybir.AxisListType.X

P = 128
D = 1024
KT = D // P
TOK = 256
TT = TOK // P
NB = 512
HALF = D // 2
HEADS, HD = 8, 64
HPJ = 4
KEYS = 2 * TOK
KEYT = KEYS // P
NE, NG, EG = 16, 4, 4
SLOTS = 64
DEPTH = 2
ALPHA = (2 * DEPTH) ** 0.25
EPS = 1e-5
LAM_INIT = 0.8 - 0.6 * math.exp(-0.3 * 0)
SCALE = HD ** -0.5
NMOD = 6 * D // NB
SH1, SC1, G1, SH2, SC2, G2 = range(6)

RING = 8
RING_A = 4
UNIT = 4096
EU = 6
GRP = 4
GU = GRP * EU
TURNS = NE // GRP
INSERT = 13

PHASE_A = ([("mod", m) for m in range(4)]
           + [(k, j) for j in range(2) for k in ("q", "k", "v")]
           + [("mod", m) for m in range(4, NMOD)] + [("wo", 0), ("wo", 1)])
A_POS = {u: n for n, u in enumerate(PHASE_A)}
NA = len(PHASE_A)
assert NA % RING_A == 0
TAIL0 = ([("e", 12)] + [("mod", m) for m in range(3)] + [("e", 13)] + [("mod", m) for m in range(3, 6)]
         + [("e", 14), ("e", 15)] + [("mod", m) for m in range(6, 10)] + [("pool", 0)]
         + [("mod", m) for m in range(10, NMOD)])


def tail_base(what):
    n = (TURNS - 1) * GU
    for w in TAIL0:
        if w == what:
            return n
        n += EU if w[0] == "e" else 1
    raise KeyError(what)


LAYER_BASE = [0, NE * EU + INSERT]

GROUPS = [(kind, j, t) for j in range(2) for kind, n in (("q", 2), ("k", 4), ("v", 4)) for t in range(n)]
EVAC, _n = [], {"dve": 0, "act": 0}
for _kind, _j, _t in GROUPS:
    _e = "dve" if _kind == "q" or (_kind == "k" and _t < TT) else "act"
    EVAC.append((_e, _n[_e]))
    _n[_e] += 1
QK = [g for g, (kind, _, _) in enumerate(GROUPS) if kind != "v"]
QK_N = {g: n for n, g in enumerate(QK)}
STEPS = [(j, t, h) for j in range(2) for t in range(TT) for h in range(HPJ)]
NS = len(STEPS)
FILL = {0: [("g", 10), ("g", 11)]}
FILL.update({s: [("g", 11 + s)] for s in range(1, 8)})
FILL[8] = [("g", 19), ("m", 4)]
FILL.update({s: [("m", s - 4)] for s in range(9, 16)})

C_ID, C_TRI, C_ONE, C_IOTA, C_SELL, C_SELC = (P * i for i in range(6))
C_BIAS = 6 * P
C_PSC = C_BIAS + NMOD * 32
C_LT = C_PSC + 2 * P
C_END = C_LT + EG * EG


def constants():
    import numpy as np
    c = np.zeros((P, C_END), np.float32)
    i = np.arange(P)
    c[:, C_ID:C_ID + P] = np.eye(P)
    c[:, C_TRI:C_TRI + P] = i[:, None] < i[None, :]
    c[:, C_ONE:C_ONE + P] = 1
    c[:, C_IOTA:C_IOTA + P] = i[None, :] % SLOTS
    c[:, C_SELL:C_SELL + P] = (i % 32 == 0)[:, None]
    c[:, C_SELC:C_SELC + P] = (i % 32 == 16)[:, None]
    for m in range(NMOD):
        c[m, C_BIAS + 32 * m:C_BIAS + 32 * m + 32] = 1
    for h in range(2):
        c[NMOD + h, C_PSC + P * h:C_PSC + P * h + P] = 1
    c[:, C_LT:C_END] = (np.arange(EG)[None, :] < np.arange(EG)[:, None]).reshape(-1)

    grid_w, theta = 64, 10000.0
    half = HD // 2
    t = np.arange(TOK)
    inv = (np.float32(theta) ** (-np.arange(0, half, 2, dtype=np.float32) / np.float32(half))).astype(np.float32)
    ar = (t // grid_w).astype(np.float32)[:, None] * inv
    ac = (t % grid_w).astype(np.float32)[:, None] * inv
    ang = np.concatenate([ar, ar, ac, ac], axis=-1)
    q = HD // 4
    sign = np.repeat(np.array([-1, 1, -1, 1], np.float32), q)
    rope = np.stack([np.cos(ang), np.sin(ang) * sign], 1).astype(np.float32)
    rope = np.ascontiguousarray(rope.reshape(TT, P, 2 * HD).transpose(1, 0, 2).reshape(P, -1))

    band = np.zeros((TOK, 4, TOK), np.float32)
    for g, win in enumerate((2, 4, 8, 16)):
        for s in range(TOK):
            lo, hi = max(s - win // 2, 0), min(s - win // 2 + win, TOK)
            band[lo:hi, g, s] = 1.0 / (hi - lo)
            band[s, g, s] -= 1.0
    return {"consts": c, "rope": rope, "band": band.reshape(TOK, -1)}


def trunk(nc, x, c, ctx, c_ctx, mod_w, mod_b, ln_g, ln_b, attn_wqkv, attn_wo, attn_lam, attn_subln,
          pool_w, pool_scale, router_w, router_b, moe_wg, moe_wu, moe_wd, consts, rope, band, out):
    with ExitStack() as st:
        def sb(name, n, dt=F32, p=P):
            return st.enter_context(nc.sbuf_tensor(name, [p, n], dt))

        sems = {}

        def sem(name):
            if name not in sems:
                sems[name] = st.enter_context(nc.semaphore(name))
            return sems[name]

        ring = sb("ring", RING * UNIT)
        mod = sb("mod", 6 * D)
        lng, lnb = sb("lng", D), sb("lnb", D)
        xl = sb("xl", TT * D)
        h2 = sb("h2", TT * D)
        tra = sb("tra", 2 * D)
        work = sb("work", 2 * D)
        cst = sb("cst", C_END)
        rows = sb("rows", NB, p=NMOD + 2)
        modp = sb("modp", NB)
        rw = sb("rw", KT * NE)
        rb = sb("rb", NE)
        cs = sb("cs", KT * 32)
        crow = sb("crow", P, p=2 * KT)
        csig = sb("csig", P, p=2 * KT)
        subln = sb("subln", P)
        stat = sb("stat", 16)
        mv = sb("mv", 4)
        small = sb("small", 6 * 2 * NE)
        pair = sb("pair", 2 * TT * NG * EG * EG)
        nchunk = sb("nchunk", 1, I32)
        iota_x = sb("iota_x", P)

        ps = st.enter_context(nc.psum_tensor("ps", [P, 8, NB], F32))
        ident = cst[:, C_ID:C_ID + P]

        def slot(s):
            return ring[:, s * UNIT:(s + 1) * UNIT]

        hT = ring[:, 4 * UNIT:5 * UNIT].rearrange("p (k t) -> p k t", k=KT)
        kT = ring[:, 5 * UNIT:6 * UNIT].rearrange("p (h t) -> p h t", h=HEADS)
        vv = ring[:, 6 * UNIT:7 * UNIT].rearrange("p (t n) -> p t n", t=KEYT)
        hnat = ring[:, 6 * UNIT:7 * UNIT].rearrange("p (t n) -> p t n", t=KEYT)
        qT = ring[:, 7 * UNIT:7 * UNIT + 2048].rearrange("p (h t) -> p h t", h=HEADS)
        osb = ring[:, 7 * UNIT + 2048:8 * UNIT].rearrange("p (t n) -> p t n", t=TT)
        cin = ring[:, 7 * UNIT + 2048:8 * UNIT].rearrange("p (t n) -> p t n", t=TT)
        modc = h2[:, 0:2 * D]
        nat = [h2[:, 0:NB], h2[:, NB:2 * NB]]
        rtmp = [h2[:, 2 * NB:3 * NB], h2[:, 3 * NB:4 * NB]]
        pr = [work[:, b * 2 * NB:(b + 1) * 2 * NB].rearrange("p (n k) -> p n k", n=2) for b in range(2)]
        att = [tra[:, b * NB:(b + 1) * NB] for b in range(2)]
        aT = [tra[:, (2 + b) * NB:(3 + b) * NB] for b in range(2)]
        oT = tra[:, :].rearrange("p (k t) -> p k t", k=KT)
        ropes = mod[:, 5 * D:5 * D + 256].rearrange("p (t c n) -> p t c n", t=TT, c=2)
        lamb = mod[:, 5 * D + 256:5 * D + 512]
        ltmp = mod[:, 5 * D + 512:5 * D + 640]
        mx = small[:, 0:4].rearrange("p (b n) -> p b n", b=2)
        nb = small[:, 4:8].rearrange("p (b n) -> p b n", b=2)
        sm = small[:, 8:12].rearrange("p (b n) -> p b n", b=2)
        rs = small[:, 12:16].rearrange("p (b n) -> p b n", b=2)
        rl = small[:, 16:18]
        ss = small[:, 32:48].rearrange("p (t h) -> p t h", t=TT)
        lam = small[:, 48:56]
        ors = small[:, 64:80].rearrange("p (t h) -> p t h", t=TT)
        sqj = modp[:, 0:P]

        h2T = tra[:, :].rearrange("p (k t) -> p k t", k=KT)
        sgat = tra[:, 0:TT * SLOTS].rearrange("p (t s) -> p t s", t=TT)
        ssc = tra[:, 128:128 + TT * P].rearrange("p (t s) -> p t s", t=TT)
        swT = [tra[:, 384 + 256 * b:640 + 256 * b] for b in range(2)]
        ysb = tra[:, 1024:1536]
        sig = tra[:, 1536:2048]
        zz = tra[:, 0:D]
        xT = [work[:, b * NB:(b + 1) * NB].rearrange("p (k s) -> p k s", k=KT) for b in range(2)]
        hmid = work[:, 2 * NB:3 * NB]
        hTt = work[:, 3 * NB:4 * NB].rearrange("p (j s) -> p j s", j=4)
        poolT = work[:, :].rearrange("p (k t) -> p k t", k=KT)
        prob = small[:, 0:32].rearrange("p (t e) -> p t e", t=TT)
        sel = small[:, 32:64].rearrange("p (t e) -> p t e", t=TT)
        wgt = small[:, 64:96].rearrange("p (t e) -> p t e", t=TT)
        rank = small[:, 96:128].rearrange("p (t e) -> p t e", t=TT)
        rt = small[:, 128:160].rearrange("p (t e) -> p t e", t=TT)
        gs = small[:, 160:168].rearrange("p (t g) -> p t g", t=TT)
        gt2 = small[:, 168:176].rearrange("p (t g) -> p t g", t=TT)
        col = small[:, 176:186]
        pair_a = pair[:, 0:TT * NG * EG * EG]
        pair_b = pair[:, TT * NG * EG * EG:]

        def ring_slot(v):
            return v % RING, v // RING + 1

        def landed(eng, v, turns=0):
            s, n = ring_slot(v)
            eng.wait_ge(sem(f"ring_loaded_{s}"), turns * (16 * GU // RING) + 16 * n)

        def used(eng, v, turns=0):
            eng.wait_ge(sem("unit_used"), turns * GU + (NA + v + 1))

        def early_used(eng, unit):
            eng.wait_ge(sem("unit_used"), A_POS[unit] + 1)

        def group_done(eng, g):
            kind, j, t = GROUPS[g]
            if t == (1 if kind == "q" else 3):
                early_used(eng, (kind, j))
            else:
                eng.wait_ge(sem("qkv_done"), sum(1 for k2, _, t2 in GROUPS[:g + 1] if t2 != (1 if k2 == "q" else 3)))

        def mixed(eng, layer, t, h):
            if layer == 0:
                if t == 0:
                    eng.wait_ge(sem("mix_done"), h + 1)
                else:
                    early_used(eng, ("wo", h))
            elif (t, h) == (1, 1):
                used(eng, tail_base(("pool", 0)))
            else:
                eng.wait_ge(sem("mix_done"), 2 + 2 * t + h + 1)

        def tail(layer):
            v = LAYER_BASE[layer] + (TURNS - 1) * GU
            for kind, n in (TAIL0 if layer == 0 else [("e", 12 + j) for j in range(GRP)]):
                yield kind, n, v
                v += EU if kind == "e" else 1

        def walk(eng, layer, expert, mod_unit=None, pool_unit=None, others=None):
            base = LAYER_BASE[layer]
            with eng.Fori(0, TURNS - 1) as i:
                for j in range(GRP):
                    expert(i * GRP + j, j, base + j * EU, i, False)
            for kind, n, v in tail(layer):
                if kind == "e":
                    expert(n, n % GRP, v, 0, n == NE - 1)
                    if n == NE - 1 and others is not None:
                        others()
                elif kind == "mod":
                    mod_unit(n, v)
                elif pool_unit is not None:
                    pool_unit(v)

        def further(eng, layer, chunk, body, first=None):
            eng.wait_ge(sem("routed"), layer + 1)
            chunks = eng.value_load(nchunk[0:1, 0:1], min_val=0, max_val=TOK // SLOTS - 1)
            with eng.If(chunks > 0):
                if first is not None:
                    first()
                with eng.Fori(0, chunks) as ci:
                    if chunk is not None:
                        chunk(ci)
                    with eng.Fori(0, NE) as e:
                        body(ci * NE + e, e)

        block = st.enter_context(nc.Block())

        @block.sync
        def _(sp):
            def load(dst, src, s):
                sp.dma_start(dst, src).then_inc(s, 16)

            def columns(w, n):
                return w[:, n * NB:(n + 1) * NB].rearrange("(k p) n -> p k n", p=P)

            for u, (kind, i) in enumerate(PHASE_A):
                if u >= RING_A:
                    sp.wait_ge(sem("unit_used"), u - RING_A + 1)
                w, n = {"mod": (mod_w[0], i), "q": (attn_wqkv[0], i), "k": (attn_wqkv[0], 2 + i),
                        "v": (attn_wqkv[0], 4 + i), "wo": (attn_wo[0], i)}[kind]
                load(slot(u % RING_A).rearrange("p (k n) -> p k n", k=KT), columns(w, n),
                     sem(f"early_loaded_{u % RING_A}"))

            def slot_free(v, turns=0):
                if isinstance(turns, int) and v < RING_A:
                    sp.wait_ge(sem("unit_used"), NA - RING_A + v + 1)
                elif isinstance(turns, int) and v < RING:
                    sp.wait_ge(sem("oT_done"), 2 * TT)
                    sp.wait_ge(sem("oT_copied"), 2 * TT)
                else:
                    used(sp, v - RING, turns)

            def load_expert(layer, e, v, turns=0):
                for n in range(EU):
                    slot_free(v + n, turns)
                    s, _ = ring_slot(v + n)
                    w = (moe_wg, moe_wu, moe_wd)[n // 2][layer]
                    src = w[bass.ds(e, 1), (n % 2) * HALF:(n % 2 + 1) * HALF, :].rearrange("e (k p) n -> p (e k) n", p=P)
                    load(slot(s).rearrange("p (k n) -> p k n", k=4), src, sem(f"ring_loaded_{s}"))

            for layer in range(DEPTH):
                base = LAYER_BASE[layer]
                if layer == 0:
                    for j in range(GRP):
                        load_expert(0, j, base + j * EU)
                with sp.Fori(1 - layer, TURNS - 1) as i:
                    for j in range(GRP):
                        load_expert(layer, i * GRP + j, base + j * EU, i)

                def further_loads(last):
                    def body(n, e):
                        used(sp, last)
                        sp.wait_ge(sem(f"x{layer}_down"), n + 1)
                        for u in range(EU):
                            w = (moe_wg, moe_wu, moe_wd)[u // 2][layer]
                            src = w[bass.ds(e, 1), (u % 2) * HALF:(u % 2 + 1) * HALF, :]\
                                .rearrange("e (k p) n -> p (e k) n", p=P)
                            load(slot(u).rearrange("p (k n) -> p k n", k=4), src, sem(f"x{layer}_loaded"))
                    further(sp, layer, None, body)
                    sp.wait_ge(sem("further_done"), layer + 1)

                for kind, n, v in tail(layer):
                    if kind == "e":
                        load_expert(layer, n, v)
                        if n == NE - 1:
                            further_loads(v + EU - 1)
                        continue
                    slot_free(v)
                    s, _ = ring_slot(v)
                    if kind == "mod":
                        load(slot(s).rearrange("p (k n) -> p k n", k=KT), columns(mod_w[1], n), sem(f"ring_loaded_{s}"))
                    else:
                        load(slot(s)[:, 0:2048].rearrange("p (k n) -> p k n", k=KT),
                             pool_w[0].rearrange("g (k p) n -> p (g k) n", p=P), sem("pool_loaded"))
                        load(slot(s)[:, 2048:4096].rearrange("p (k n) -> p k n", k=TT),
                             band.rearrange("(k p) n -> p k n", p=P), sem(f"ring_loaded_{s}"))
            for t in range(TT):
                sp.wait_ge(sem("dn_done"), 3 * TT + t + 1)
                load(out[0, t * P:(t + 1) * P, :], xl[:, t * D:(t + 1) * D], sem("stored"))
            sp.wait_ge(sem("stored"), 16 * TT)

        @block.tensor
        def _(pe):
            mm = nc.tensor.matmul

            def bank(b, p0=0, p1=P, n0=0, n1=NB):
                return ps[p0:p1, b, n0:n1]

            def turn_blocks(b, src, n=4):
                for k in range(n):
                    last = nc.tensor.transpose(bank(b, 0, P, k * P, k * P + P), src[:, k * P:k * P + P], ident)
                return last

            def early(unit):
                u = A_POS[unit]
                pe.wait_ge(sem(f"early_loaded_{u % RING_A}"), 16 * (u // RING_A + 1))
                return slot(u % RING_A).rearrange("p (k n) -> p k n", k=KT)

            def adaln(n, m, w, bp, bb):
                if m == 0:
                    pe.wait_ge(sem("rows_loaded"), 32 if n == 0 else 48)
                if n:
                    pe.wait_ge(sem("mod_ready"), n)
                for r in range(2):
                    for g in range(4):
                        k = 4 * r + g
                        mm(bank(bp, 32 * g, 32 * g + 32), cs[:, 32 * k:32 * k + 32], w[:, k, :], start=(r == 0),
                           stop=(r == 1 and g > 0), skip_group_check=True)
                mm(bank(bp, 0, 32), cst[0:NMOD, C_BIAS + 32 * m:C_BIAS + 32 * m + 32], rows[0:NMOD, :],
                   start=False, stop=True, skip_group_check=True).then_inc(sem("unit_used"), 1)
                pe.wait_ge(sem("modp_copied"), n + 1)
                mm(bank(bb), cst[:, C_SELL:C_SELL + P], modp[:, :], start=True, stop=True).then_inc(sem("modb_done"), 1)

            pe.wait_ge(sem("consts_loaded"), 16)
            pe.wait_ge(sem("crow_ready"), 1)
            nc.tensor.transpose(bank(7, 0, P, 0, 2 * KT), crow[:, :], cst[0:2 * KT, C_ID:C_ID + 2 * KT])\
                .then_inc(sem("ccol_done"), 1)
            pe.wait_ge(sem("cs_ready"), 2)
            for m in range(4):
                w = early(("mod", m))
                if m:
                    pe.wait_ge(sem("modc_ready"), m)
                adaln(m, m, w, 0, 1)
                mm(bank(2), cst[:, C_SELC:C_SELC + P], modp[:, :], start=True, stop=True).then_inc(sem("modc_done"), 1)
            for i in range(KEYT):
                pe.wait_ge(sem("hnat_ready"), i + 1)
                for b in range(2):
                    part = 2 * i + b
                    if part >= 4:
                        pe.wait_ge(sem("hT_copied"), part - 3)
                    turn_blocks(4 + part % 4, hnat[:, i, b * NB:(b + 1) * NB]).then_inc(sem("hT_done"), 1)
            pe.wait_ge(sem("hT_copied"), 2 * KEYT)
            pe.wait_ge(sem("modc_ready"), 4)
            pe.wait_ge(sem("mod_ready"), 4)

            def out_of_psum(g):
                e, n = EVAC[g]
                pe.wait_ge(sem(f"qkv_out_{e}"), n + 1)

            def group(g):
                kind, j, t = GROUPS[g]
                w = early((kind, j))
                if g >= 2:
                    out_of_psum(g - 2)
                for k in range(KT):
                    last = mm(bank(g % 2), hT[:, k, t * P:t * P + P], w[:, k, :], start=(k == 0), stop=(k == KT - 1))
                last.then_inc(sem("unit_used" if t == (1 if kind == "q" else 3) else "qkv_done"), 1)

            def turn(g):
                if g in QK_N:
                    n = QK_N[g]
                    out_of_psum(g)
                    if n:
                        pe.wait_ge(sem("qkT_copied"), n)
                    turn_blocks(6, nat[n % 2]).then_inc(sem("qkT_done"), 1)

            for g in range(10):
                group(g)
                if g:
                    turn(g - 1)

            def scores(s):
                j, t, h = STEPS[s]
                pe.wait_ge(sem("qkT_copied"), 6 * (j + 1))
                if s:
                    pe.wait_ge(sem("exp_done"), 2 * s)
                for n in range(2):
                    last = mm(bank(2 + n), qT[HD * n:HD * n + HD, HPJ * j + h, t * P:t * P + P],
                              kT[HD * n:HD * n + HD, HPJ * j + h, :], start=True, stop=True)
                last.then_inc(sem("scores_done"), 1)

            def turn_probs(s):
                pe.wait_ge(sem("att_ready"), s + 1)
                if s:
                    pe.wait_ge(sem("aT_copied"), s)
                turn_blocks(4, att[s % 2]).then_inc(sem("aT_done"), 1)

            def values(s):
                j, t, h = STEPS[s]
                hh = HPJ * j + h
                pe.wait_ge(sem("aT_copied"), s + 1)
                out_of_psum(9 if j == 0 else 19)
                if s:
                    pe.wait_ge(sem("o_copied"), s)
                for k in range(KEYT):
                    last = mm(bank(5, 0, P, 0, P), aT[s % 2][:, k * P:k * P + P], vv[:, k, hh * P:hh * P + P],
                              start=(k == 0), stop=(k == KEYT - 1))
                last.then_inc(sem("pv_done"), 1)

            prev = 9
            for s in range(NS + 2):
                for kind, i in FILL.get(s, []):
                    if kind == "g":
                        group(i)
                        turn(prev)
                        prev = i
                    else:
                        if i == 4:
                            out_of_psum(18)
                            out_of_psum(19)
                        adaln(i, i, early(("mod", i)), 0, 1)
                if s < NS:
                    scores(s)
                if 1 <= s <= NS:
                    turn_probs(s - 1)
                if s >= 2:
                    values(s - 2)
            wo = [early(("wo", i)) for i in range(2)]
            pe.wait_ge(sem("mod_ready"), NMOD)
            pe.wait_ge(sem("o_copied"), NS)
            for t in range(TT):
                pe.wait_ge(sem("o_normed"), t + 1)
                for b in range(2):
                    turn_blocks((6, 4)[t] + b, osb[:, t, b * NB:(b + 1) * NB]).then_inc(sem("oT_done"), 1)
                pe.wait_ge(sem("oT_copied"), 2 * (t + 1))
                for h in range(2):
                    for k in range(KT):
                        last = mm(bank(2 * t + h), oT[:, k, t * P:t * P + P], wo[h][:, k, :],
                                  start=(k == 0), stop=(k == KT - 1))
                    last.then_inc(sem("unit_used" if t else "mix_done"), 1)

            ROUTE = (4, 6, 5, 7)

            def route(layer):
                for part in range(2 * TT):
                    t, b = part // 2, part % 2
                    pe.wait_ge(sem("tokens_ready"), 2 * TT * layer + t + 1)
                    turn_blocks(ROUTE[part], h2[:, t * D + b * NB:t * D + (b + 1) * NB]).then_inc(sem("h2T_done"), 1)
                pe.wait_ge(sem("h2T_copied"), 4 * (layer + 1))
                for t in range(TT):
                    for k in range(KT):
                        last = mm(bank(4, 0, P, NE * t, NE * t + NE), h2T[:, k, t * P:t * P + P],
                                  rw[:, k * NE:(k + 1) * NE], start=(k == 0), stop=(k == KT - 1), skip_group_check=True)
                last.then_inc(sem("logits_done"), 1)
                pe.wait_ge(sem("sel_ready"), layer + 1)
                tri, one = cst[:, C_TRI:C_TRI + P], cst[:, C_ONE:C_ONE + P]
                for lhs, t, c, first, end in ((tri, 0, 0, 1, 1), (one, 0, 1, 1, 0), (tri, 1, 1, 0, 1),
                                              (one, 0, 2, 1, 0), (one, 1, 2, 0, 1)):
                    last = mm(bank(6, 0, P, NE * c, NE * c + NE), lhs, sel[:, t, :], start=bool(first), stop=bool(end),
                              skip_group_check=True)
                last.then_inc(sem("rank_done"), 1)

            def gather():
                for k in range(KT):
                    for t in range(TT):
                        last = mm(bank(6, 0, P, SLOTS * k, SLOTS * k + SLOTS),
                                  h2[:, t * D + k * P:t * D + k * P + P], sgat[:, t, :],
                                  start=(t == 0), stop=(t == TT - 1), skip_group_check=True)
                return last

            def two_halves(b, lhs, w, k0):
                for k in range(4):
                    for h in range(2):
                        last = mm(ps[SLOTS * h:SLOTS * h + SLOTS, b, :], lhs(k0 + k), w[:, k, h * NB:(h + 1) * NB],
                                  start=(k0 + k == 0), stop=(k0 + k == KT - 1), skip_group_check=True)
                return last

            def scatter(sw):
                for t in range(TT):
                    for h in range(2):
                        last = mm(bank(2 * t + h), sw[SLOTS * h:SLOTS * h + SLOTS, t * P:t * P + P],
                                  ysb[SLOTS * h:SLOTS * h + SLOTS, :], start=False, stop=True, skip_group_check=True)
                return last

            def down_lhs(k):
                return hTt[:, k % 4, SLOTS * (k // 4):SLOTS * (k // 4) + SLOTS]

            def ring_unit(v, turns=0):
                landed(pe, v, turns)
                return slot(ring_slot(v)[0]).rearrange("p (k n) -> p k n", k=4)

            for layer in range(DEPTH):
                route(layer)
                q0 = NE * layer
                pe.wait_ge(sem("ssc_zeroed"), layer + 1)
                for b in range(4):
                    mm(bank(b, 0, P, 0, 2), ssc[:, 0, :], ssc[:, 1, 0:2], start=True, stop=True,
                       skip_group_check=True).then_inc(sem("acc_open"), 1)
                pe.wait_ge(sem("sgat_ready"), q0 + 1)
                gather().then_inc(sem("gather_done"), 1)
                pe.wait_ge(sem("ssc_ready"), q0 + 1)
                turn_blocks(4, tra[:, 128:128 + TT * P], 2).then_inc(sem("sw_turned"), 1)

                def expert(e, j, v, turns, last_one):
                    q = e + q0
                    xb = xT[j % 2]
                    pe.wait_ge(sem("xT_copied"), q + 1)
                    pe.wait_ge(sem("swT_copied"), q + 1)
                    for b in range(2):
                        for n in range(2):
                            two_halves(4 + b, lambda k: xb[:, k, :], ring_unit(v + 2 * b + n, turns), 4 * n)\
                                .then_inc(sem("unit_used"), 1)
                    if not last_one:
                        pe.wait_ge(sem("sgat_ready"), q + 2)
                        gather().then_inc(sem("gather_done"), 1)
                    pe.wait_ge(sem("h_ready"), q + 1)
                    turn_blocks(7, hmid).then_inc(sem("hT_turned"), 1)
                    if not last_one:
                        pe.wait_ge(sem("ssc_ready"), q + 2)
                        turn_blocks(4, tra[:, 128:128 + TT * P], 2).then_inc(sem("sw_turned"), 1)
                        pe.wait_ge(sem("xT_copied"), q + 2)
                    pe.wait_ge(sem("hTt_copied"), q + 1)
                    for n in range(2):
                        two_halves(6, down_lhs, ring_unit(v + 4 + n, turns), 4 * n).then_inc(sem("unit_used"), 1)
                    pe.wait_ge(sem("ys_copied"), q + 1)
                    scatter(swT[j % 2]).then_inc(sem("scattered"), 1)

                def mod_unit(m, v):
                    landed(pe, v)
                    adaln(NMOD + m, m, slot(ring_slot(v)[0]).rearrange("p (k n) -> p k n", k=KT), 5, 7)
                    if m == 5:
                        pe.wait_ge(sem("mod_ready"), NMOD + m + 1)
                        for h in range(2):
                            mm(bank((5, 7)[h]), cst[0:NMOD + 2, C_PSC + P * h:C_PSC + P * h + P], rows[0:NMOD + 2, :],
                               start=True, stop=True).then_inc(sem("psc_done"), 1)
                        pe.wait_ge(sem("psc_applied"), 2)
                    if m in (2, 9, 11):
                        pe.wait_ge(sem("mod_ready"), NMOD + m + 1)

                def pool_unit(v):
                    pe.wait_ge(sem("pool_loaded"), 16)
                    landed(pe, v)
                    w = slot(ring_slot(v)[0])
                    pw = w[:, 0:2048].rearrange("p (k n) -> p k n", k=KT)
                    bd = w[:, 2048:4096].rearrange("p (k g n) -> p k g n", k=TT, g=4)
                    pe.wait_ge(sem("tokens_ready"), 2 * TT)
                    for g in range(4):
                        for k in range(2):
                            kk = 2 * g + k
                            for t in range(TT):
                                last = mm(bank(ROUTE[g], 0, P, k * TOK, (k + 1) * TOK),
                                          h2[:, t * D + kk * P:t * D + kk * P + P], bd[:, t, g, :],
                                          start=(t == 0), stop=(t == TT - 1), skip_group_check=True)
                        last.then_inc(sem("poolT_done"), 1)
                    for t in range(TT):
                        for h in range(2):
                            pe.wait_ge(sem("poolT_copied"), 2 * h + 2 if t == 0 else 4)
                            for g in (2 * h, 2 * h + 1):
                                for k in range(2):
                                    last = mm(bank(2 * t + h, 0, P, (g % 2) * TOK, (g % 2 + 1) * TOK),
                                              poolT[:, 2 * g + k, t * P:t * P + P], pw[:, 2 * g + k, :],
                                              start=(k == 0), stop=(k == 1), skip_group_check=True)
                            last.then_inc(sem("unit_used" if (t, h) == (1, 1) else "mix_done"), 1)

                def further_experts():
                    def body(n, e):
                        pe.wait_ge(sem(f"x{layer}_sel"), n + 1)
                        gather()
                        turn_blocks(4, tra[:, 128:128 + TT * P], 2).then_inc(sem(f"x{layer}_gathered"), 1)
                        pe.wait_ge(sem(f"x{layer}_in"), n + 1)
                        pe.wait_ge(sem(f"x{layer}_loaded"), n * (16 * EU) + 16 * EU)
                        for b in range(2):
                            for u in range(2):
                                last = two_halves(4 + b, lambda k: xT[0][:, k, :],
                                                  slot(2 * b + u).rearrange("p (k n) -> p k n", k=4), 4 * u)
                        last.then_inc(sem(f"x{layer}_up"), 1)
                        pe.wait_ge(sem(f"x{layer}_h"), n + 1)
                        turn_blocks(7, hmid).then_inc(sem(f"x{layer}_turned"), 1)
                        pe.wait_ge(sem(f"x{layer}_hT"), n + 1)
                        for u in range(2):
                            last = two_halves(6, down_lhs, slot(4 + u).rearrange("p (k n) -> p k n", k=4), 4 * u)
                        last.then_inc(sem(f"x{layer}_down"), 1)
                        pe.wait_ge(sem(f"x{layer}_ys"), n + 1)
                        scatter(swT[0]).then_inc(sem(f"x{layer}_scattered"), 1)

                    def first():
                        pe.drain().then_inc(sem(f"x{layer}_down"), 1)
                        pe.drain().then_inc(sem(f"x{layer}_scattered"), 1)
                    further(pe, layer, None, body, first)
                    pe.drain().then_inc(sem("further_done"), 1)

                walk(pe, layer, expert, mod_unit, pool_unit, further_experts)

        @block.scalar
        def _(act):
            def bank(b, n0=0, n1=NB):
                return ps[:, b, n0:n1]

            def load(dst, src, s):
                act.dma_start(dst, src).then_inc(sem(s), 16)

            def load_rows(layer):
                load(rows[0:NMOD, :], mod_b[layer].rearrange("(m n) -> m n", n=NB), "rows_loaded")

            def load_ln(n):
                load(lng[:, :], ln_g[n // 2, n % 2].partition_broadcast(P), "ln_loaded")
                load(lnb[:, :], ln_b[n // 2, n % 2].partition_broadcast(P), "ln_loaded")

            load(crow[0:KT, :], c.rearrange("a (k p) -> (a k) p", p=P), "c_loaded")
            load(crow[KT:2 * KT, :], c_ctx.rearrange("(k p) -> k p", p=P), "c_loaded")
            load(cst[:, :], consts, "consts_loaded")
            load_rows(0)
            load(rows[NMOD:NMOD + 2, :], pool_scale[0].rearrange("(m n) -> m n", n=NB), "rows_loaded")
            load(xl[:, :].rearrange("p (t n) -> p t n", t=TT), x[0].rearrange("(t p) n -> p t n", p=P), "x_loaded")
            load(cin, ctx[0].rearrange("(t p) n -> p t n", p=P), "ctx_loaded")
            load(mod[:, 5 * D:5 * D + 256], rope, "attn_small_loaded")
            load(lamb, attn_lam[0].rearrange("a b -> (a b)").partition_broadcast(P), "attn_small_loaded")
            load(subln[:, :], attn_subln[0].partition_broadcast(P), "attn_small_loaded")
            load(rw[:, :].rearrange("p (k n) -> p k n", k=KT), router_w.rearrange("(k p) n -> p k n", p=P), "router_loaded")
            load(rb[:, :], router_b.partition_broadcast(P), "router_loaded")
            load_ln(0)

            act.wait_ge(sem("c_loaded"), 32)
            nc.scalar.activation(csig[:, :], crow[:, :], ACT.Sigmoid).then_inc(sem("csig_ready"), 1)
            act.wait_ge(sem("lam_sums"), 1)
            nc.scalar.activation(lam[:, 2:4], lam[:, 0:2], ACT.Exp).then_inc(sem("lam_exp"), 1)
            for part in range(2 * KEYT):
                i, b = part // 2, part % 2
                act.wait_ge(sem("hT_done"), part + 1)
                nc.scalar.copy(hT[:, 4 * b:4 * b + 4, i * P:i * P + P],
                               bank(4 + part % 4).rearrange("p (k t) -> p k t", k=4)).then_inc(sem("hT_copied"), 1)

            def evacuate(g):
                kind, j, t = GROUPS[g]
                if EVAC[g][0] != "act":
                    return
                group_done(act, g)
                if kind == "v":
                    dst = vv[:, t, j * NB:(j + 1) * NB]
                else:
                    n = QK_N[g]
                    act.wait_ge(sem("qkT_done"), n - 1)
                    dst = nat[n % 2]
                nc.scalar.copy(dst, bank(g % 2)).then_inc(sem("qkv_out_act"), 1)

            def copy_turned(g):
                if g in QK_N:
                    kind, j, t = GROUPS[g]
                    act.wait_ge(sem("qkT_done"), QK_N[g] + 1)
                    dst = (qT if kind == "q" else kT)[:, HPJ * j:HPJ * (j + 1), t * P:t * P + P]
                    nc.scalar.copy(dst, bank(6).rearrange("p (h t) -> p h t", h=HPJ)).then_inc(sem("qkT_copied"), 1)

            for g in range(10):
                evacuate(g)
                if g:
                    copy_turned(g - 1)
            prev = 9
            for s in range(NS + 2):
                for kind, i in FILL.get(s, []):
                    if kind == "g":
                        evacuate(i)
                        copy_turned(prev)
                        prev = i
                if s < NS:
                    act.wait_ge(sem("nb_ready"), s + 1)
                    for n in range(2):
                        nc.scalar.activation(pr[s % 2][:, n, :], bank(2 + n), ACT.Exp, bias=nb[:, s % 2, n:n + 1],
                                             scale=SCALE, accum_out=sm[:, s % 2, n:n + 1]).then_inc(sem("exp_done"), 1)
                if 1 <= s <= NS:
                    act.wait_ge(sem("aT_done"), s)
                    nc.scalar.copy(aT[(s - 1) % 2], bank(4)).then_inc(sem("aT_copied"), 1)
                if s >= 2:
                    j, t, h = STEPS[s - 2]
                    hh = HPJ * j + h
                    act.wait_ge(sem("pv_done"), s - 1)
                    nc.scalar.activation(bank(5, P, 2 * P), bank(5, 0, P), ACT.Square,
                                         accum_out=ss[:, t, hh:hh + 1]).then_inc(sem("o_squared"), 1)
                    nc.scalar.copy(osb[:, t, hh * P:hh * P + P], bank(5, 0, P)).then_inc(sem("o_copied"), 1)
            act.wait_ge(sem("ss_ready"), 1)
            nc.scalar.activation(small[:, 64:80], small[:, 32:48], ACT.Sqrt).then_inc(sem("ostd_ready"), 1)
            for part in range(2 * TT):
                t, b = part // 2, part % 2
                act.wait_ge(sem("oT_done"), part + 1)
                nc.scalar.copy(oT[:, 4 * b:4 * b + 4, t * P:t * P + P],
                               bank((6, 4)[t] + b).rearrange("p (k t) -> p k t", k=4)).then_inc(sem("oT_copied"), 1)

            def std(n):
                for t in range(TT):
                    act.wait_ge(sem("var_ready"), TT * n + t + 1)
                    nc.scalar.activation(mv[:, 3:4], mv[:, 2:3], ACT.Sqrt).then_inc(sem("std_ready"), 1)

            std(0)
            for layer in range(DEPTH):
                q0 = NE * layer
                act.wait_ge(sem("dn_done"), (2 * layer + 1) * TT)
                load_ln(2 * layer + 1)
                if layer == 0:
                    load_rows(1)
                for part in range(2 * TT):
                    t, b = part // 2, part % 2
                    act.wait_ge(sem("h2T_done"), 4 * layer + part + 1)
                    nc.scalar.copy(h2T[:, 4 * b:4 * b + 4, t * P:t * P + P],
                                   bank((4, 6, 5, 7)[part]).rearrange("p (k t) -> p k t", k=4))\
                        .then_inc(sem("h2T_copied"), 1)
                act.wait_ge(sem("rmax_ready"), layer + 1)
                for t in range(TT):
                    nc.scalar.activation(prob[:, t, :], prob[:, t, :], ACT.Exp, bias=col[:, t:t + 1],
                                         accum_out=col[:, 2 + t:3 + t]).then_inc(sem("rexp_done"), 1)
                act.wait_ge(sem("gather_done"), q0 + 1)
                nc.scalar.copy(work[:, 0:NB], bank(6)).then_inc(sem("xT_copied"), 1)

                def expert(e, j, v, turns, last_one):
                    q = e + q0
                    used(act, v + 1, turns)
                    nc.scalar.activation(sig, bank(4), ACT.Sigmoid).then_inc(sem("sig_ready"), 1)
                    if not last_one:
                        act.wait_ge(sem("gather_done"), q + 2)
                        b = (j + 1) % 2
                        nc.scalar.copy(work[:, b * NB:(b + 1) * NB], bank(6)).then_inc(sem("xT_copied"), 1)
                    used(act, v + 5, turns)
                    nc.scalar.copy(ysb, bank(6)).then_inc(sem("ys_copied"), 1)

                def mod_unit(m, v):
                    if m == 7:
                        std(1)
                        act.wait_ge(sem("dn_done"), 2 * TT)
                        load_ln(2)

                def pool_unit(v):
                    for g in range(4):
                        act.wait_ge(sem("poolT_done"), g + 1)
                        nc.scalar.copy(work[:, g * NB:(g + 1) * NB], bank((4, 6, 5, 7)[g]))\
                            .then_inc(sem("poolT_copied"), 1)
                    std(2)

                def further_experts():
                    def body(n, e):
                        act.wait_ge(sem(f"x{layer}_up"), n + 1)
                        nc.scalar.activation(sig, bank(4), ACT.Sigmoid).then_inc(sem(f"x{layer}_sig"), 1)
                    further(act, layer, None, body)

                walk(act, layer, expert, mod_unit, pool_unit, further_experts)
            std(3)

        @block.vector
        def _(dve):
            v_ = nc.vector
            chain = [0]

            def link(ins):
                chain[0] += 1
                ins.then_inc(sem("dve_chain"), 1)
                dve.wait_ge(sem("dve_chain"), chain[0])

            def bank(b, n0=0, n1=NB):
                return ps[:, b, n0:n1]

            dve.wait_ge(sem("csig_ready"), 1)
            v_.tensor_tensor(crow[:, :], crow[:, :], csig[:, :], ALU.mult).then_inc(sem("crow_ready"), 1)
            dve.wait_ge(sem("attn_small_loaded"), 48)
            lv = lamb.rearrange("p (a b n) -> p a b n", a=2, b=2)
            link(v_.tensor_tensor(ltmp.rearrange("p (a n) -> p a n", a=2), lv[:, :, 0, :], lv[:, :, 1, :], ALU.mult))
            v_.tensor_reduce(lam[:, 0:2], ltmp.rearrange("p (a n) -> p a n", a=2), AX, ALU.add)\
                .then_inc(sem("lam_sums"), 1)
            link(v_.tensor_scalar(subln[:, :], subln[:, :], 1.0 - LAM_INIT, None, ALU.mult))
            dve.wait_ge(sem("lam_exp"), 1)
            link(v_.tensor_tensor(lam[:, 4:5], lam[:, 3:4], lam[:, 2:3], ALU.subtract))
            link(v_.tensor_scalar(lam[:, 5:6], lam[:, 4:5], -LAM_INIT, None, ALU.add))
            dve.wait_ge(sem("ccol_done"), 1)
            csv = cs[:, :].rearrange("p (k n) -> p k n", k=KT)
            for b in range(2):
                v_.tensor_copy(csv[:, :, 16 * b:16 * b + 16],
                               bank(7, KT * b, KT * b + KT).unsqueeze(2).to_broadcast([P, KT, 16]))\
                    .then_inc(sem("cs_ready"), 1)

            def adaln(n, m, done):
                done()
                v_.tensor_copy(modp[:, :], bank(0 if n < NMOD else 5)).then_inc(sem("modp_copied"), 1)
                dve.wait_ge(sem("modb_done"), n + 1)
                one = 0.0 if m // 2 in (SH1, SH2) else 1.0
                v_.tensor_scalar(mod[:, m * NB:(m + 1) * NB], bank(1 if n < NMOD else 7), one, None, ALU.add)\
                    .then_inc(sem("mod_ready"), 1)

            for m in range(4):
                adaln(m, m, lambda: early_used(dve, ("mod", m)))
                dve.wait_ge(sem("modc_done"), m + 1)
                v_.tensor_scalar(modc[:, m * NB:(m + 1) * NB], bank(2), 0.0 if m // 2 == SH1 else 1.0, None, ALU.add)\
                    .then_inc(sem("modc_ready"), 1)
            dve.wait_ge(sem("mod_ready"), 4)
            dve.wait_ge(sem("modc_ready"), 4)
            dve.wait_ge(sem("x_loaded"), 16)
            dve.wait_ge(sem("ctx_loaded"), 16)
            for i in range(KEYT):
                src = xl[:, i * D:(i + 1) * D] if i < TT else cin[:, i - TT, :]
                mm_ = mod if i < TT else modc
                link(v_.tensor_tensor(hnat[:, i, :], src, mm_[:, D:2 * D], ALU.mult))
                v_.tensor_tensor(hnat[:, i, :], hnat[:, i, :], mm_[:, 0:D], ALU.add).then_inc(sem("hnat_ready"), 1)
            dve.wait_ge(sem("hnat_ready"), KEYT)

            def evacuate(g):
                if EVAC[g][0] != "dve":
                    return
                kind, j, t = GROUPS[g]
                n = QK_N[g]
                group_done(dve, g)
                if n >= 2:
                    dve.wait_ge(sem("qkT_done"), n - 1)
                if EVAC[g][1]:
                    dve.wait_ge(sem("qkv_out_dve"), EVAC[g][1])
                heads = 2 * HPJ
                src = bank(g % 2)
                c_ = ropes[:, t, 0, :].unsqueeze(1).to_broadcast([P, heads, HD])
                v_.tensor_tensor(rtmp[0].rearrange("p (h n) -> p h n", h=heads), src.rearrange("p (h n) -> p h n", h=heads),
                                 c_, ALU.mult)
                q4 = HD // 4
                view = src.rearrange("p (h a b n) -> p h a b n", h=heads, a=2, b=2)
                dst = rtmp[1].rearrange("p (h a b n) -> p h a b n", h=heads, a=2, b=2)
                sn = ropes[:, t, 1, :].rearrange("p (a b n) -> p a b n", a=2, b=2)
                for a in range(2):
                    for b in range(2):
                        last = v_.tensor_tensor(dst[:, :, a, b, :], view[:, :, a, 1 - b, :],
                                                sn[:, a, b, :].unsqueeze(1).to_broadcast([P, heads, q4]), ALU.mult)
                link(last)
                v_.tensor_tensor(nat[n % 2], rtmp[0], rtmp[1], ALU.add).then_inc(sem("qkv_out_dve"), 1)

            for g in range(10):
                evacuate(g)
            for s in range(NS):
                for kind, i in FILL.get(s, []):
                    if kind == "g":
                        evacuate(i)
                    else:
                        adaln(i, i, lambda: early_used(dve, ("mod", i)))
                b = s % 2
                dve.wait_ge(sem("scores_done"), s + 1)
                link(v_.tensor_reduce(mx[:, b, :], ps[:, 2:4, :], AX, ALU.max))
                v_.tensor_scalar(nb[:, b, :], mx[:, b, :], -SCALE, None, ALU.mult).then_inc(sem("nb_ready"), 1)
                dve.wait_ge(sem("exp_done"), 2 * s + 2)
                link(v_.reciprocal(rs[:, b, :], sm[:, b, :]))
                link(v_.tensor_tensor(rl[:, b:b + 1], rs[:, b, 1:2], lam[:, 5:6], ALU.mult))
                link(v_.tensor_scalar(pr[b][:, 1, :], pr[b][:, 1, :], rl[:, b:b + 1], None, ALU.mult))
                v_.scalar_tensor_tensor(out=att[b], in0=pr[b][:, 0, :], scalar=rs[:, b, 0:1], in1=pr[b][:, 1, :],
                                        op0=ALU.mult, op1=ALU.add).then_inc(sem("att_ready"), 1)
            dve.wait_ge(sem("o_copied"), NS)
            dve.wait_ge(sem("o_squared"), NS)
            v_.tensor_scalar(small[:, 32:48], small[:, 32:48], 1.0 / P, EPS, ALU.mult, ALU.add).then_inc(sem("ss_ready"), 1)
            dve.wait_ge(sem("ostd_ready"), 1)
            link(v_.reciprocal(small[:, 64:80], small[:, 64:80]))
            for t in range(TT):
                o3 = osb[:, t, :].rearrange("p (h n) -> p h n", h=HEADS)
                link(v_.tensor_tensor(o3, o3, ors[:, t, :].unsqueeze(2).to_broadcast([P, HEADS, P]), ALU.mult))
                v_.tensor_tensor(o3, o3, subln[:, :].unsqueeze(1).to_broadcast([P, HEADS, P]), ALU.mult)\
                    .then_inc(sem("o_normed"), 1)

            def deepnorm(n, t, ready, gate, shift, scale):
                z, xt = h2[:, t * D:(t + 1) * D], xl[:, t * D:(t + 1) * D]
                for h in range(2):
                    c0, c1 = h * NB, (h + 1) * NB
                    ready(h)
                    link(v_.tensor_tensor(z[:, c0:c1], bank(2 * t + h), mod[:, gate * D + c0:gate * D + c1], ALU.mult))
                    link(v_.scalar_tensor_tensor(out=z[:, c0:c1], in0=xt[:, c0:c1], scalar=ALPHA, in1=z[:, c0:c1],
                                                 op0=ALU.mult, op1=ALU.add))
                    link(v_.bn_stats(stat[:, 6 * h:6 * h + 6], z[:, c0:c1]))
                link(v_.bn_aggr(mv[:, 0:2], stat[:, 0:12]))
                v_.tensor_scalar(mv[:, 2:3], mv[:, 1:2], EPS, None, ALU.add).then_inc(sem("var_ready"), 1)
                dve.wait_ge(sem("std_ready"), TT * n + t + 1)
                link(v_.reciprocal(mv[:, 2:3], mv[:, 3:4]))
                link(v_.tensor_scalar(z, z, mv[:, 0:1], mv[:, 2:3], ALU.subtract, ALU.mult))
                if t == 0:
                    dve.wait_ge(sem("ln_loaded"), 32 * (n + 1))
                link(v_.tensor_tensor(z, z, lng[:, :], ALU.mult))
                v_.tensor_tensor(xt, z, lnb[:, :], ALU.add).then_inc(sem("dn_done"), 1)
                if scale is not None:
                    dve.wait_ge(sem("dn_done"), TT * n + t + 1)
                    link(v_.tensor_tensor(z, xt, mod[:, scale * D:(scale + 1) * D], ALU.mult))
                    v_.tensor_tensor(z, z, mod[:, shift * D:(shift + 1) * D], ALU.add).then_inc(sem("tokens_ready"), 1)

            def slots_of(e, io, s_gat, s_sc, n_gat=None):
                for t in range(TT):
                    last = v_.tensor_scalar(sgat[:, t, :], io[:, 0:SLOTS], small[:, bass.ds(e + (128 + NE * t), 1)], None,
                                            ALU.is_equal)
                if s_gat is not None:
                    last.then_inc(s_gat, 1)
                if n_gat is not None:
                    n_gat()
                for t in range(TT):
                    last = v_.tensor_scalar(ssc[:, t, :], io[:, 0:P], small[:, bass.ds(e + (128 + NE * t), 1)],
                                            small[:, bass.ds(e + (64 + NE * t), 1)], ALU.is_equal, ALU.mult)
                last.then_inc(s_sc, 1)

            iota = cst[:, C_IOTA:C_IOTA + P]

            def route(layer):
                dve.wait_ge(sem("logits_done"), layer + 1)
                dve.wait_ge(sem("router_loaded"), 32)
                g8 = [P, TT * NG, EG, EG]
                link(v_.tensor_tensor(prob, bank(4, 0, TT * NE).rearrange("p (t e) -> p t e", t=TT),
                                      rb[:, :].unsqueeze(1).to_broadcast([P, TT, NE]), ALU.add))
                link(v_.tensor_reduce(col[:, 0:2], prob, AX, ALU.max))
                v_.tensor_scalar(col[:, 0:2], col[:, 0:2], -1.0, None, ALU.mult).then_inc(sem("rmax_ready"), 1)
                dve.wait_ge(sem("rexp_done"), TT * (layer + 1))
                link(v_.reciprocal(col[:, 2:4], col[:, 2:4]))
                link(v_.tensor_tensor(prob, prob, col[:, 2:4].unsqueeze(2).to_broadcast([P, TT, NE]), ALU.mult))
                pg = small[:, 0:32].rearrange("p (g j) -> p g j", j=EG)
                over_k, over_j = pg.unsqueeze(2).to_broadcast(g8), pg.unsqueeze(3).to_broadcast(g8)
                pa = pair_a.rearrange("p (g j k) -> p g j k", j=EG, k=EG)
                pb = pair_b.rearrange("p (g j k) -> p g j k", j=EG, k=EG)
                lt = cst[:, C_LT:C_END].rearrange("p (j k) -> p j k", j=EG)
                v_.tensor_tensor(pa, over_k, over_j, ALU.is_gt)
                link(v_.tensor_tensor(pb, over_k, over_j, ALU.is_equal))
                link(v_.tensor_tensor(pb, pb, lt.unsqueeze(1).to_broadcast(g8), ALU.mult))
                link(v_.tensor_tensor(pa, pa, pb, ALU.add))
                link(v_.tensor_reduce(rt, pa, AX, ALU.add))
                link(v_.tensor_scalar(sel, rt, float(2), None, ALU.is_lt))
                link(v_.tensor_tensor(wgt, sel, prob, ALU.mult))
                link(v_.tensor_reduce(gs, small[:, 64:96].rearrange("p (g j) -> p g j", j=EG), AX, ALU.add))
                link(v_.tensor_reduce(col[:, 4:6], gs, AX, ALU.max))
                link(v_.tensor_tensor(gs, gs, col[:, 4:6].unsqueeze(2).to_broadcast([P, TT, NG]), ALU.is_equal))
                g2_ = [P, TT, NG, NG]
                pc = pair[:, 0:TT * NG * NG].rearrange("p (t g k) -> p t g k", t=TT, g=NG)
                link(v_.tensor_tensor(pc, gs.unsqueeze(2).to_broadcast(g2_), lt.unsqueeze(1).to_broadcast(g2_), ALU.mult))
                link(v_.tensor_reduce(gt2, pc, AX, ALU.add))
                link(v_.scalar_tensor_tensor(out=gs, in0=gt2, scalar=0.0, in1=gs, op0=ALU.is_equal, op1=ALU.mult))
                ge = small[:, 160:168].unsqueeze(2).to_broadcast([P, TT * NG, EG])
                sg, wg_ = (small[:, a:a + 32].rearrange("p (g j) -> p g j", j=EG) for a in (32, 64))
                v_.tensor_tensor(sg, sg, ge, ALU.mult).then_inc(sem("sel_ready"), 1)
                link(v_.tensor_tensor(wg_, wg_, ge, ALU.mult))
                link(v_.tensor_reduce(col[:, 6:8], wgt, AX, ALU.add))
                link(v_.reciprocal(col[:, 6:8], col[:, 6:8]))
                link(v_.tensor_tensor(wgt, wgt, col[:, 6:8].unsqueeze(2).to_broadcast([P, TT, NE]), ALU.mult))
                v_.memset(tra[:, 128:128 + TT * P], 0.0).then_inc(sem("ssc_zeroed"), 1)
                dve.wait_ge(sem("rank_done"), layer + 1)
                link(v_.scalar_tensor_tensor(out=rt, in0=bank(6, 0, TT * NE).rearrange("p (t e) -> p t e", t=TT), scalar=1.0,
                                             in1=sel, op0=ALU.add, op1=ALU.mult))
                link(v_.tensor_scalar(rt, rt, -1.0, None, ALU.add))
                link(v_.tensor_reduce(col[:, 8:9], bank(6, TT * NE, (TT + 1) * NE), AX, ALU.max))
                for n in range(1, TOK // SLOTS):
                    last = v_.tensor_scalar(col[:, 3 + n:4 + n], col[:, 8:9], float(n * SLOTS), None, ALU.is_gt)
                link(last)
                link(v_.tensor_tensor(col[:, 4:5], col[:, 4:5], col[:, 5:6], ALU.add))
                link(v_.tensor_tensor(nchunk[:, :], col[:, 4:5], col[:, 6:7], ALU.add))
                v_.tensor_copy(iota_x[:, :], iota).then_inc(sem("routed"), 1)
                dve.wait_ge(sem("acc_open"), 4 * (layer + 1))

            for t in range(TT):
                deepnorm(0, t, lambda h: mixed(dve, 0, t, h), G1, SH2, SC2)
            for layer in range(DEPTH):
                q0 = NE * layer
                route(layer)
                slots_of(0, iota, sem("sgat_ready"), sem("ssc_ready"))
                dve.wait_ge(sem("sw_turned"), q0 + 1)
                v_.tensor_copy(swT[0], bank(4, 0, TT * P)).then_inc(sem("swT_copied"), 1)

                def expert(e, j, v, turns, last_one):
                    q = e + q0
                    if not last_one:
                        dve.wait_ge(sem("gather_done"), q + 1)
                        slots_of(e + 1, iota, sem("sgat_ready"), sem("ssc_ready"),
                                 lambda: dve.wait_ge(sem("sw_turned"), q + 1))
                    dve.wait_ge(sem("sig_ready"), q + 1)
                    v_.tensor_tensor(hmid, bank(4), sig, ALU.mult).then_inc(sem("silu_ready"), 1)
                    dve.wait_ge(sem("silu_ready"), q + 1)
                    used(dve, v + 3, turns)
                    v_.tensor_tensor(hmid, hmid, bank(5), ALU.mult).then_inc(sem("h_ready"), 1)
                    dve.wait_ge(sem("hT_turned"), q + 1)
                    v_.tensor_copy(work[:, 3 * NB:4 * NB], bank(7)).then_inc(sem("hTt_copied"), 1)
                    if not last_one:
                        dve.wait_ge(sem("sw_turned"), q + 2)
                        v_.tensor_copy(swT[(j + 1) % 2], bank(4, 0, TT * P)).then_inc(sem("swT_copied"), 1)

                def mod_unit(m, v):
                    n = NMOD + m
                    if m == 8:
                        moe_norm(0, 1)
                    adaln(n, m, lambda: used(dve, v))
                    if m == 5:
                        dve.wait_ge(sem("mod_ready"), n + 1)
                        for h in range(2):
                            dve.wait_ge(sem("psc_done"), h + 1)
                            g = mod[:, G1 * D + h * NB:G1 * D + (h + 1) * NB]
                            v_.tensor_tensor(g, g, bank((5, 7)[h]), ALU.mult).then_inc(sem("psc_applied"), 1)
                    if m == 5:
                        dve.wait_ge(sem("psc_applied"), 2)

                def moe_norm(layer, t):
                    def ready(h):
                        dve.wait_ge(sem("scattered"), NE * (layer + 1))
                    if layer == 0 and t == 0:
                        dve.wait_ge(sem("mod_ready"), NMOD + 6)
                    deepnorm(2 * layer + 1, t, ready, G2, SH1 if layer == 0 else None, SC1 if layer == 0 else None)

                def pool_unit(v):
                    dve.wait_ge(sem("mod_ready"), NMOD + 10)
                    for t in range(TT):
                        deepnorm(2, t, lambda h: mixed(dve, 1, t, h), G1, SH2, SC2)

                def further_experts():
                    ci_now = [0]

                    def chunk(ci):
                        ci_now[0] = ci
                        v_.tensor_scalar(iota_x[:, :], iota_x[:, :], float(SLOTS), None, ALU.add)\
                            .then_inc(sem(f"x{layer}_iota"), 1)

                    def body(n, e):
                        x_ = f"x{layer}_"
                        dve.wait_ge(sem(x_ + "iota"), ci_now[0] + 1)
                        dve.wait_ge(sem(x_ + "scattered"), n + 1)
                        slots_of(e, iota_x, None, sem(x_ + "sel"))
                        dve.wait_ge(sem(x_ + "gathered"), n + 1)
                        v_.tensor_copy(work[:, 0:NB], bank(6))
                        v_.tensor_copy(swT[0], bank(4, 0, TT * P)).then_inc(sem(x_ + "in"), 1)
                        dve.wait_ge(sem(x_ + "sig"), n + 1)
                        v_.tensor_tensor(hmid, bank(4), sig, ALU.mult).then_inc(sem(x_ + "silu"), 1)
                        dve.wait_ge(sem(x_ + "silu"), n + 1)
                        v_.tensor_tensor(hmid, hmid, bank(5), ALU.mult).then_inc(sem(x_ + "h"), 1)
                        dve.wait_ge(sem(x_ + "turned"), n + 1)
                        v_.tensor_copy(work[:, 3 * NB:4 * NB], bank(7)).then_inc(sem(x_ + "hT"), 1)
                        dve.wait_ge(sem(x_ + "down"), n + 2)
                        v_.tensor_copy(ysb, bank(6)).then_inc(sem(x_ + "ys"), 1)
                    dve.wait_ge(sem("scattered"), NE * (layer + 1))
                    further(dve, layer, chunk, body)
                    dve.wait_ge(sem("further_done"), layer + 1)
                    if layer == 0:
                        moe_norm(0, 0)

                walk(dve, layer, expert, mod_unit, pool_unit, further_experts)
            for t in range(TT):
                moe_norm(1, t)


_INS = ["x", "c", "ctx", "c_ctx", "mod_w", "mod_b", "ln_g", "ln_b", "attn_wqkv", "attn_wo", "attn_lam", "attn_subln",
        "pool_w", "pool_scale", "router_w", "router_b", "moe_wg", "moe_wu", "moe_wd"]


def kernel(**inputs):
    import concourse.bacc as bacc
    import numpy as np
    from concourse.bass_utils import run_bass_kernel_spmd

    nc = bacc.Bacc("TRN2", target_bir_lowering=False, num_devices=1)
    given = {name: np.ascontiguousarray(inputs[name]) for name in _INS}
    given.update(constants())
    arrays, args = {}, []
    for name, a in given.items():
        arrays[f"in_{name}"] = a
        args.append(nc.dram_tensor(f"in_{name}", a.shape, mybir.dt.from_np(a.dtype), kind="ExternalInput").ap())
    args.append(nc.dram_tensor("out_latent", (1, TOK, D), F32, kind="ExternalOutput").ap())
    trunk(nc, *args)
    r = run_bass_kernel_spmd(nc, [arrays], core_ids=[0])
    return r.results[0]["out_latent"]
```

```python
import math
from contextlib import ExitStack

import concourse.bass as bass
from concourse import mybir

F32 = mybir.dt.float32
I32 = mybir.dt.int32
ALU = mybir.AluOpType
ACT = mybir.ActivationFunctionType
AX = mybir.AxisListType.X

P = 128
D = 1024
KT = D // P
TOK = 256
TT = TOK // P
NB = 512
HALF = D // 2
HEADS, HD = 8, 64
HPJ = 4
KEYS = 2 * TOK
KEYT = KEYS // P
NE, NG, EG = 16, 4, 4
SLOTS = 64
DEPTH = 2
ALPHA = (2 * DEPTH) ** 0.25
EPS = 1e-5
LAM_INIT = 0.8 - 0.6 * math.exp(-0.3 * 0)
SCALE = HD ** -0.5
NMOD = 6 * D // NB
SH1, SC1, G1, SH2, SC2, G2 = range(6)

RING = 8
SHIFT = 2
UNIT = 4096
EU = 6
GRP = 4
GU = GRP * EU
TURNS = NE // GRP
INSERT = 1

PHASE_A = ([("mod", m) for m in range(4)]
           + [(k, j) for j in range(2) for k in ("q", "k", "v")] + [("wo", 0), ("wo", 1)])
A_POS = {u: n for n, u in enumerate(PHASE_A)}
NA = len(PHASE_A)
SUMS = [(0, m) for m in range(4, NMOD)] + [(1, m) for m in range(NMOD)]
SUMS0 = NMOD - 4
NSUM = len(SUMS)
EARLY_BC = [(0, m) for m in range(4, 10)]
TAIL_BC = {(0, 12): [(0, 10), (0, 11)] + [(1, m) for m in range(4)],
           (0, 13): [(1, m) for m in range(4, 10)],
           (1, 12): [(1, 10), (1, 11)]}
BC = [(0, m) for m in range(4)] + EARLY_BC + TAIL_BC[0, 12] + TAIL_BC[0, 13] + TAIL_BC[1, 12]
TAIL0 = [("e", n) for n in range(12, NE)] + [("pool", 0)]


def tail_base(what):
    n = (TURNS - 1) * GU
    for w in TAIL0:
        if w == what:
            return n
        n += EU if w[0] == "e" else 1
    raise KeyError(what)


LAYER_BASE = [0, NE * EU + INSERT]

GROUPS = [(kind, j, t) for j in range(2) for kind, n in (("q", 2), ("k", 4), ("v", 4)) for t in range(n)]
EVAC, _n = [], {"dve": 0, "act": 0}
for _kind, _j, _t in GROUPS:
    _e = "dve" if _kind == "q" or (_kind == "k" and _t < TT) else "act"
    EVAC.append((_e, _n[_e]))
    _n[_e] += 1
QK = [g for g, (kind, _, _) in enumerate(GROUPS) if kind != "v"]
QK_N = {g: n for n, g in enumerate(QK)}
STEPS = [(j, t, h) for j in range(2) for t in range(TT) for h in range(HPJ)]
NS = len(STEPS)
FILL = {s: [] for s in range(NS + 3)}
for _s in range(10):
    FILL[_s].append(("g", 10 + _s))
for _s in range(12):
    FILL[_s].append(("r", 8 + _s))
for _s in range(6):
    FILL[12 + _s // 2].append(("b", 4 + _s))

C_ID, C_TRI, C_ONE, C_IOTA, C_SELL, C_SELC = (P * i for i in range(6))
C_ROW = 6 * P
C_PLUS = C_ROW + 2 * NMOD - 1
C_LT = C_PLUS + 1
C_END = C_LT + EG * EG


def constants():
    import numpy as np
    c = np.zeros((P, C_END), np.float32)
    i = np.arange(P)
    c[:, C_ID:C_ID + P] = np.eye(P)
    c[:, C_TRI:C_TRI + P] = i[:, None] < i[None, :]
    c[:, C_ONE:C_ONE + P] = 1
    c[:, C_IOTA:C_IOTA + P] = i[None, :] % SLOTS
    c[:, C_SELL:C_SELL + P] = (i % 32 == 0)[:, None]
    c[:, C_SELC:C_SELC + P] = (i % 32 == 16)[:, None]
    c[:, C_ROW + NMOD - 1] = 1
    c[:NMOD, C_PLUS] = [m // 2 not in (SH1, SH2) for m in range(NMOD)]
    c[:, C_LT:C_END] = (np.arange(EG)[None, :] < np.arange(EG)[:, None]).reshape(-1)

    grid_w, theta = 64, 10000.0
    half = HD // 2
    t = np.arange(TOK)
    inv = (np.float32(theta) ** (-np.arange(0, half, 2, dtype=np.float32) / np.float32(half))).astype(np.float32)
    ar = (t // grid_w).astype(np.float32)[:, None] * inv
    ac = (t % grid_w).astype(np.float32)[:, None] * inv
    ang = np.concatenate([ar, ar, ac, ac], axis=-1)
    q = HD // 4
    sign = np.repeat(np.array([-1, 1, -1, 1], np.float32), q)
    rope = np.stack([np.cos(ang), np.sin(ang) * sign], 1).astype(np.float32)
    rope = np.ascontiguousarray(rope.reshape(TT, P, 2 * HD).transpose(1, 0, 2).reshape(P, -1))

    band = np.zeros((TOK, 4, TOK), np.float32)
    for g, win in enumerate((2, 4, 8, 16)):
        for s in range(TOK):
            lo, hi = max(s - win // 2, 0), min(s - win // 2 + win, TOK)
            band[lo:hi, g, s] = 1.0 / (hi - lo)
            band[s, g, s] -= 1.0
    return {"consts": c, "rope": rope, "band": band.reshape(TOK, -1)}


def trunk(nc, x, c, ctx, c_ctx, mod_w, mod_b, ln_g, ln_b, attn_wqkv, attn_wo, attn_lam, attn_subln,
          pool_w, pool_scale, router_w, router_b, moe_wg, moe_wu, moe_wd, consts, rope, band, out):
    with ExitStack() as st:
        def sb(name, n, dt=F32, p=P):
            return st.enter_context(nc.sbuf_tensor(name, [p, n], dt))

        sems = {}

        def sem(name):
            if name not in sems:
                sems[name] = st.enter_context(nc.semaphore(name))
            return sems[name]

        ring = sb("ring", RING * UNIT)
        mod = sb("mod", 6 * D)
        ln = sb("ln", 2 * D)
        lng, lnb = ln[:, 0:D], ln[:, D:2 * D]
        xl = sb("xl", TT * D)
        h2 = sb("h2", TT * D)
        tra = sb("tra", 2 * D)
        work = sb("work", 2 * D)
        cst = sb("cst", C_END)
        rows = [sb(f"rows{i}", NB, p=NMOD) for i in range(DEPTH)]
        modp = sb("modp", 2 * NB)
        pick = sb("pick", 2 * P, p=NMOD)
        rw = sb("rw", KT * NE)
        rb = sb("rb", NE)
        cs = sb("cs", KT * 32)
        stat = sb("stat", 16)
        mv = sb("mv", 4)
        small = sb("small", 6 * 2 * NE)
        pair = sb("pair", 2 * TT * NG * EG * EG)
        nchunk = sb("nchunk", 1, I32)

        ps = st.enter_context(nc.psum_tensor("ps", [P, 8, NB], F32))
        ident = cst[:, C_ID:C_ID + P]
        row_b, row_g = modp[0:NMOD, 0:NB], modp[0:NMOD, NB:2 * NB]

        def slot(s):
            return ring[:, s * UNIT:(s + 1) * UNIT]

        hT = ring[:, 4 * UNIT:5 * UNIT].rearrange("p (k t) -> p k t", k=KT)
        kT = ring[:, 5 * UNIT:6 * UNIT].rearrange("p (h t) -> p h t", h=HEADS)
        vv = ring[:, 6 * UNIT:7 * UNIT].rearrange("p (t n) -> p t n", t=KEYT)
        hnat = ring[:, 6 * UNIT:7 * UNIT].rearrange("p (t n) -> p t n", t=KEYT)
        qT = [a.rearrange("p (n h t) -> p n h t", n=2, h=HPJ) for a in (ring[:, 7 * UNIT:7 * UNIT + 2048], ln[:, :])]
        osb = ring[:, 7 * UNIT + 2048:8 * UNIT].rearrange("p (t n) -> p t n", t=TT)
        cin = ring[:, 7 * UNIT + 2048:8 * UNIT].rearrange("p (t n) -> p t n", t=TT)
        modc = h2[:, 0:2 * D]
        nat = [h2[:, 0:NB], h2[:, NB:2 * NB]]
        rtmp = [h2[:, 2 * NB:3 * NB], h2[:, 3 * NB:4 * NB]]
        pr = [work[:, b * 2 * NB:(b + 1) * 2 * NB].rearrange("p (n k) -> p n k", n=2) for b in range(2)]
        att = [tra[:, b * NB:(b + 1) * NB] for b in range(2)]
        aT = [tra[:, (2 + b) * NB:(3 + b) * NB] for b in range(2)]
        oT = tra[:, :].rearrange("p (k t) -> p k t", k=KT)
        ropes = mod[:, 5 * D:5 * D + 256].rearrange("p (t c n) -> p t c n", t=TT, c=2)
        lamb = mod[:, 5 * D + 256:5 * D + 512]
        ltmp = mod[:, 5 * D + 512:5 * D + 640]
        mx = small[:, 0:4].rearrange("p (b n) -> p b n", b=2)
        nb = small[:, 4:8].rearrange("p (b n) -> p b n", b=2)
        sm = small[:, 8:12].rearrange("p (b n) -> p b n", b=2)
        rs = small[:, 12:16].rearrange("p (b n) -> p b n", b=2)
        rl = small[:, 16:18]
        ss = small[:, 32:48].rearrange("p (t h) -> p t h", t=TT)
        lam = small[:, 48:56]
        ors = small[:, 64:80].rearrange("p (t h) -> p t h", t=TT)
        subln = mod[:, 5 * D + 640:5 * D + 768]
        crow, csig = work[0:2 * KT, 0:P], work[0:2 * KT, P:2 * P]

        h2T = tra[:, :].rearrange("p (k t) -> p k t", k=KT)
        sgat = tra[:, 0:TT * SLOTS].rearrange("p (t s) -> p t s", t=TT)
        ssc = tra[:, 128:128 + TT * P].rearrange("p (t s) -> p t s", t=TT)
        swT = [tra[:, 384 + 256 * b:640 + 256 * b] for b in range(2)]
        iota_x = tra[:, 896:1024]
        ysb = tra[:, 1024:1536]
        sig = tra[:, 1536:2048]
        xT = [work[:, b * NB:(b + 1) * NB].rearrange("p (k s) -> p k s", k=KT) for b in range(2)]
        hmid = work[:, 2 * NB:3 * NB]
        hTt = work[:, 3 * NB:4 * NB].rearrange("p (j s) -> p j s", j=4)
        poolT = work[:, :].rearrange("p (k t) -> p k t", k=KT)
        prob = small[:, 0:32].rearrange("p (t e) -> p t e", t=TT)
        sel = small[:, 32:64].rearrange("p (t e) -> p t e", t=TT)
        wgt = small[:, 64:96].rearrange("p (t e) -> p t e", t=TT)
        rank = small[:, 96:128].rearrange("p (t e) -> p t e", t=TT)
        rt = small[:, 128:160].rearrange("p (t e) -> p t e", t=TT)
        gs = small[:, 160:168].rearrange("p (t g) -> p t g", t=TT)
        gt2 = small[:, 168:176].rearrange("p (t g) -> p t g", t=TT)
        col = small[:, 176:186]
        pair_a = pair[:, 0:TT * NG * EG * EG]
        pair_b = pair[:, TT * NG * EG * EG:]

        def ring_slot(v):
            return (v + SHIFT) % RING, v // RING + 1

        def landed(eng, v, turns=0):
            s, n = ring_slot(v)
            eng.wait_ge(sem(f"ring_loaded_{s}"), turns * (16 * GU // RING) + 16 * n)

        def used(eng, v, turns=0):
            eng.wait_ge(sem("unit_used"), turns * GU + (NA + v + 1))

        def early_used(eng, unit):
            eng.wait_ge(sem("unit_used"), A_POS[unit] + 1)

        def score_bank(s):
            return 0 if s >= 10 and s % 2 == 0 else 2

        def group_done(eng, g):
            kind, j, t = GROUPS[g]
            if t == (1 if kind == "q" else 3):
                early_used(eng, (kind, j))
            else:
                eng.wait_ge(sem("qkv_done"), sum(1 for k2, _, t2 in GROUPS[:g + 1] if t2 != (1 if k2 == "q" else 3)))

        def mixed(eng, layer, t, h):
            if layer == 0:
                if t == 0:
                    eng.wait_ge(sem("mix_done"), h + 1)
                else:
                    early_used(eng, ("wo", h))
            elif (t, h) == (1, 1):
                used(eng, tail_base(("pool", 0)))
            else:
                eng.wait_ge(sem("mix_done"), 2 + 2 * t + h + 1)

        def tail(layer):
            v = LAYER_BASE[layer] + (TURNS - 1) * GU
            for kind, n in (TAIL0 if layer == 0 else [("e", 12 + j) for j in range(GRP)]):
                yield kind, n, v
                v += EU if kind == "e" else 1

        def walk(eng, layer, expert, broadcasts=None, pool_unit=None, others=None):
            base = LAYER_BASE[layer]
            with eng.Fori(0, TURNS - 1) as i:
                for j in range(GRP):
                    expert(i * GRP + j, j, base + j * EU, i, False)
            for kind, n, v in tail(layer):
                if kind == "e":
                    expert(n, n % GRP, v, 0, n == NE - 1)
                    if (layer, n) in TAIL_BC:
                        broadcasts(TAIL_BC[layer, n])
                    if n == NE - 1:
                        others()
                elif pool_unit is not None:
                    pool_unit(v)

        def further(eng, layer, chunk, body, first=None, end=None):
            eng.wait_ge(sem("routed"), layer + 1)
            chunks = eng.value_load(nchunk[0:1, 0:1], min_val=0, max_val=TOK // SLOTS - 1)
            with eng.If(chunks > 0):
                if first is not None:
                    first()
                with eng.Fori(0, chunks) as ci:
                    if chunk is not None:
                        chunk(ci)
                    with eng.Fori(0, NE) as e:
                        body(ci * NE + e, e)
                if end is not None:
                    end()

        def columns(w, n):
            return w[:, n * NB:(n + 1) * NB].rearrange("(k p) n -> p k n", p=P)

        def early_slot(u):
            return (u, 1) if u < 4 else (u % 2, 1 + (u - 2) // 2)

        block = st.enter_context(nc.Block())

        @block.sync
        def _(sp):
            def load(dst, src, s):
                sp.dma_start(dst, src).then_inc(s, 16)

            for u, (kind, i) in enumerate(PHASE_A):
                if u >= 4:
                    sp.wait_ge(sem("unit_used"), u - 3 if u < 6 else u - 1)
                w, n = {"mod": (mod_w[0], i), "q": (attn_wqkv[0], i), "k": (attn_wqkv[0], 2 + i),
                        "v": (attn_wqkv[0], 4 + i), "wo": (attn_wo[0], i)}[kind]
                s, _ = early_slot(u)
                load(slot(s).rearrange("p (k n) -> p k n", k=KT), columns(w, n), sem(f"early_loaded_{s}"))

            def slot_free(v, turns=0):
                if isinstance(turns, int) and v < 2:
                    sp.wait_ge(sem("summed"), NSUM - 1 + v)
                elif isinstance(turns, int) and v < 6:
                    sp.wait_ge(sem("oT_done"), 2 * TT)
                elif isinstance(turns, int) and v < RING:
                    sp.wait_ge(sem("unit_used"), NA - RING + v + 1)
                else:
                    used(sp, v - RING, turns)

            def load_expert(layer, e, v, turns=0):
                for n in range(EU):
                    slot_free(v + n, turns)
                    s, _ = ring_slot(v + n)
                    w = (moe_wg, moe_wu, moe_wd)[n // 2][layer]
                    src = w[bass.ds(e, 1), (n % 2) * HALF:(n % 2 + 1) * HALF, :].rearrange("e (k p) n -> p (e k) n", p=P)
                    load(slot(s).rearrange("p (k n) -> p k n", k=4), src, sem(f"ring_loaded_{s}"))

            for layer in range(DEPTH):
                base = LAYER_BASE[layer]
                if layer == 0:
                    for j in range(GRP):
                        load_expert(0, j, base + j * EU)
                with sp.Fori(1 - layer, TURNS - 1) as i:
                    for j in range(GRP):
                        load_expert(layer, i * GRP + j, base + j * EU, i)

                def further_loads(last):
                    def body(n, e):
                        used(sp, last)
                        sp.wait_ge(sem(f"x{layer}_down"), n + 1)
                        for u in range(EU):
                            w = (moe_wg, moe_wu, moe_wd)[u // 2][layer]
                            src = w[bass.ds(e, 1), (u % 2) * HALF:(u % 2 + 1) * HALF, :]\
                                .rearrange("e (k p) n -> p (e k) n", p=P)
                            load(slot(u).rearrange("p (k n) -> p k n", k=4), src, sem(f"x{layer}_loaded"))
                    further(sp, layer, None, body,
                            end=lambda: sp.wait_ge(sem("further_done"), layer + 1))

                for kind, n, v in tail(layer):
                    if kind == "e":
                        load_expert(layer, n, v)
                        if n == NE - 1:
                            further_loads(v + EU - 1)
                        continue
                    slot_free(v)
                    s, _ = ring_slot(v)
                    load(slot(s)[:, 0:2048].rearrange("p (k n) -> p k n", k=KT),
                         pool_w[0].rearrange("g (k p) n -> p (g k) n", p=P), sem("pool_loaded"))
                    load(slot(s)[:, 2048:4096].rearrange("p (k n) -> p k n", k=TT),
                         band.rearrange("(k p) n -> p k n", p=P), sem(f"ring_loaded_{s}"))
            for t in range(TT):
                sp.wait_ge(sem("xl_done"), 3 * TT + t + 1)
                load(out[0, t * P:(t + 1) * P, :], xl[:, t * D:(t + 1) * D], sem("stored"))
            sp.wait_ge(sem("stored"), 16 * TT)

        @block.gpsimd
        def _(pool):
            for n, (layer, m) in enumerate(SUMS):
                s = 2 + n % 2
                if n < 2:
                    pool.wait_ge(sem("unit_used"), s + 1)
                else:
                    pool.wait_ge(sem("summed"), n - 1)
                pool.dma_start(slot(s).rearrange("p (k n) -> p k n", k=KT), columns(mod_w[layer], m))\
                    .then_inc(sem(f"sum_loaded_{n % 2}"), 16)

        @block.tensor
        def _(pe):
            mm = nc.tensor.matmul

            def bank(b, p0=0, p1=P, n0=0, n1=NB):
                return ps[p0:p1, b, n0:n1]

            def turn_blocks(b, src, n=4):
                for k in range(n):
                    last = nc.tensor.transpose(bank(b, 0, P, k * P, k * P + P), src[:, k * P:k * P + P], ident)
                return last

            def early(unit):
                s, n = early_slot(A_POS[unit])
                pe.wait_ge(sem(f"early_loaded_{s}"), 16 * n)
                return slot(s).rearrange("p (k n) -> p k n", k=KT)

            def broadcast(b, bk):
                pe.wait_ge(sem("pick_ready"), b + 1)
                layer = BC[b][0]
                mm(bank(bk), pick[0:NMOD, (b % 2) * P:(b % 2 + 1) * P], rows[layer][0:NMOD, :],
                   start=True, stop=True).then_inc(sem("bc_done"), 1)

            pe.wait_ge(sem("consts_loaded"), 16)
            pe.wait_ge(sem("crow_ready"), 1)
            nc.tensor.transpose(bank(7, 0, P, 0, 2 * KT), crow, cst[0:2 * KT, C_ID:C_ID + 2 * KT])\
                .then_inc(sem("ccol_done"), 1)
            pe.wait_ge(sem("cs_ready"), 2)
            pe.wait_ge(sem("rows_loaded_0"), 16)
            for m in range(4):
                w = early(("mod", m))
                for r in range(2):
                    for g in range(4):
                        k = 4 * r + g
                        last = mm(bank(3 * (m % 2), 32 * g, 32 * g + 32), cs[:, 32 * k:32 * k + 32], w[:, k, :],
                                  start=(r == 0), stop=(r == 1), skip_group_check=True)
                last.then_inc(sem("unit_used"), 1)
                pe.wait_ge(sem("modp_copied"), m + 1)
                pe.wait_ge(sem("pick_ready"), m + 1)
                if m:
                    pe.wait_ge(sem("mod_ready"), m)
                    pe.wait_ge(sem("modc_ready"), m)
                for bk, c0 in ((1, C_SELL), (2, C_SELC)):
                    mm(bank(bk), cst[:, c0:c0 + P], modp[:, 0:NB], start=True, stop=False)
                    mm(bank(bk), pick[0:NMOD, (m % 2) * P:(m % 2 + 1) * P], rows[0][0:NMOD, :], start=False, stop=True)\
                        .then_inc(sem("bc_done" if bk == 1 else "modc_done"), 1)

            def row_sum(n):
                layer, m = SUMS[n]
                pe.wait_ge(sem("summed"), n + 1)
                if n == SUMS0:
                    pe.wait_ge(sem("rows_ready"), 1)
                mm(bank(7, 0, NMOD), cst[:, C_ROW + NMOD - 1 - m:C_ROW + 2 * NMOD - 1 - m],
                   modp[:, (n % 2) * NB:(n % 2 + 1) * NB], start=n in (0, SUMS0), stop=n in (SUMS0 - 1, NSUM - 1),
                   skip_group_check=True).then_inc(sem("row_done"), 1)

            for i in range(KEYT):
                pe.wait_ge(sem("hnat_ready"), i + 1)
                for b in range(2):
                    part = 2 * i + b
                    if part >= 4:
                        pe.wait_ge(sem("hT_copied"), part - 3)
                    turn_blocks(4 + part % 4, hnat[:, i, b * NB:(b + 1) * NB]).then_inc(sem("hT_done"), 1)
            pe.wait_ge(sem("hT_copied"), 2 * KEYT)
            pe.wait_ge(sem("modc_ready"), 4)
            pe.wait_ge(sem("mod_ready"), 4)

            def out_of_psum(g):
                e, n = EVAC[g]
                pe.wait_ge(sem(f"qkv_out_{e}"), n + 1)

            def group(g):
                kind, j, t = GROUPS[g]
                w = early((kind, j))
                if g >= 2:
                    out_of_psum(g - 2)
                for k in range(KT):
                    last = mm(bank(g % 2), hT[:, k, t * P:t * P + P], w[:, k, :], start=(k == 0), stop=(k == KT - 1))
                last.then_inc(sem("unit_used" if t == (1 if kind == "q" else 3) else "qkv_done"), 1)

            def turn(g):
                if g in QK_N:
                    n = QK_N[g]
                    out_of_psum(g)
                    if n:
                        pe.wait_ge(sem("qkT_copied"), n)
                    turn_blocks(6, nat[n % 2]).then_inc(sem("qkT_done"), 1)

            for g in range(10):
                group(g)
                if g:
                    turn(g - 1)
                if g >= 2:
                    row_sum(g - 2)

            def scores(s):
                j, t, h = STEPS[s]
                pe.wait_ge(sem("qkT_copied"), 6 * (j + 1))
                pe.wait_ge(sem("q_cleared"), 2)
                if s == 10:
                    out_of_psum(18)
                    out_of_psum(19)
                elif s:
                    pe.wait_ge(sem("exp_done"), 2 * (s if s < 10 else s - 1))
                for n in range(2):
                    last = mm(bank(score_bank(s) + n), qT[j][:, n, h, t * P:t * P + P],
                              kT[:, HPJ * j + h, :], start=True, stop=True)
                last.then_inc(sem("scores_done"), 1)

            def turn_probs(s):
                pe.wait_ge(sem("att_ready"), s + 1)
                if s:
                    pe.wait_ge(sem("aT_copied"), s)
                turn_blocks(4, att[s % 2]).then_inc(sem("aT_done"), 1)

            def values(s):
                j, t, h = STEPS[s]
                hh = HPJ * j + h
                pe.wait_ge(sem("aT_copied"), s + 1)
                out_of_psum(9 if j == 0 else 19)
                if s:
                    pe.wait_ge(sem("o_copied"), s)
                for k in range(KEYT):
                    last = mm(bank(5, 0, P, 0, P), aT[s % 2][:, k * P:k * P + P], vv[:, k, hh * P:hh * P + P],
                              start=(k == 0), stop=(k == KEYT - 1))
                last.then_inc(sem("pv_done"), 1)

            prev = 9
            for s in range(NS + 3):
                for kind, i in FILL[s]:
                    if kind == "g":
                        group(i)
                        turn(prev)
                        prev = i
                    elif kind == "r":
                        row_sum(i)
                    else:
                        if i == 4:
                            pe.wait_ge(sem("qkT_copied"), len(QK))
                        elif i == 5:
                            pe.wait_ge(sem("rows_ready"), 2)
                        else:
                            pe.wait_ge(sem("mod_ready"), i - 1)
                        broadcast(i, 6 + i % 2)
                if s < NS:
                    scores(s)
                if 2 <= s < NS + 2:
                    turn_probs(s - 2)
                if s >= 3:
                    values(s - 3)
            wo = [early(("wo", i)) for i in range(2)]
            pe.wait_ge(sem("mod_ready"), 4 + len(EARLY_BC))
            pe.wait_ge(sem("o_copied"), NS)
            for t in range(TT):
                pe.wait_ge(sem("o_normed"), t + 1)
                for b in range(2):
                    turn_blocks((6, 4)[t] + b, osb[:, t, b * NB:(b + 1) * NB]).then_inc(sem("oT_done"), 1)
                pe.wait_ge(sem("oT_copied"), 2 * (t + 1))
                for h in range(2):
                    for k in range(KT):
                        last = mm(bank(2 * t + h), oT[:, k, t * P:t * P + P], wo[h][:, k, :],
                                  start=(k == 0), stop=(k == KT - 1))
                    last.then_inc(sem("unit_used" if t else "mix_done"), 1)

            ROUTE = (4, 6, 5, 7)

            def route(layer):
                for part in range(2 * TT):
                    t, b = part // 2, part % 2
                    pe.wait_ge(sem("tokens_ready"), 2 * TT * layer + t + 1)
                    turn_blocks(ROUTE[part], h2[:, t * D + b * NB:t * D + (b + 1) * NB]).then_inc(sem("h2T_done"), 1)
                pe.wait_ge(sem("h2T_copied"), 4 * (layer + 1))
                for t in range(TT):
                    for k in range(KT):
                        last = mm(bank(4, 0, P, NE * t, NE * t + NE), h2T[:, k, t * P:t * P + P],
                                  rw[:, k * NE:(k + 1) * NE], start=(k == 0), stop=(k == KT - 1), skip_group_check=True)
                last.then_inc(sem("logits_done"), 1)
                pe.wait_ge(sem("sel_ready"), layer + 1)
                tri, one = cst[:, C_TRI:C_TRI + P], cst[:, C_ONE:C_ONE + P]
                for lhs, t, c, first, end in ((tri, 0, 0, 1, 1), (one, 0, 1, 1, 0), (tri, 1, 1, 0, 1),
                                              (one, 0, 2, 1, 0), (one, 1, 2, 0, 1)):
                    last = mm(bank(6, 0, P, NE * c, NE * c + NE), lhs, sel[:, t, :], start=bool(first), stop=bool(end),
                              skip_group_check=True)
                last.then_inc(sem("rank_done"), 1)

            def gather():
                for k in range(KT):
                    for t in range(TT):
                        last = mm(bank(6, 0, P, SLOTS * k, SLOTS * k + SLOTS),
                                  h2[:, t * D + k * P:t * D + k * P + P], sgat[:, t, :],
                                  start=(t == 0), stop=(t == TT - 1), skip_group_check=True)
                return last

            def two_halves(b, lhs, w, k0):
                for k in range(4):
                    for h in range(2):
                        last = mm(ps[SLOTS * h:SLOTS * h + SLOTS, b, :], lhs(k0 + k), w[:, k, h * NB:(h + 1) * NB],
                                  start=(k0 + k == 0), stop=(k0 + k == KT - 1), skip_group_check=True)
                return last

            def scatter(sw):
                for t in range(TT):
                    for h in range(2):
                        last = mm(bank(2 * t + h), sw[SLOTS * h:SLOTS * h + SLOTS, t * P:t * P + P],
                                  ysb[SLOTS * h:SLOTS * h + SLOTS, :], start=False, stop=True, skip_group_check=True)
                return last

            def down_lhs(k):
                return hTt[:, k % 4, SLOTS * (k // 4):SLOTS * (k // 4) + SLOTS]

            def ring_unit(v, turns=0):
                landed(pe, v, turns)
                return slot(ring_slot(v)[0]).rearrange("p (k n) -> p k n", k=4)

            for layer in range(DEPTH):
                route(layer)
                q0 = NE * layer
                pe.wait_ge(sem("ssc_zeroed"), layer + 1)
                for b in range(4):
                    mm(bank(b, 0, P, 0, 2), ssc[:, 0, :], ssc[:, 1, 0:2], start=True, stop=True,
                       skip_group_check=True).then_inc(sem("acc_open"), 1)
                pe.wait_ge(sem("sgat_ready"), q0 + 1)
                gather().then_inc(sem("gather_done"), 1)
                pe.wait_ge(sem("ssc_ready"), q0 + 1)
                turn_blocks(4, tra[:, 128:128 + TT * P], 2).then_inc(sem("sw_turned"), 1)

                def expert(e, j, v, turns, last_one):
                    q = e + q0
                    xb = xT[j % 2]
                    pe.wait_ge(sem("xT_copied"), q + 1)
                    pe.wait_ge(sem("swT_copied"), q + 1)
                    for b in range(2):
                        for n in range(2):
                            two_halves(4 + b, lambda k: xb[:, k, :], ring_unit(v + 2 * b + n, turns), 4 * n)\
                                .then_inc(sem("unit_used"), 1)
                    if not last_one:
                        pe.wait_ge(sem("sgat_ready"), q + 2)
                        gather().then_inc(sem("gather_done"), 1)
                    pe.wait_ge(sem("h_ready"), q + 1)
                    turn_blocks(7, hmid).then_inc(sem("hT_turned"), 1)
                    if not last_one:
                        pe.wait_ge(sem("ssc_ready"), q + 2)
                        turn_blocks(4, tra[:, 128:128 + TT * P], 2).then_inc(sem("sw_turned"), 1)
                        pe.wait_ge(sem("xT_copied"), q + 2)
                    pe.wait_ge(sem("hTt_copied"), q + 1)
                    for n in range(2):
                        two_halves(6, down_lhs, ring_unit(v + 4 + n, turns), 4 * n).then_inc(sem("unit_used"), 1)
                    pe.wait_ge(sem("ys_copied"), q + 1)
                    scatter(swT[j % 2]).then_inc(sem("scattered"), 1)

                def broadcasts(what):
                    if (1, 0) in what:
                        pe.wait_ge(sem("terms_ready"), 1)
                        mm(bank(7, 0, NMOD), cst[0:NMOD, C_ID + 2:C_ID + 2 + NMOD], row_b, start=True, stop=True)\
                            .then_inc(sem("terms_moved"), 1)
                        pe.wait_ge(sem("rows_ready"), DEPTH + 1)
                    for row in what:
                        b = BC.index(row)
                        pe.wait_ge(sem("mod_ready"), b - 1)
                        broadcast(b, 5 if b % 2 else 7)
                    pe.wait_ge(sem("mod_ready"), b + 1)

                def pool_unit(v):
                    pe.wait_ge(sem("pool_loaded"), 16)
                    landed(pe, v)
                    w = slot(ring_slot(v)[0])
                    pw = w[:, 0:2048].rearrange("p (k n) -> p k n", k=KT)
                    bd = w[:, 2048:4096].rearrange("p (k g n) -> p k g n", k=TT, g=4)
                    pe.wait_ge(sem("tokens_ready"), 2 * TT)
                    for g in range(4):
                        for k in range(2):
                            kk = 2 * g + k
                            for t in range(TT):
                                last = mm(bank(ROUTE[g], 0, P, k * TOK, (k + 1) * TOK),
                                          h2[:, t * D + kk * P:t * D + kk * P + P], bd[:, t, g, :],
                                          start=(t == 0), stop=(t == TT - 1), skip_group_check=True)
                        last.then_inc(sem("poolT_done"), 1)
                    for t in range(TT):
                        for h in range(2):
                            pe.wait_ge(sem("poolT_copied"), 2 * h + 2 if t == 0 else 4)
                            for g in (2 * h, 2 * h + 1):
                                for k in range(2):
                                    last = mm(bank(2 * t + h, 0, P, (g % 2) * TOK, (g % 2 + 1) * TOK),
                                              poolT[:, 2 * g + k, t * P:t * P + P], pw[:, 2 * g + k, :],
                                              start=(k == 0), stop=(k == 1), skip_group_check=True)
                            last.then_inc(sem("unit_used" if (t, h) == (1, 1) else "mix_done"), 1)

                def further_experts():
                    def body(n, e):
                        pe.wait_ge(sem(f"x{layer}_sel"), n + 1)
                        gather()
                        turn_blocks(4, tra[:, 128:128 + TT * P], 2).then_inc(sem(f"x{layer}_gathered"), 1)
                        pe.wait_ge(sem(f"x{layer}_in"), n + 1)
                        pe.wait_ge(sem(f"x{layer}_loaded"), n * (16 * EU) + 16 * EU)
                        for b in range(2):
                            for u in range(2):
                                last = two_halves(4 + b, lambda k: xT[0][:, k, :],
                                                  slot(2 * b + u).rearrange("p (k n) -> p k n", k=4), 4 * u)
                        last.then_inc(sem(f"x{layer}_up"), 1)
                        pe.wait_ge(sem(f"x{layer}_h"), n + 1)
                        turn_blocks(7, hmid).then_inc(sem(f"x{layer}_turned"), 1)
                        pe.wait_ge(sem(f"x{layer}_hT"), n + 1)
                        for u in range(2):
                            last = two_halves(6, down_lhs, slot(4 + u).rearrange("p (k n) -> p k n", k=4), 4 * u)
                        last.then_inc(sem(f"x{layer}_down"), 1)
                        pe.wait_ge(sem(f"x{layer}_ys"), n + 1)
                        scatter(swT[0]).then_inc(sem(f"x{layer}_scattered"), 1)

                    def first():
                        pe.drain().then_inc(sem(f"x{layer}_down"), 1)
                        pe.drain().then_inc(sem(f"x{layer}_scattered"), 1)
                    further(pe, layer, None, body, first)
                    pe.drain().then_inc(sem("further_done"), 1)

                walk(pe, layer, expert, broadcasts, pool_unit, further_experts)

        @block.scalar
        def _(act):
            def bank(b, n0=0, n1=NB):
                return ps[:, b, n0:n1]

            def load(dst, src, s):
                act.dma_start(dst, src).then_inc(sem(s), 16)

            def load_rows(layer):
                load(rows[layer][0:NMOD, :], mod_b[layer].rearrange("(m n) -> m n", n=NB), f"rows_loaded_{layer}")

            def load_ln(n):
                load(lng, ln_g[n // 2, n % 2].partition_broadcast(P), "ln_loaded")
                load(lnb, ln_b[n // 2, n % 2].partition_broadcast(P), "ln_loaded")

            load(crow[0:KT], c.rearrange("a (k p) -> (a k) p", p=P), "c_loaded")
            load(crow[KT:2 * KT], c_ctx.rearrange("(k p) -> k p", p=P), "c_loaded")
            load(cst[:, :], consts, "consts_loaded")
            load_rows(0)
            load(xl[:, :].rearrange("p (t n) -> p t n", t=TT), x[0].rearrange("(t p) n -> p t n", p=P), "x_loaded")
            load(cin, ctx[0].rearrange("(t p) n -> p t n", p=P), "ctx_loaded")
            load(mod[:, 5 * D:5 * D + 256], rope, "attn_small_loaded")
            load(lamb, attn_lam[0].rearrange("a b -> (a b)").partition_broadcast(P), "attn_small_loaded")
            load(subln, attn_subln[0].partition_broadcast(P), "attn_small_loaded")
            load(rw[:, :].rearrange("p (k n) -> p k n", k=KT), router_w.rearrange("(k p) n -> p k n", p=P), "router_loaded")
            load(rb[:, :], router_b.partition_broadcast(P), "router_loaded")
            load_rows(1)

            act.wait_ge(sem("c_loaded"), 32)
            nc.scalar.activation(csig, crow, ACT.Sigmoid).then_inc(sem("csig_ready"), 1)
            act.wait_ge(sem("lam_sums"), 1)
            nc.scalar.activation(lam[:, 2:4], lam[:, 0:2], ACT.Exp).then_inc(sem("lam_exp"), 1)
            for part in range(2 * KEYT):
                i, b = part // 2, part % 2
                act.wait_ge(sem("hT_done"), part + 1)
                nc.scalar.copy(hT[:, 4 * b:4 * b + 4, i * P:i * P + P],
                               bank(4 + part % 4).rearrange("p (k t) -> p k t", k=4)).then_inc(sem("hT_copied"), 1)

            def evacuate(g):
                kind, j, t = GROUPS[g]
                if EVAC[g][0] != "act":
                    return
                group_done(act, g)
                if kind == "v":
                    dst = vv[:, t, j * NB:(j + 1) * NB]
                else:
                    n = QK_N[g]
                    act.wait_ge(sem("qkT_done"), n - 1)
                    dst = nat[n % 2]
                nc.scalar.copy(dst, bank(g % 2)).then_inc(sem("qkv_out_act"), 1)

            def copy_turned(g):
                if g in QK_N:
                    kind, j, t = GROUPS[g]
                    act.wait_ge(sem("qkT_done"), QK_N[g] + 1)
                    src = bank(6).rearrange("p (h t) -> p h t", h=HPJ)
                    if kind == "k":
                        last = nc.scalar.copy(kT[:, HPJ * j:HPJ * (j + 1), t * P:t * P + P], src)
                    else:
                        for n in range(2):
                            last = nc.scalar.copy(qT[j][HD * n:HD * n + HD, n, :, t * P:t * P + P],
                                                  src[HD * n:HD * n + HD])
                    last.then_inc(sem("qkT_copied"), 1)

            for g in range(10):
                evacuate(g)
                if g:
                    copy_turned(g - 1)
            prev = 9
            for s in range(NS + 3):
                for kind, i in FILL[s]:
                    if kind == "g":
                        evacuate(i)
                        copy_turned(prev)
                        prev = i
                if s < NS:
                    act.wait_ge(sem("nb_ready"), s + 1)
                    for n in range(2):
                        nc.scalar.activation(pr[s % 2][:, n, :], bank(score_bank(s) + n), ACT.Exp,
                                             bias=nb[:, s % 2, n:n + 1], scale=SCALE,
                                             accum_out=sm[:, s % 2, n:n + 1]).then_inc(sem("exp_done"), 1)
                    if s == NS - 1:
                        load_ln(0)
                if 2 <= s < NS + 2:
                    act.wait_ge(sem("aT_done"), s - 1)
                    nc.scalar.copy(aT[s % 2], bank(4)).then_inc(sem("aT_copied"), 1)
                if s >= 3:
                    j, t, h = STEPS[s - 3]
                    hh = HPJ * j + h
                    act.wait_ge(sem("pv_done"), s - 2)
                    nc.scalar.activation(bank(5, P, 2 * P), bank(5, 0, P), ACT.Square,
                                         accum_out=ss[:, t, hh:hh + 1]).then_inc(sem("o_squared"), 1)
                    nc.scalar.copy(osb[:, t, hh * P:hh * P + P], bank(5, 0, P)).then_inc(sem("o_copied"), 1)
            act.wait_ge(sem("ss_ready"), 1)
            nc.scalar.activation(small[:, 64:80], small[:, 32:48], ACT.Sqrt).then_inc(sem("ostd_ready"), 1)
            for part in range(2 * TT):
                t, b = part // 2, part % 2
                act.wait_ge(sem("oT_done"), part + 1)
                nc.scalar.copy(oT[:, 4 * b:4 * b + 4, t * P:t * P + P],
                               bank((6, 4)[t] + b).rearrange("p (k t) -> p k t", k=4)).then_inc(sem("oT_copied"), 1)

            def std(n):
                for t in range(TT):
                    act.wait_ge(sem("var_ready"), TT * n + t + 1)
                    nc.scalar.activation(mv[:, 3:4], mv[:, 2:3], ACT.Sqrt).then_inc(sem("std_ready"), 1)

            def load_norms():
                act.wait_ge(sem("rows_cleared"), 1)
                two = lambda a: a.rearrange("(m n) -> m n", n=NB)
                for row, n in ((2 * SC1, 1), (2 * SC2, 2)):
                    load(row_g[row:row + 2, :], two(ln_g[n // 2, n % 2]), "joins_loaded")
                    load(row_b[row:row + 2, :], two(ln_b[n // 2, n % 2]), "joins_loaded")
                load(row_g[2 * G1:2 * G1 + 2, :], two(pool_scale[0]), "joins_loaded")
                act.wait_ge(sem("xl_done"), TT)
                load_ln(1)

            std(0)
            for layer in range(DEPTH):
                q0 = NE * layer
                for part in range(2 * TT):
                    t, b = part // 2, part % 2
                    act.wait_ge(sem("h2T_done"), 4 * layer + part + 1)
                    nc.scalar.copy(h2T[:, 4 * b:4 * b + 4, t * P:t * P + P],
                                   bank((4, 6, 5, 7)[part]).rearrange("p (k t) -> p k t", k=4))\
                        .then_inc(sem("h2T_copied"), 1)
                act.wait_ge(sem("rmax_ready"), layer + 1)
                for t in range(TT):
                    nc.scalar.activation(prob[:, t, :], prob[:, t, :], ACT.Exp, bias=col[:, t:t + 1],
                                         accum_out=col[:, 2 + t:3 + t]).then_inc(sem("rexp_done"), 1)
                act.wait_ge(sem("gather_done"), q0 + 1)
                nc.scalar.copy(work[:, 0:NB], bank(6)).then_inc(sem("xT_copied"), 1)
                if layer == 0:
                    load_norms()

                def expert(e, j, v, turns, last_one):
                    q = e + q0
                    used(act, v + 1, turns)
                    nc.scalar.activation(sig, bank(4), ACT.Sigmoid).then_inc(sem("sig_ready"), 1)
                    if not last_one:
                        act.wait_ge(sem("gather_done"), q + 2)
                        b = (j + 1) % 2
                        nc.scalar.copy(work[:, b * NB:(b + 1) * NB], bank(6)).then_inc(sem("xT_copied"), 1)
                    used(act, v + 5, turns)
                    nc.scalar.copy(ysb, bank(6)).then_inc(sem("ys_copied"), 1)

                def pool_unit(v):
                    std(1)
                    for g in range(4):
                        act.wait_ge(sem("poolT_done"), g + 1)
                        nc.scalar.copy(work[:, g * NB:(g + 1) * NB], bank((4, 6, 5, 7)[g]))\
                            .then_inc(sem("poolT_copied"), 1)
                    act.wait_ge(sem("xl_done"), 2 * TT)
                    load_ln(2)
                    std(2)

                def further_experts():
                    def body(n, e):
                        act.wait_ge(sem(f"x{layer}_up"), n + 1)
                        nc.scalar.activation(sig, bank(4), ACT.Sigmoid).then_inc(sem(f"x{layer}_sig"), 1)
                    further(act, layer, None, body)

                def broadcasts(what):
                    if layer == 1:
                        act.wait_ge(sem("xl_done"), 3 * TT)
                        load_ln(3)

                walk(act, layer, expert, broadcasts, pool_unit, further_experts)
            std(3)

        @block.vector
        def _(dve):
            v_ = nc.vector
            chain = [0]

            def link(ins):
                chain[0] += 1
                ins.then_inc(sem("dve_chain"), 1)
                dve.wait_ge(sem("dve_chain"), chain[0])

            def bank(b, n0=0, n1=NB):
                return ps[:, b, n0:n1]

            for q_ in qT:
                v_.memset(q_[HD:P, 0, :, :], 0.0)
                v_.memset(q_[0:HD, 1, :, :], 0.0).then_inc(sem("q_cleared"), 1)
            dve.wait_ge(sem("csig_ready"), 1)
            v_.tensor_tensor(crow, crow, csig, ALU.mult).then_inc(sem("crow_ready"), 1)
            dve.wait_ge(sem("attn_small_loaded"), 48)
            lv = lamb.rearrange("p (a b n) -> p a b n", a=2, b=2)
            link(v_.tensor_tensor(ltmp.rearrange("p (a n) -> p a n", a=2), lv[:, :, 0, :], lv[:, :, 1, :], ALU.mult))
            v_.tensor_reduce(lam[:, 0:2], ltmp.rearrange("p (a n) -> p a n", a=2), AX, ALU.add)\
                .then_inc(sem("lam_sums"), 1)
            link(v_.tensor_scalar(subln, subln, 1.0 - LAM_INIT, None, ALU.mult))
            dve.wait_ge(sem("lam_exp"), 1)
            link(v_.tensor_tensor(lam[:, 4:5], lam[:, 3:4], lam[:, 2:3], ALU.subtract))
            link(v_.tensor_scalar(lam[:, 5:6], lam[:, 4:5], -LAM_INIT, None, ALU.add))
            dve.wait_ge(sem("ccol_done"), 1)
            csv = cs[:, :].rearrange("p (k n) -> p k n", k=KT)
            for b in range(2):
                v_.tensor_copy(csv[:, :, 16 * b:16 * b + 16],
                               bank(7, KT * b, KT * b + KT).unsqueeze(2).to_broadcast([P, KT, 16]))\
                    .then_inc(sem("cs_ready"), 1)

            def picker(b, row):
                if b >= 2:
                    dve.wait_ge(sem("bc_done"), min(b, len(BC)) - 1)
                return v_.tensor_copy(pick[:, (b % 2) * P:(b % 2 + 1) * P],
                                      cst[0:NMOD, C_ID + row:C_ID + row + 1].to_broadcast([NMOD, P]))

            def broadcast_out(b, bk):
                layer, m = BC[b]
                dve.wait_ge(sem("bc_done"), b + 1)
                one = 0.0 if layer == 1 or m // 2 in (SH1, SH2) else 1.0
                v_.tensor_scalar(mod[:, m * NB:(m + 1) * NB], bank(bk), one, None, ALU.add).then_inc(sem("mod_ready"), 1)

            dve.wait_ge(sem("consts_loaded"), 16)
            for m in range(4):
                if m >= 2:
                    dve.wait_ge(sem("modc_done"), m - 1)
                picker(m, m).then_inc(sem("pick_ready"), 1)
                early_used(dve, ("mod", m))
                v_.tensor_copy(modp[:, 0:NB], bank(3 * (m % 2))).then_inc(sem("modp_copied"), 1)
                broadcast_out(m, 1)
                dve.wait_ge(sem("modc_done"), m + 1)
                v_.tensor_scalar(modc[:, m * NB:(m + 1) * NB], bank(2), 0.0 if m // 2 == SH1 else 1.0, None, ALU.add)\
                    .then_inc(sem("modc_ready"), 1)

            def unit_sum(n):
                dve.wait_ge(sem(f"sum_loaded_{n % 2}"), 16 * (n // 2 + 1))
                if n >= 2:
                    dve.wait_ge(sem("row_done"), n - 1)
                w = slot(2 + n % 2).rearrange("p (k n) -> p k n", k=KT)
                acc = modp[:, (n % 2) * NB:(n % 2 + 1) * NB]
                for k in range(KT):
                    ck = cs[:, 32 * k:32 * k + 1]
                    if k == 0:
                        ins = v_.tensor_scalar(acc, w[:, 0, :], ck, None, ALU.mult)
                    else:
                        ins = v_.scalar_tensor_tensor(out=acc, in0=w[:, k, :], scalar=ck, in1=acc, op0=ALU.mult,
                                                      op1=ALU.add)
                    if k < KT - 1:
                        link(ins)
                ins.then_inc(sem("summed"), 1)

            def rows_sum(layer):
                dve.wait_ge(sem("row_done"), (SUMS0, NSUM)[layer])
                dve.wait_ge(sem(f"rows_loaded_{layer}"), 16)
                r_ = rows[layer][0:NMOD, :]
                v_.tensor_tensor(r_, r_, ps[0:NMOD, 7, :], ALU.add).then_inc(sem("rows_ready"), 1)

            dve.wait_ge(sem("mod_ready"), 4)
            dve.wait_ge(sem("modc_ready"), 4)
            dve.wait_ge(sem("x_loaded"), 16)
            dve.wait_ge(sem("ctx_loaded"), 16)
            for i in range(KEYT):
                src = xl[:, i * D:(i + 1) * D] if i < TT else cin[:, i - TT, :]
                mm_ = mod if i < TT else modc
                link(v_.tensor_tensor(hnat[:, i, :], src, mm_[:, D:2 * D], ALU.mult))
                v_.tensor_tensor(hnat[:, i, :], hnat[:, i, :], mm_[:, 0:D], ALU.add).then_inc(sem("hnat_ready"), 1)
            dve.wait_ge(sem("hnat_ready"), KEYT)

            def evacuate(g):
                if EVAC[g][0] != "dve":
                    return
                kind, j, t = GROUPS[g]
                n = QK_N[g]
                group_done(dve, g)
                if n >= 2:
                    dve.wait_ge(sem("qkT_done"), n - 1)
                if EVAC[g][1]:
                    dve.wait_ge(sem("qkv_out_dve"), EVAC[g][1])
                heads = 2 * HPJ
                src = bank(g % 2)
                c_ = ropes[:, t, 0, :].unsqueeze(1).to_broadcast([P, heads, HD])
                v_.tensor_tensor(rtmp[0].rearrange("p (h n) -> p h n", h=heads), src.rearrange("p (h n) -> p h n", h=heads),
                                 c_, ALU.mult)
                q4 = HD // 4
                view = src.rearrange("p (h a b n) -> p h a b n", h=heads, a=2, b=2)
                dst = rtmp[1].rearrange("p (h a b n) -> p h a b n", h=heads, a=2, b=2)
                sn = ropes[:, t, 1, :].rearrange("p (a b n) -> p a b n", a=2, b=2)
                for a in range(2):
                    for b in range(2):
                        last = v_.tensor_tensor(dst[:, :, a, b, :], view[:, :, a, 1 - b, :],
                                                sn[:, a, b, :].unsqueeze(1).to_broadcast([P, heads, q4]), ALU.mult)
                link(last)
                v_.tensor_tensor(nat[n % 2], rtmp[0], rtmp[1], ALU.add).then_inc(sem("qkv_out_dve"), 1)

            for g in range(10):
                evacuate(g)
                unit_sum(g)
            rows_sum(0)
            for s in range(NS + 1):
                for kind, i in FILL[s]:
                    if kind == "g":
                        evacuate(i)
                    elif kind == "b":
                        picker(i, BC[i][1]).then_inc(sem("pick_ready"), 1)
                        if i > 4:
                            broadcast_out(i - 1, 6 + (i - 1) % 2)
                if s < NS:
                    b = s % 2
                    dve.wait_ge(sem("scores_done"), s + 1)
                    link(v_.tensor_reduce(mx[:, b, :], ps[:, score_bank(s):score_bank(s) + 2, :], AX, ALU.max))
                    v_.tensor_scalar(nb[:, b, :], mx[:, b, :], -SCALE, None, ALU.mult).then_inc(sem("nb_ready"), 1)
                if s:
                    b = (s - 1) % 2
                    dve.wait_ge(sem("exp_done"), 2 * s)
                    link(v_.reciprocal(rs[:, b, :], sm[:, b, :]))
                    link(v_.tensor_tensor(rl[:, b:b + 1], rs[:, b, 1:2], lam[:, 5:6], ALU.mult))
                    link(v_.tensor_scalar(pr[b][:, 1, :], pr[b][:, 1, :], rl[:, b:b + 1], None, ALU.mult))
                    if s >= 3:
                        dve.wait_ge(sem("aT_done"), s - 2)
                    v_.scalar_tensor_tensor(out=att[b], in0=pr[b][:, 0, :], scalar=rs[:, b, 0:1], in1=pr[b][:, 1, :],
                                            op0=ALU.mult, op1=ALU.add).then_inc(sem("att_ready"), 1)
                if 10 + s < NSUM:
                    unit_sum(10 + s)
                if s == 11:
                    rows_sum(1)
                    v_.memset(row_b, 0.0)
                    v_.memset(row_g, 1.0).then_inc(sem("rows_cleared"), 1)
            broadcast_out(3 + len(EARLY_BC), 6 + (3 + len(EARLY_BC)) % 2)
            dve.wait_ge(sem("o_copied"), NS)
            dve.wait_ge(sem("o_squared"), NS)
            v_.tensor_scalar(small[:, 32:48], small[:, 32:48], 1.0 / P, EPS, ALU.mult, ALU.add).then_inc(sem("ss_ready"), 1)
            dve.wait_ge(sem("ostd_ready"), 1)
            link(v_.reciprocal(small[:, 64:80], small[:, 64:80]))
            for t in range(TT):
                o3 = osb[:, t, :].rearrange("p (h n) -> p h n", h=HEADS)
                link(v_.tensor_tensor(o3, o3, ors[:, t, :].unsqueeze(2).to_broadcast([P, HEADS, P]), ALU.mult))
                v_.tensor_tensor(o3, o3, subln.unsqueeze(1).to_broadcast([P, HEADS, P]), ALU.mult)\
                    .then_inc(sem("o_normed"), 1)

            def fuse(shift, scale):
                dve.wait_ge(sem("ln_loaded"), 32)
                sc_, sh_ = mod[:, scale * D:(scale + 1) * D], mod[:, shift * D:(shift + 1) * D]
                z = h2[:, 0:D]
                link(v_.tensor_tensor(z, sc_, lnb, ALU.mult))
                link(v_.tensor_tensor(sh_, sh_, z, ALU.add))
                link(v_.tensor_tensor(sc_, sc_, lng, ALU.mult))

            def join_rows():
                dve.wait_ge(sem("joins_loaded"), 5 * 16)
                r_ = rows[1][:, :]
                link(v_.tensor_scalar(r_, r_, cst[0:NMOD, C_PLUS:C_PLUS + 1], None, ALU.add))
                v_.tensor_tensor(row_b, row_b, r_, ALU.mult).then_inc(sem("terms_ready"), 1)
                dve.wait_ge(sem("terms_ready"), 1)
                link(v_.tensor_tensor(r_, r_, row_g, ALU.mult))
                dve.wait_ge(sem("terms_moved"), 1)
                v_.tensor_tensor(r_, r_, ps[0:NMOD, 7, :], ALU.add).then_inc(sem("rows_ready"), 1)

            def deepnorm(n, ready, gate, shift=None, scale=None):
                def tokens(t):
                    z = xl[:, t * D:(t + 1) * D]
                    for h in range(2):
                        c0, c1 = h * NB, (h + 1) * NB
                        ready(t, h)
                        y = h2[:, t * D + c0:t * D + c1]
                        link(v_.tensor_tensor(y, bank(2 * t + h), mod[:, gate * D + c0:gate * D + c1], ALU.mult))
                        link(v_.scalar_tensor_tensor(out=z[:, c0:c1], in0=z[:, c0:c1], scalar=ALPHA, in1=y,
                                                     op0=ALU.mult, op1=ALU.add))
                        link(v_.bn_stats(stat[:, 6 * h:6 * h + 6], z[:, c0:c1]))
                    link(v_.bn_aggr(mv[:, 0:2], stat[:, 0:12]))
                    v_.tensor_scalar(mv[:, 2:3], mv[:, 1:2], EPS, None, ALU.add).then_inc(sem("var_ready"), 1)
                    dve.wait_ge(sem("std_ready"), TT * n + t + 1)
                    link(v_.reciprocal(mv[:, 2:3], mv[:, 3:4]))
                    link(v_.tensor_scalar(z, z, mv[:, 0:1], mv[:, 2:3], ALU.subtract, ALU.mult))
                    if scale is not None:
                        hh = h2[:, t * D:(t + 1) * D]
                        link(v_.tensor_tensor(hh, z, mod[:, scale * D:(scale + 1) * D], ALU.mult))
                        v_.tensor_tensor(hh, hh, mod[:, shift * D:(shift + 1) * D], ALU.add)\
                            .then_inc(sem("tokens_ready"), 1)

                for t in range(TT):
                    tokens(t)
                    if scale is None:
                        stream(n, t)

            def stream(n, t):
                dve.wait_ge(sem("ln_loaded"), 32 * (n + 1))
                z = xl[:, t * D:(t + 1) * D]
                link(v_.tensor_tensor(z, z, lng, ALU.mult))
                v_.tensor_tensor(z, z, lnb, ALU.add).then_inc(sem("xl_done"), 1)

            def slots_of(e, io, s_gat, s_sc, n_gat=None):
                for t in range(TT):
                    last = v_.tensor_scalar(sgat[:, t, :], io[:, 0:SLOTS], small[:, bass.ds(e + (128 + NE * t), 1)], None,
                                            ALU.is_equal)
                if s_gat is not None:
                    last.then_inc(s_gat, 1)
                if n_gat is not None:
                    n_gat()
                for t in range(TT):
                    last = v_.tensor_scalar(ssc[:, t, :], io[:, 0:P], small[:, bass.ds(e + (128 + NE * t), 1)],
                                            small[:, bass.ds(e + (64 + NE * t), 1)], ALU.is_equal, ALU.mult)
                last.then_inc(s_sc, 1)

            iota = cst[:, C_IOTA:C_IOTA + P]

            def route(layer):
                dve.wait_ge(sem("logits_done"), layer + 1)
                dve.wait_ge(sem("router_loaded"), 32)
                g8 = [P, TT * NG, EG, EG]
                link(v_.tensor_tensor(prob, bank(4, 0, TT * NE).rearrange("p (t e) -> p t e", t=TT),
                                      rb[:, :].unsqueeze(1).to_broadcast([P, TT, NE]), ALU.add))
                link(v_.tensor_reduce(col[:, 0:2], prob, AX, ALU.max))
                v_.tensor_scalar(col[:, 0:2], col[:, 0:2], -1.0, None, ALU.mult).then_inc(sem("rmax_ready"), 1)
                dve.wait_ge(sem("rexp_done"), TT * (layer + 1))
                link(v_.reciprocal(col[:, 2:4], col[:, 2:4]))
                link(v_.tensor_tensor(prob, prob, col[:, 2:4].unsqueeze(2).to_broadcast([P, TT, NE]), ALU.mult))
                pg = small[:, 0:32].rearrange("p (g j) -> p g j", j=EG)
                over_k, over_j = pg.unsqueeze(2).to_broadcast(g8), pg.unsqueeze(3).to_broadcast(g8)
                pa = pair_a.rearrange("p (g j k) -> p g j k", j=EG, k=EG)
                pb = pair_b.rearrange("p (g j k) -> p g j k", j=EG, k=EG)
                lt = cst[:, C_LT:C_END].rearrange("p (j k) -> p j k", j=EG)
                v_.tensor_tensor(pa, over_k, over_j, ALU.is_gt)
                link(v_.tensor_tensor(pb, over_k, over_j, ALU.is_equal))
                link(v_.tensor_tensor(pb, pb, lt.unsqueeze(1).to_broadcast(g8), ALU.mult))
                link(v_.tensor_tensor(pa, pa, pb, ALU.add))
                link(v_.tensor_reduce(rt, pa, AX, ALU.add))
                link(v_.tensor_scalar(sel, rt, float(2), None, ALU.is_lt))
                link(v_.tensor_tensor(wgt, sel, prob, ALU.mult))
                link(v_.tensor_reduce(gs, small[:, 64:96].rearrange("p (g j) -> p g j", j=EG), AX, ALU.add))
                link(v_.tensor_reduce(col[:, 4:6], gs, AX, ALU.max))
                link(v_.tensor_tensor(gs, gs, col[:, 4:6].unsqueeze(2).to_broadcast([P, TT, NG]), ALU.is_equal))
                g2_ = [P, TT, NG, NG]
                pc = pair[:, 0:TT * NG * NG].rearrange("p (t g k) -> p t g k", t=TT, g=NG)
                link(v_.tensor_tensor(pc, gs.unsqueeze(2).to_broadcast(g2_), lt.unsqueeze(1).to_broadcast(g2_), ALU.mult))
                link(v_.tensor_reduce(gt2, pc, AX, ALU.add))
                link(v_.scalar_tensor_tensor(out=gs, in0=gt2, scalar=0.0, in1=gs, op0=ALU.is_equal, op1=ALU.mult))
                ge = small[:, 160:168].unsqueeze(2).to_broadcast([P, TT * NG, EG])
                sg, wg_ = (small[:, a:a + 32].rearrange("p (g j) -> p g j", j=EG) for a in (32, 64))
                v_.tensor_tensor(sg, sg, ge, ALU.mult).then_inc(sem("sel_ready"), 1)
                link(v_.tensor_tensor(wg_, wg_, ge, ALU.mult))
                link(v_.tensor_reduce(col[:, 6:8], wgt, AX, ALU.add))
                link(v_.reciprocal(col[:, 6:8], col[:, 6:8]))
                link(v_.tensor_tensor(wgt, wgt, col[:, 6:8].unsqueeze(2).to_broadcast([P, TT, NE]), ALU.mult))
                v_.memset(tra[:, 128:128 + TT * P], 0.0).then_inc(sem("ssc_zeroed"), 1)
                dve.wait_ge(sem("rank_done"), layer + 1)
                link(v_.scalar_tensor_tensor(out=rt, in0=bank(6, 0, TT * NE).rearrange("p (t e) -> p t e", t=TT), scalar=1.0,
                                             in1=sel, op0=ALU.add, op1=ALU.mult))
                link(v_.tensor_scalar(rt, rt, -1.0, None, ALU.add))
                link(v_.tensor_reduce(col[:, 8:9], bank(6, TT * NE, (TT + 1) * NE), AX, ALU.max))
                for n in range(1, TOK // SLOTS):
                    last = v_.tensor_scalar(col[:, 3 + n:4 + n], col[:, 8:9], float(n * SLOTS), None, ALU.is_gt)
                link(last)
                link(v_.tensor_tensor(col[:, 4:5], col[:, 4:5], col[:, 5:6], ALU.add))
                link(v_.tensor_tensor(nchunk[:, :], col[:, 4:5], col[:, 6:7], ALU.add))
                v_.tensor_copy(iota_x[:, :], iota).then_inc(sem("routed"), 1)
                dve.wait_ge(sem("acc_open"), 4 * (layer + 1))

            fuse(SH2, SC2)
            deepnorm(0, lambda t, h: mixed(dve, 0, t, h), G1, SH2, SC2)
            for layer in range(DEPTH):
                q0 = NE * layer
                route(layer)
                slots_of(0, iota, sem("sgat_ready"), sem("ssc_ready"))
                dve.wait_ge(sem("sw_turned"), q0 + 1)
                v_.tensor_copy(swT[0], bank(4, 0, TT * P)).then_inc(sem("swT_copied"), 1)
                if layer == 0:
                    for t in range(TT):
                        stream(0, t)

                def expert(e, j, v, turns, last_one):
                    q = e + q0
                    if not last_one:
                        dve.wait_ge(sem("gather_done"), q + 1)
                        slots_of(e + 1, iota, sem("sgat_ready"), sem("ssc_ready"),
                                 lambda: dve.wait_ge(sem("sw_turned"), q + 1))
                    dve.wait_ge(sem("sig_ready"), q + 1)
                    v_.tensor_tensor(hmid, bank(4), sig, ALU.mult).then_inc(sem("silu_ready"), 1)
                    dve.wait_ge(sem("silu_ready"), q + 1)
                    used(dve, v + 3, turns)
                    v_.tensor_tensor(hmid, hmid, bank(5), ALU.mult).then_inc(sem("h_ready"), 1)
                    dve.wait_ge(sem("hT_turned"), q + 1)
                    v_.tensor_copy(work[:, 3 * NB:4 * NB], bank(7)).then_inc(sem("hTt_copied"), 1)
                    if not last_one:
                        dve.wait_ge(sem("sw_turned"), q + 2)
                        v_.tensor_copy(swT[(j + 1) % 2], bank(4, 0, TT * P)).then_inc(sem("swT_copied"), 1)

                def broadcasts(what):
                    first, end = BC.index(what[0]), BC.index(what[-1]) + 1
                    if (1, 0) in what:
                        join_rows()
                    for b in range(first, end, 2):
                        for b2 in (b, b + 1):
                            picker(b2, BC[b2][1]).then_inc(sem("pick_ready"), 1)
                        for b2 in (b, b + 1):
                            broadcast_out(b2, 5 if b2 % 2 else 7)
                    if layer == 1:
                        for t in range(TT):
                            stream(2, t)

                def pool_unit(v):
                    deepnorm(2, lambda t, h: mixed(dve, 1, t, h), G1, SH2, SC2)

                def further_experts():
                    ci_now = [0]

                    def chunk(ci):
                        ci_now[0] = ci
                        v_.tensor_scalar(iota_x[:, :], iota_x[:, :], float(SLOTS), None, ALU.add)\
                            .then_inc(sem(f"x{layer}_iota"), 1)

                    def body(n, e):
                        x_ = f"x{layer}_"
                        dve.wait_ge(sem(x_ + "iota"), ci_now[0] + 1)
                        dve.wait_ge(sem(x_ + "scattered"), n + 1)
                        slots_of(e, iota_x, None, sem(x_ + "sel"))
                        dve.wait_ge(sem(x_ + "gathered"), n + 1)
                        v_.tensor_copy(work[:, 0:NB], bank(6))
                        v_.tensor_copy(swT[0], bank(4, 0, TT * P)).then_inc(sem(x_ + "in"), 1)
                        dve.wait_ge(sem(x_ + "sig"), n + 1)
                        v_.tensor_tensor(hmid, bank(4), sig, ALU.mult).then_inc(sem(x_ + "silu"), 1)
                        dve.wait_ge(sem(x_ + "silu"), n + 1)
                        v_.tensor_tensor(hmid, hmid, bank(5), ALU.mult).then_inc(sem(x_ + "h"), 1)
                        dve.wait_ge(sem(x_ + "turned"), n + 1)
                        v_.tensor_copy(work[:, 3 * NB:4 * NB], bank(7)).then_inc(sem(x_ + "hT"), 1)
                        dve.wait_ge(sem(x_ + "down"), n + 2)
                        v_.tensor_copy(ysb, bank(6)).then_inc(sem(x_ + "ys"), 1)
                    dve.wait_ge(sem("scattered"), NE * (layer + 1))
                    further(dve, layer, chunk, body,
                            end=lambda: dve.wait_ge(sem("further_done"), layer + 1))
                    if layer == 0:
                        deepnorm(1, lambda t, h: None, G2, SH1, SC1)
                        for t in range(TT):
                            stream(1, t)

                walk(dve, layer, expert, broadcasts, pool_unit, further_experts)
            deepnorm(3, lambda t, h: None, G2)


_INS = ["x", "c", "ctx", "c_ctx", "mod_w", "mod_b", "ln_g", "ln_b", "attn_wqkv", "attn_wo", "attn_lam", "attn_subln",
        "pool_w", "pool_scale", "router_w", "router_b", "moe_wg", "moe_wu", "moe_wd"]


def kernel(**inputs):
    import concourse.bacc as bacc
    import numpy as np
    from concourse.bass_utils import run_bass_kernel_spmd

    nc = bacc.Bacc("TRN2", target_bir_lowering=False, num_devices=1)
    given = {name: np.ascontiguousarray(inputs[name]) for name in _INS}
    given.update(constants())
    arrays, args = {}, []
    for name, a in given.items():
        arrays[f"in_{name}"] = a
        args.append(nc.dram_tensor(f"in_{name}", a.shape, mybir.dt.from_np(a.dtype), kind="ExternalInput").ap())
    args.append(nc.dram_tensor("out_latent", (1, TOK, D), F32, kind="ExternalOutput").ap())
    trunk(nc, *args)
    r = run_bass_kernel_spmd(nc, [arrays], core_ids=[0])
    return r.results[0]["out_latent"]
```

```python
import math
from contextlib import ExitStack

import concourse.bass as bass
from concourse import mybir

F32 = mybir.dt.float32
I32 = mybir.dt.int32
ALU = mybir.AluOpType
ACT = mybir.ActivationFunctionType
AX = mybir.AxisListType.X

P = 128
D = 1024
KT = D // P
TOK = 256
TT = TOK // P
NB = 512
HALF = D // 2
HEADS, HD = 8, 64
HPJ = 4
KEYS = 2 * TOK
KEYT = KEYS // P
NE, NG, EG = 16, 4, 4
SLOTS = 64
DEPTH = 2
ALPHA = (2 * DEPTH) ** 0.25
EPS = 1e-5
LAM_INIT = 0.8 - 0.6 * math.exp(-0.3 * 0)
SCALE = HD ** -0.5
NMOD = 6 * D // NB
SH1, SC1, G1, SH2, SC2, G2 = range(6)

RING = 8
SHIFT = 2
UNIT = 4096
EU = 6
GRP = 4
GU = GRP * EU
TURNS = NE // GRP
INSERT = 1

PHASE_A = ([("mod", m) for m in range(4)]
           + [(k, j) for j in range(2) for k in ("q", "k", "v")] + [("wo", 0), ("wo", 1)])
A_POS = {u: n for n, u in enumerate(PHASE_A)}
NA = len(PHASE_A)
SUMS = [(0, m) for m in range(4, NMOD)] + [(1, m) for m in range(NMOD)]
SUMS0 = NMOD - 4
NSUM = len(SUMS)
EARLY_BC = [(0, m) for m in range(4, 10)]
TAIL_BC = {(0, 12): [(0, 10), (0, 11)] + [(1, m) for m in range(4)],
           (0, 13): [(1, m) for m in range(4, 10)],
           (1, 12): [(1, 10), (1, 11)]}
BC = [(0, m) for m in range(4)] + EARLY_BC + TAIL_BC[0, 12] + TAIL_BC[0, 13] + TAIL_BC[1, 12]
TAIL0 = [("e", n) for n in range(12, NE)] + [("pool", 0)]


def tail_base(what):
    n = (TURNS - 1) * GU
    for w in TAIL0:
        if w == what:
            return n
        n += EU if w[0] == "e" else 1
    raise KeyError(what)


LAYER_BASE = [0, NE * EU + INSERT]

GROUPS = [(kind, j, t) for j in range(2) for kind, n in (("q", 2), ("k", 4), ("v", 4)) for t in range(n)]
EVAC, _n = [], {"dve": 0, "act": 0}
for _kind, _j, _t in GROUPS:
    _e = "dve" if _kind == "q" or (_kind == "k" and _t < TT) else "act"
    EVAC.append((_e, _n[_e]))
    _n[_e] += 1
QK = [g for g, (kind, _, _) in enumerate(GROUPS) if kind != "v"]
QK_N = {g: n for n, g in enumerate(QK)}
STEPS = [(j, t, h) for j in range(2) for t in range(TT) for h in range(HPJ)]
NS = len(STEPS)
FILL = {s: [] for s in range(NS + 3)}
for _s in range(10):
    FILL[_s].append(("g", 10 + _s))
for _s in range(12):
    FILL[_s].append(("r", 8 + _s))
PICK_AT = {10: 4, 11: 5, 12: 6, 13: 7, 14: 8, 15: 9}
BC_AT = {11: (4,), 12: (5,), 13: (6,), 14: (7,), 16: (8, 9)}
BC_BANK = {4: 6, 5: 7, 6: 6, 7: 7, 8: 2, 9: 3}
OUT_AT = {12: (4,), 13: (5,), 14: (6,), 15: (7,), 16: (8, 9)}

C_ID, C_TRI, C_ONE, C_IOTA, C_SELL, C_SELC = (P * i for i in range(6))
C_ROW = 6 * P
C_PLUS = C_ROW + 2 * NMOD - 1
C_LT = C_PLUS + 1
C_SUM = C_LT + EG * EG
C_END = C_SUM + NE


def constants():
    import numpy as np
    c = np.zeros((P, C_END), np.float32)
    i = np.arange(P)
    c[:, C_ID:C_ID + P] = np.eye(P)
    c[:, C_TRI:C_TRI + P] = i[:, None] < i[None, :]
    c[:, C_ONE:C_ONE + P] = 1
    c[:, C_IOTA:C_IOTA + P] = i[None, :] % SLOTS
    c[:, C_SELL:C_SELL + P] = (i % 32 == 0)[:, None]
    c[:, C_SELC:C_SELC + P] = (i % 32 == 16)[:, None]
    c[:, C_ROW + NMOD - 1] = 1
    c[:NMOD, C_PLUS] = [m // 2 not in (SH1, SH2) for m in range(NMOD)]
    c[:, C_LT:C_SUM] = (np.arange(EG)[None, :] < np.arange(EG)[:, None]).reshape(-1)
    c[:, C_SUM:C_END] = (i % 32)[:, None] == np.arange(NE)[None, :]

    grid_w, theta = 64, 10000.0
    half = HD // 2
    t = np.arange(TOK)
    inv = (np.float32(theta) ** (-np.arange(0, half, 2, dtype=np.float32) / np.float32(half))).astype(np.float32)
    ar = (t // grid_w).astype(np.float32)[:, None] * inv
    ac = (t % grid_w).astype(np.float32)[:, None] * inv
    ang = np.concatenate([ar, ar, ac, ac], axis=-1)
    q = HD // 4
    sign = np.repeat(np.array([-1, 1, -1, 1], np.float32), q)
    rope = np.stack([np.cos(ang), np.sin(ang) * sign], 1).astype(np.float32)
    rope = np.ascontiguousarray(rope.reshape(TT, P, 2 * HD).transpose(1, 0, 2).reshape(P, -1))

    band = np.zeros((TOK, 4, TOK), np.float32)
    for g, win in enumerate((2, 4, 8, 16)):
        for s in range(TOK):
            lo, hi = max(s - win // 2, 0), min(s - win // 2 + win, TOK)
            band[lo:hi, g, s] = 1.0 / (hi - lo)
            band[s, g, s] -= 1.0
    return {"consts": c, "rope": rope, "band": band.reshape(TOK, -1)}


def trunk(nc, x, c, ctx, c_ctx, mod_w, mod_b, ln_g, ln_b, attn_wqkv, attn_wo, attn_lam, attn_subln,
          pool_w, pool_scale, router_w, router_b, moe_wg, moe_wu, moe_wd, consts, rope, band, out):
    with ExitStack() as st:
        def sb(name, n, dt=F32, p=P):
            return st.enter_context(nc.sbuf_tensor(name, [p, n], dt))

        sems = {}

        def sem(name):
            if name not in sems:
                sems[name] = st.enter_context(nc.semaphore(name))
            return sems[name]

        ring = sb("ring", RING * UNIT)
        mod = sb("mod", 6 * D)
        ln = sb("ln", 2 * D)
        lng, lnb = ln[:, 0:D], ln[:, D:2 * D]
        xl = sb("xl", TT * D)
        h2 = sb("h2", TT * D)
        tra = sb("tra", 2 * D)
        work = sb("work", 2 * D)
        cst = sb("cst", C_END)
        rows = [sb(f"rows{i}", NB, p=NMOD) for i in range(DEPTH)]
        modp = sb("modp", 2 * NB)
        pick = sb("pick", 2 * P, p=NMOD)
        rw = sb("rw", KT * 32)
        rb = sb("rb", NE)
        cs = sb("cs", KT * 32)
        stat = sb("stat", 16)
        mv = sb("mv", 4 * TT)
        small = sb("small", 6 * 2 * NE)
        nchunk = sb("nchunk", 1, I32)

        ps = st.enter_context(nc.psum_tensor("ps", [P, 8, NB], F32))
        ident = cst[:, C_ID:C_ID + P]
        row_b, row_g = modp[0:NMOD, 0:NB], modp[0:NMOD, NB:2 * NB]

        def slot(s):
            return ring[:, s * UNIT:(s + 1) * UNIT]

        hT = ring[:, 4 * UNIT:5 * UNIT].rearrange("p (k t) -> p k t", k=KT)
        kT = ring[:, 5 * UNIT:6 * UNIT].rearrange("p (h t) -> p h t", h=HEADS)
        vv = ring[:, 6 * UNIT:7 * UNIT].rearrange("p (t n) -> p t n", t=KEYT)
        hnat = ring[:, 6 * UNIT:7 * UNIT].rearrange("p (t n) -> p t n", t=KEYT)
        qT = [a.rearrange("p (n h t) -> p n h t", n=2, h=HPJ) for a in (ring[:, 7 * UNIT:7 * UNIT + 2048], ln[:, :])]
        osb = ring[:, 7 * UNIT + 2048:8 * UNIT].rearrange("p (t n) -> p t n", t=TT)
        cin = ring[:, 7 * UNIT + 2048:8 * UNIT].rearrange("p (t n) -> p t n", t=TT)
        modc = h2[:, 0:2 * D]
        nat = [h2[:, 0:NB], h2[:, NB:2 * NB]]
        rtmp = [h2[:, 2 * NB:3 * NB], h2[:, 3 * NB:4 * NB]]
        pr = [work[:, b * 2 * NB:(b + 1) * 2 * NB].rearrange("p (n k) -> p n k", n=2) for b in range(2)]
        att = [tra[:, b * NB:(b + 1) * NB] for b in range(2)]
        aT = [tra[:, (2 + b) * NB:(3 + b) * NB] for b in range(2)]
        oT = [a[:, 0:D].rearrange("p (k t) -> p k t", k=KT) for a in (h2, tra)]
        ropes = mod[:, 5 * D:5 * D + 256].rearrange("p (t c n) -> p t c n", t=TT, c=2)
        lamb = mod[:, 5 * D + 256:5 * D + 512]
        ltmp = mod[:, 5 * D + 512:5 * D + 640]
        mx = small[:, 0:4].rearrange("p (b n) -> p b n", b=2)
        nb = small[:, 4:8].rearrange("p (b n) -> p b n", b=2)
        sm = small[:, 8:12].rearrange("p (b n) -> p b n", b=2)
        rs = small[:, 12:16].rearrange("p (b n) -> p b n", b=2)
        rl = small[:, 16:18]
        ss = small[:, 32:48].rearrange("p (t h) -> p t h", t=TT)
        lam = small[:, 48:56]
        ors = small[:, 64:80].rearrange("p (t h) -> p t h", t=TT)
        subln = mod[:, 5 * D + 640:5 * D + 768]
        crow, csig = work[0:2 * KT, 0:P], work[0:2 * KT, P:2 * P]

        h2T = tra[:, :].rearrange("p (k t) -> p k t", k=KT)
        sgat = tra[:, 0:TT * SLOTS].rearrange("p (t s) -> p t s", t=TT)
        ssc = tra[:, 128:128 + TT * P].rearrange("p (t s) -> p t s", t=TT)
        swT = [tra[:, 384 + 256 * b:640 + 256 * b] for b in range(2)]
        iota_x = tra[:, 896:1024]
        ysb = tra[:, 1024:1536]
        xrows = ysb
        sig = tra[:, 1536:2048]
        xT = [work[:, b * NB:(b + 1) * NB].rearrange("p (j s) -> p j s", j=4) for b in range(2)]
        hmid = work[:, 2 * NB:3 * NB]
        hTt = work[:, 3 * NB:4 * NB].rearrange("p (j s) -> p j s", j=4)
        poolT = work[:, :].rearrange("p (k t) -> p k t", k=KT)
        lparts = work[:, 0:TOK]
        prob = small[:, 0:32].rearrange("p (t e) -> p t e", t=TT)
        sel = small[:, 32:64].rearrange("p (t e) -> p t e", t=TT)
        wgt = small[:, 64:96].rearrange("p (t e) -> p t e", t=TT)
        rank = small[:, 96:128].rearrange("p (t e) -> p t e", t=TT)
        rt = small[:, 128:160].rearrange("p (t e) -> p t e", t=TT)
        gs = small[:, 160:168].rearrange("p (t g) -> p t g", t=TT)
        gt2 = small[:, 168:176].rearrange("p (t g) -> p t g", t=TT)
        col = small[:, 176:186]
        pair = work[:, 2 * NB:2 * NB + 2 * TT * NG * EG * EG]
        pair_a = pair[:, 0:TT * NG * EG * EG]
        pair_b = pair[:, TT * NG * EG * EG:]

        def ring_slot(v):
            return (v + SHIFT) % RING, v // RING + 1

        def landed(eng, v, turns=0):
            s, n = ring_slot(v)
            eng.wait_ge(sem(f"ring_loaded_{s}"), turns * (16 * GU // RING) + 16 * n)

        def used(eng, v, turns=0):
            eng.wait_ge(sem("unit_used"), turns * GU + (NA + v + 1))

        def early_used(eng, unit):
            eng.wait_ge(sem("unit_used"), A_POS[unit] + 1)

        def score_bank(s):
            return 0 if s in (10, 12, 14) else 2

        def group_done(eng, g):
            kind, j, t = GROUPS[g]
            if t == (1 if kind == "q" else 3):
                early_used(eng, (kind, j))
            else:
                eng.wait_ge(sem("qkv_done"), sum(1 for k2, _, t2 in GROUPS[:g + 1] if t2 != (1 if k2 == "q" else 3)))

        def mixed(eng, layer, t, h):
            if layer == 0:
                if t == 0:
                    eng.wait_ge(sem("mix_done"), 2)
                else:
                    early_used(eng, ("wo", h))
            elif (t, h) == (1, 1):
                used(eng, tail_base(("pool", 0)))
            else:
                eng.wait_ge(sem("mix_done"), 2 + 2 * t + h + 1)

        def tail(layer):
            v = LAYER_BASE[layer] + (TURNS - 1) * GU
            for kind, n in (TAIL0 if layer == 0 else [("e", 12 + j) for j in range(GRP)]):
                yield kind, n, v
                v += EU if kind == "e" else 1

        def walk(eng, layer, expert, broadcasts=None, pool_unit=None, others=None):
            base = LAYER_BASE[layer]
            with eng.Fori(0, TURNS - 1) as i:
                for j in range(GRP):
                    expert(i * GRP + j, j, base + j * EU, i, False)
            for kind, n, v in tail(layer):
                if kind == "e":
                    expert(n, n % GRP, v, 0, n == NE - 1)
                    if (layer, n) in TAIL_BC:
                        broadcasts(TAIL_BC[layer, n])
                    if n == NE - 1:
                        others()
                elif pool_unit is not None:
                    pool_unit(v)

        def further(eng, layer, chunk, body, first=None, end=None):
            eng.wait_ge(sem("routed"), layer + 1)
            chunks = eng.value_load(nchunk[0:1, 0:1], min_val=0, max_val=TOK // SLOTS - 1)
            with eng.If(chunks > 0):
                if first is not None:
                    first()
                with eng.Fori(0, chunks) as ci:
                    if chunk is not None:
                        chunk(ci)
                    with eng.Fori(0, NE) as e:
                        body(ci * NE + e, e)
                if end is not None:
                    end()

        def columns(w, n):
            return w[:, n * NB:(n + 1) * NB].rearrange("(k p) n -> p k n", p=P)

        def early_slot(u):
            return (u, 1) if u < 4 else (u % 2, 1 + (u - 2) // 2)

        block = st.enter_context(nc.Block())

        @block.sync
        def _(sp):
            def load(dst, src, s):
                sp.dma_start(dst, src).then_inc(s, 16)

            load(crow[0:KT], c.rearrange("a (k p) -> (a k) p", p=P), sem("c_loaded"))
            load(crow[KT:2 * KT], c_ctx.rearrange("(k p) -> k p", p=P), sem("c_loaded"))
            load(cst[:, :], consts, sem("consts_loaded"))
            for u, (kind, i) in enumerate(PHASE_A):
                if u >= 4:
                    sp.wait_ge(sem("unit_used"), u - 3 if u < 6 else u - 1)
                w, n = {"mod": (mod_w[0], i), "q": (attn_wqkv[0], i), "k": (attn_wqkv[0], 2 + i),
                        "v": (attn_wqkv[0], 4 + i), "wo": (attn_wo[0], i)}[kind]
                s, _ = early_slot(u)
                load(slot(s).rearrange("p (k n) -> p k n", k=KT), columns(w, n), sem(f"early_loaded_{s}"))
                if u == 0:
                    load(rows[0][:, :], mod_b[0].rearrange("(m n) -> m n", n=NB), sem("rows_loaded_0"))
                if u == 3:
                    load(xl[:, :].rearrange("p (t n) -> p t n", t=TT), x[0].rearrange("(t p) n -> p t n", p=P),
                         sem("x_loaded"))
                    load(cin, ctx[0].rearrange("(t p) n -> p t n", p=P), sem("ctx_loaded"))

            def slot_free(v, turns=0):
                if isinstance(turns, int) and v < 2:
                    sp.wait_ge(sem("summed"), NSUM - 1 + v)
                elif isinstance(turns, int) and v < 6:
                    sp.wait_ge(sem("oT_done"), 2 * TT)
                elif isinstance(turns, int) and v < RING:
                    sp.wait_ge(sem("unit_used"), NA - RING + v + 1)
                else:
                    used(sp, v - RING, turns)

            def load_expert(layer, e, v, turns=0):
                for n in range(EU):
                    slot_free(v + n, turns)
                    s, _ = ring_slot(v + n)
                    w = (moe_wg, moe_wu, moe_wd)[n // 2][layer]
                    src = w[bass.ds(e, 1), (n % 2) * HALF:(n % 2 + 1) * HALF, :].rearrange("e (k p) n -> p (e k) n", p=P)
                    load(slot(s).rearrange("p (k n) -> p k n", k=4), src, sem(f"ring_loaded_{s}"))

            for layer in range(DEPTH):
                base = LAYER_BASE[layer]
                if layer == 0:
                    for j in range(GRP):
                        load_expert(0, j, base + j * EU)
                with sp.Fori(1 - layer, TURNS - 1) as i:
                    for j in range(GRP):
                        load_expert(layer, i * GRP + j, base + j * EU, i)

                def further_loads(last):
                    def body(n, e):
                        used(sp, last)
                        sp.wait_ge(sem(f"x{layer}_down"), n + 1)
                        for u in range(EU):
                            w = (moe_wg, moe_wu, moe_wd)[u // 2][layer]
                            src = w[bass.ds(e, 1), (u % 2) * HALF:(u % 2 + 1) * HALF, :]\
                                .rearrange("e (k p) n -> p (e k) n", p=P)
                            load(slot(u).rearrange("p (k n) -> p k n", k=4), src, sem(f"x{layer}_loaded"))
                    further(sp, layer, None, body,
                            end=lambda: sp.wait_ge(sem("further_done"), layer + 1))

                for kind, n, v in tail(layer):
                    if kind == "e":
                        load_expert(layer, n, v)
                        if n == NE - 1:
                            further_loads(v + EU - 1)
                        continue
                    slot_free(v)
                    s, _ = ring_slot(v)
                    load(slot(s)[:, 0:2048].rearrange("p (k n) -> p k n", k=KT),
                         pool_w[0].rearrange("g (k p) n -> p (g k) n", p=P), sem("pool_loaded"))
                    load(slot(s)[:, 2048:4096].rearrange("p (k n) -> p k n", k=TT),
                         band.rearrange("(k p) n -> p k n", p=P), sem(f"ring_loaded_{s}"))
            for t in range(TT):
                sp.wait_ge(sem("xl_done"), 3 * TT + t + 1)
                load(out[0, t * P:(t + 1) * P, :], xl[:, t * D:(t + 1) * D], sem("stored"))
            sp.wait_ge(sem("stored"), 16 * TT)

        @block.gpsimd
        def _(pool):
            for n, (layer, m) in enumerate(SUMS):
                s = 2 + n % 2
                if n < 2:
                    pool.wait_ge(sem("unit_used"), s + 1)
                else:
                    pool.wait_ge(sem("summed"), n - 1)
                pool.dma_start(slot(s).rearrange("p (k n) -> p k n", k=KT), columns(mod_w[layer], m))\
                    .then_inc(sem(f"sum_loaded_{n % 2}"), 16)

        @block.tensor
        def _(pe):
            mm = nc.tensor.matmul

            def bank(b, p0=0, p1=P, n0=0, n1=NB):
                return ps[p0:p1, b, n0:n1]

            def turn_blocks(b, src, n=4):
                for k in range(n):
                    last = nc.tensor.transpose(bank(b, 0, P, k * P, k * P + P), src[:, k * P:k * P + P], ident)
                return last

            def early(unit):
                s, n = early_slot(A_POS[unit])
                pe.wait_ge(sem(f"early_loaded_{s}"), 16 * n)
                return slot(s).rearrange("p (k n) -> p k n", k=KT)

            def broadcast(b, bk):
                pe.wait_ge(sem("pick_ready"), b + 1)
                layer = BC[b][0]
                mm(bank(bk), pick[0:NMOD, (b % 2) * P:(b % 2 + 1) * P], rows[layer][0:NMOD, :],
                   start=True, stop=True).then_inc(sem("bc_done"), 1)

            pe.wait_ge(sem("consts_loaded"), 16)
            pe.wait_ge(sem("crow_ready"), 1)
            nc.tensor.transpose(bank(7, 0, P, 0, 2 * KT), crow, cst[0:2 * KT, C_ID:C_ID + 2 * KT])\
                .then_inc(sem("ccol_done"), 1)
            pe.wait_ge(sem("cs_ready"), 2)
            pe.wait_ge(sem("rows_loaded_0"), 16)
            for m in range(4 + 1):
                if m < 4:
                    w = early(("mod", m))
                    if m >= 2:
                        pe.wait_ge(sem("modp_copied"), m - 1)
                    for r in range(2):
                        for g in range(4):
                            k = 4 * r + g
                            last = mm(bank(3 * (m % 2), 32 * g, 32 * g + 32), cs[:, 32 * k:32 * k + 32], w[:, k, :],
                                      start=(r == 0), stop=(r == 1), skip_group_check=True)
                    last.then_inc(sem("unit_used"), 1)
                if m:
                    n = m - 1
                    pe.wait_ge(sem("modp_copied"), n + 1)
                    pe.wait_ge(sem("pick_ready"), n + 1)
                    if n >= 2:
                        pe.wait_ge(sem("mod_ready"), n - 1)
                        pe.wait_ge(sem("modc_ready"), n - 1)
                    for bk, c0 in ((1, C_SELL), (2, C_SELC)):
                        to = bank(bk + 4 * (n % 2))
                        mm(to, cst[:, c0:c0 + P], modp[:, (n % 2) * NB:(n % 2 + 1) * NB], start=True, stop=False)
                        mm(to, pick[0:NMOD, (n % 2) * P:(n % 2 + 1) * P], rows[0][0:NMOD, :], start=False, stop=True)\
                            .then_inc(sem("bc_done" if bk == 1 else "modc_done"), 1)

            def row_sum(n):
                layer, m = SUMS[n]
                pe.wait_ge(sem("summed"), n + 1)
                if n == SUMS0:
                    pe.wait_ge(sem("rows_ready"), 1)
                mm(bank(7, 0, NMOD), cst[:, C_ROW + NMOD - 1 - m:C_ROW + 2 * NMOD - 1 - m],
                   modp[:, (n % 2) * NB:(n % 2 + 1) * NB], start=n in (0, SUMS0), stop=n in (SUMS0 - 1, NSUM - 1),
                   skip_group_check=True).then_inc(sem("row_done"), 1)

            pe.wait_ge(sem("modc_ready"), 4)
            pe.wait_ge(sem("mod_ready"), 4)
            for i in range(KEYT):
                pe.wait_ge(sem("hnat_ready"), i + 1)
                for b in range(2):
                    part = 2 * i + b
                    if part >= 4:
                        pe.wait_ge(sem("hT_copied"), part - 3)
                    turn_blocks(4 + part % 4, hnat[:, i, b * NB:(b + 1) * NB]).then_inc(sem("hT_done"), 1)
            pe.wait_ge(sem("hT_copied"), 2 * KEYT)

            def out_of_psum(g):
                e, n = EVAC[g]
                pe.wait_ge(sem(f"qkv_out_{e}"), n + 1)

            def group(g):
                kind, j, t = GROUPS[g]
                w = early((kind, j))
                if g >= 2:
                    out_of_psum(g - 2)
                for k in range(KT):
                    last = mm(bank(g % 2), hT[:, k, t * P:t * P + P], w[:, k, :], start=(k == 0), stop=(k == KT - 1))
                last.then_inc(sem("unit_used" if t == (1 if kind == "q" else 3) else "qkv_done"), 1)

            def turn(g):
                if g in QK_N:
                    n = QK_N[g]
                    out_of_psum(g)
                    if n:
                        pe.wait_ge(sem("qkT_copied"), n)
                    turn_blocks(6, nat[n % 2]).then_inc(sem("qkT_done"), 1)

            for g in range(10):
                group(g)
                if g:
                    turn(g - 1)
                if g >= 2:
                    row_sum(g - 2)

            def scores(s):
                j, t, h = STEPS[s]
                pe.wait_ge(sem("qkT_copied"), 6 * (j + 1))
                pe.wait_ge(sem("q_cleared"), 2)
                if s == 10:
                    out_of_psum(18)
                    out_of_psum(19)
                elif s:
                    pe.wait_ge(sem("exp_done"), 2 * (s if s < 10 else s - 1))
                for n in range(2):
                    last = mm(bank(score_bank(s) + n), qT[j][:, n, h, t * P:t * P + P],
                              kT[:, HPJ * j + h, :], start=True, stop=True)
                last.then_inc(sem("scores_done"), 1)

            def turn_probs(s):
                pe.wait_ge(sem("att_ready"), s + 1)
                if s:
                    pe.wait_ge(sem("aT_copied"), s)
                turn_blocks(4, att[s % 2]).then_inc(sem("aT_done"), 1)

            def values(s):
                j, t, h = STEPS[s]
                hh = HPJ * j + h
                pe.wait_ge(sem("aT_copied"), s + 1)
                out_of_psum(9 if j == 0 else 19)
                if s:
                    pe.wait_ge(sem("o_copied"), s)
                for k in range(KEYT):
                    last = mm(bank(5, 0, P, 0, P), aT[s % 2][:, k * P:k * P + P], vv[:, k, hh * P:hh * P + P],
                              start=(k == 0), stop=(k == KEYT - 1))
                last.then_inc(sem("pv_done"), 1)

            prev = 9
            def turn_heads(t):
                pe.wait_ge(sem("o_normed"), t + 1)
                if t == 0:
                    pe.wait_ge(sem("mod_ready"), 4 + 4)
                for b in range(2):
                    turn_blocks((6, 4)[t] + b, osb[:, t, b * NB:(b + 1) * NB]).then_inc(sem("oT_done"), 1)

            def project(t, h):
                wo = early(("wo", h))
                pe.wait_ge(sem("oT_copied"), 2 * (t + 1))
                for k in range(KT):
                    last = mm(bank(2 * t + h), oT[t][:, k, :], wo[:, k, :], start=(k == 0), stop=(k == KT - 1))
                last.then_inc(sem("unit_used" if t else "mix_done"), 1)

            for s in range(NS + 3):
                for kind, i in FILL[s]:
                    if kind == "g":
                        group(i)
                        turn(prev)
                        prev = i
                    else:
                        row_sum(i)
                if s < NS:
                    scores(s)
                if 2 <= s < NS + 2:
                    turn_probs(s - 2)
                if s >= 3:
                    values(s - 3)
                if s == NS:
                    turn_heads(0)
                    project(0, 0)
                for i in BC_AT.get(s, ()):
                    if i == 4:
                        pe.wait_ge(sem("qkT_copied"), len(QK))
                    elif i == 5:
                        pe.wait_ge(sem("rows_ready"), 2)
                    elif i < 8:
                        pe.wait_ge(sem("mod_ready"), i - 1)
                    else:
                        pe.wait_ge(sem("exp_done"), 2 * NS)
                    broadcast(i, BC_BANK[i])
            project(0, 1)
            pe.wait_ge(sem("mod_ready"), 4 + len(EARLY_BC))
            pe.wait_ge(sem("aT_copied"), NS)
            pe.wait_ge(sem("o_copied"), NS)
            turn_heads(1)
            for h in range(2):
                project(1, h)

            ROUTE = (4, 6, 5, 7)

            def keep_clock(bk, n):
                for _ in range(n):
                    mm(bank(bk), ident, cst[:, 0:NB], start=True, stop=True, skip_group_check=True)

            def route(layer):
                for part in range(2 * TT):
                    t, b = part // 2, part % 2
                    if part == 2:
                        keep_clock(ROUTE[2], 4)
                    pe.wait_ge(sem("tokens_ready"), 2 * TT * layer + t + 1)
                    turn_blocks(ROUTE[part], h2[:, t * D + b * NB:t * D + (b + 1) * NB]).then_inc(sem("h2T_done"), 1)
                pe.wait_ge(sem("h2T_copied"), 4 * (layer + 1))
                pe.wait_ge(sem("router_loaded"), 32)
                pe.wait_ge(sem("rw_padded"), 1)
                for r in range(2):
                    for g in range(4):
                        k = 4 * r + g
                        last = mm(bank(4, 32 * g, 32 * g + 32, 0, TOK), rw[:, 32 * k:32 * k + 32],
                                  h2T[:, k, :], start=(r == 0), stop=(r == 1), skip_group_check=True)
                last.then_inc(sem("parts_done"), 1)
                pe.wait_ge(sem("parts_copied"), layer + 1)
                for t in range(TT):
                    last = mm(bank(5, 0, P, NE * t, NE * t + NE), lparts[:, t * P:t * P + P], cst[:, C_SUM:C_END],
                              start=True, stop=True, skip_group_check=True)
                last.then_inc(sem("logits_done"), 1)
                keep_clock(7, 5)
                pe.wait_ge(sem("sel_ready"), layer + 1)
                tri, one = cst[:, C_TRI:C_TRI + P], cst[:, C_ONE:C_ONE + P]
                for lhs, t, c, first, end in ((tri, 0, 0, 1, 1), (one, 0, 1, 1, 0), (tri, 1, 1, 0, 1),
                                              (one, 0, 2, 1, 0), (one, 1, 2, 0, 1)):
                    last = mm(bank(6, 0, P, NE * c, NE * c + NE), lhs, sel[:, t, :], start=bool(first), stop=bool(end),
                              skip_group_check=True)
                last.then_inc(sem("rank_done"), 1)

            def gather():
                for t in range(TT):
                    for h in range(2):
                        last = mm(ps[SLOTS * h:SLOTS * h + SLOTS, 6, :], sgat[:, t, :],
                                  h2[:, t * D + h * NB:t * D + (h + 1) * NB],
                                  start=(t == 0), stop=(t == TT - 1), skip_group_check=True)
                return last

            def two_halves(b, lhs, w, k0):
                for k in range(4):
                    for h in range(2):
                        last = mm(ps[SLOTS * h:SLOTS * h + SLOTS, b, :], lhs(k0 + k), w[:, k, h * NB:(h + 1) * NB],
                                  start=(k0 + k == 0), stop=(k0 + k == KT - 1), skip_group_check=True)
                return last

            def scatter(sw):
                for t in range(TT):
                    for h in range(2):
                        last = mm(bank(2 * t + h), sw[SLOTS * h:SLOTS * h + SLOTS, t * P:t * P + P],
                                  ysb[SLOTS * h:SLOTS * h + SLOTS, :], start=False, stop=True, skip_group_check=True)
                return last

            def k_tile(turned):
                return lambda k: turned[:, k % 4, SLOTS * (k // 4):SLOTS * (k // 4) + SLOTS]

            def ring_unit(v, turns=0):
                landed(pe, v, turns)
                return slot(ring_slot(v)[0]).rearrange("p (k n) -> p k n", k=4)

            for layer in range(DEPTH):
                route(layer)
                q0 = NE * layer
                pe.wait_ge(sem("ssc_zeroed"), layer + 1)
                for b in range(4):
                    mm(bank(b, 0, P, 0, 2), ssc[:, 0, :], ssc[:, 1, 0:2], start=True, stop=True,
                       skip_group_check=True).then_inc(sem("acc_open"), 1)
                pe.wait_ge(sem("sgat_ready"), q0 + 1)
                gather().then_inc(sem("gather_done"), 1)
                pe.wait_ge(sem("ssc_ready"), q0 + 1)
                turn_blocks(4, tra[:, 128:128 + TT * P], 2).then_inc(sem("sw_turned"), 1)
                pe.wait_ge(sem("xrows_copied"), q0 + 1)
                turn_blocks(6, xrows).then_inc(sem("x_turned"), 1)

                def expert(e, j, v, turns, last_one):
                    q = e + q0
                    xb = xT[j % 2]
                    pe.wait_ge(sem("xT_copied"), q + 1)
                    pe.wait_ge(sem("swT_copied"), q + 1)
                    for b in range(2):
                        for n in range(2):
                            two_halves(4 + b, k_tile(xb), ring_unit(v + 2 * b + n, turns), 4 * n)\
                                .then_inc(sem("unit_used"), 1)
                    if not last_one:
                        pe.wait_ge(sem("sgat_ready"), q + 2)
                        gather().then_inc(sem("gather_done"), 1)
                    pe.wait_ge(sem("h_ready"), q + 1)
                    turn_blocks(7, hmid).then_inc(sem("hT_turned"), 1)
                    if not last_one:
                        pe.wait_ge(sem("ssc_ready"), q + 2)
                        turn_blocks(4, tra[:, 128:128 + TT * P], 2).then_inc(sem("sw_turned"), 1)
                        pe.wait_ge(sem("xrows_copied"), q + 2)
                        turn_blocks(6, xrows).then_inc(sem("x_turned"), 1)
                        pe.wait_ge(sem("xT_copied"), q + 2)
                    pe.wait_ge(sem("hTt_copied"), q + 1)
                    for n in range(2):
                        two_halves(6, k_tile(hTt), ring_unit(v + 4 + n, turns), 4 * n).then_inc(sem("unit_used"), 1)
                    pe.wait_ge(sem("ys_copied"), q + 1)
                    scatter(swT[j % 2]).then_inc(sem("scattered"), 1)

                def broadcasts(what):
                    if (1, 0) in what:
                        pe.wait_ge(sem("terms_ready"), 1)
                        mm(bank(7, 0, NMOD), cst[0:NMOD, C_ID + 2:C_ID + 2 + NMOD], row_b, start=True, stop=True)\
                            .then_inc(sem("terms_moved"), 1)
                        pe.wait_ge(sem("rows_ready"), DEPTH + 1)
                    for row in what:
                        b = BC.index(row)
                        pe.wait_ge(sem("mod_ready"), b - 1)
                        broadcast(b, 5 if b % 2 else 7)
                    pe.wait_ge(sem("mod_ready"), b + 1)

                def pool_unit(v):
                    pe.wait_ge(sem("pool_loaded"), 16)
                    landed(pe, v)
                    w = slot(ring_slot(v)[0])
                    pw = w[:, 0:2048].rearrange("p (k n) -> p k n", k=KT)
                    bd = w[:, 2048:4096].rearrange("p (k g n) -> p k g n", k=TT, g=4)
                    keep_clock(4, 14)
                    pe.wait_ge(sem("tokens_ready"), 2 * TT)
                    for g in range(4):
                        for k in range(2):
                            kk = 2 * g + k
                            for t in range(TT):
                                last = mm(bank(ROUTE[g], 0, P, k * TOK, (k + 1) * TOK),
                                          h2[:, t * D + kk * P:t * D + kk * P + P], bd[:, t, g, :],
                                          start=(t == 0), stop=(t == TT - 1), skip_group_check=True)
                        last.then_inc(sem("poolT_done"), 1)
                    for t in range(TT):
                        for h in range(2):
                            pe.wait_ge(sem("poolT_copied"), 2 * h + 2 if t == 0 else 4)
                            for g in (2 * h, 2 * h + 1):
                                for k in range(2):
                                    last = mm(bank(2 * t + h, 0, P, (g % 2) * TOK, (g % 2 + 1) * TOK),
                                              poolT[:, 2 * g + k, t * P:t * P + P], pw[:, 2 * g + k, :],
                                              start=(k == 0), stop=(k == 1), skip_group_check=True)
                            last.then_inc(sem("unit_used" if (t, h) == (1, 1) else "mix_done"), 1)

                def further_experts():
                    def body(n, e):
                        pe.wait_ge(sem(f"x{layer}_sel"), n + 1)
                        gather()
                        turn_blocks(4, tra[:, 128:128 + TT * P], 2).then_inc(sem(f"x{layer}_gathered"), 1)
                        pe.wait_ge(sem(f"x{layer}_rows"), n + 1)
                        turn_blocks(6, xrows).then_inc(sem(f"x{layer}_xturned"), 1)
                        pe.wait_ge(sem(f"x{layer}_in"), n + 1)
                        pe.wait_ge(sem(f"x{layer}_loaded"), n * (16 * EU) + 16 * EU)
                        for b in range(2):
                            for u in range(2):
                                last = two_halves(4 + b, k_tile(xT[0]),
                                                  slot(2 * b + u).rearrange("p (k n) -> p k n", k=4), 4 * u)
                        last.then_inc(sem(f"x{layer}_up"), 1)
                        pe.wait_ge(sem(f"x{layer}_h"), n + 1)
                        turn_blocks(7, hmid).then_inc(sem(f"x{layer}_turned"), 1)
                        pe.wait_ge(sem(f"x{layer}_hT"), n + 1)
                        for u in range(2):
                            last = two_halves(6, k_tile(hTt), slot(4 + u).rearrange("p (k n) -> p k n", k=4), 4 * u)
                        last.then_inc(sem(f"x{layer}_down"), 1)
                        pe.wait_ge(sem(f"x{layer}_ys"), n + 1)
                        scatter(swT[0]).then_inc(sem(f"x{layer}_scattered"), 1)

                    def first():
                        pe.drain().then_inc(sem(f"x{layer}_down"), 1)
                        pe.drain().then_inc(sem(f"x{layer}_scattered"), 1)
                    further(pe, layer, None, body, first)
                    pe.drain().then_inc(sem("further_done"), 1)

                walk(pe, layer, expert, broadcasts, pool_unit, further_experts)

        @block.scalar
        def _(act):
            def bank(b, n0=0, n1=NB):
                return ps[:, b, n0:n1]

            def load(dst, src, s):
                act.dma_start(dst, src).then_inc(sem(s), 16)

            def load_ln(n):
                load(lng, ln_g[n // 2, n % 2].partition_broadcast(P), "ln_loaded")
                load(lnb, ln_b[n // 2, n % 2].partition_broadcast(P), "ln_loaded")

            load(mod[:, 5 * D:5 * D + 256], rope, "attn_small_loaded")
            load(lamb, attn_lam[0].rearrange("a b -> (a b)").partition_broadcast(P), "attn_small_loaded")
            load(subln, attn_subln[0].partition_broadcast(P), "attn_small_loaded")
            load(rw[:, :].rearrange("p (k n) -> p k n", k=KT)[:, :, 0:NE], router_w.rearrange("(k p) n -> p k n", p=P), "router_loaded")
            load(rb[:, :], router_b.partition_broadcast(P), "router_loaded")
            load(rows[1][:, :], mod_b[1].rearrange("(m n) -> m n", n=NB), "rows_loaded_1")

            act.wait_ge(sem("c_loaded"), 32)
            nc.scalar.activation(csig, crow, ACT.Sigmoid).then_inc(sem("csig_ready"), 1)
            for m in range(4):
                act.wait_ge(sem("modc_done"), m + 1)
                nc.scalar.copy(modc[:, m * NB:(m + 1) * NB], bank(2 + 4 * (m % 2))).then_inc(sem("modc_ready"), 1)
            for part in range(2 * KEYT):
                i, b = part // 2, part % 2
                act.wait_ge(sem("hT_done"), part + 1)
                nc.scalar.copy(hT[:, 4 * b:4 * b + 4, i * P:i * P + P],
                               bank(4 + part % 4).rearrange("p (k t) -> p k t", k=4)).then_inc(sem("hT_copied"), 1)

            def evacuate(g):
                kind, j, t = GROUPS[g]
                if EVAC[g][0] != "act":
                    return
                group_done(act, g)
                if kind == "v":
                    dst = vv[:, t, j * NB:(j + 1) * NB]
                else:
                    n = QK_N[g]
                    act.wait_ge(sem("qkT_done"), n - 1)
                    dst = nat[n % 2]
                nc.scalar.copy(dst, bank(g % 2)).then_inc(sem("qkv_out_act"), 1)

            def copy_turned(g):
                if g in QK_N:
                    kind, j, t = GROUPS[g]
                    act.wait_ge(sem("qkT_done"), QK_N[g] + 1)
                    src = bank(6).rearrange("p (h t) -> p h t", h=HPJ)
                    if kind == "k":
                        last = nc.scalar.copy(kT[:, HPJ * j:HPJ * (j + 1), t * P:t * P + P], src)
                    else:
                        for n in range(2):
                            last = nc.scalar.copy(qT[j][HD * n:HD * n + HD, n, :, t * P:t * P + P],
                                                  src[HD * n:HD * n + HD])
                    last.then_inc(sem("qkT_copied"), 1)

            act.wait_ge(sem("lam_sums"), 1)
            nc.scalar.activation(lam[:, 2:4], lam[:, 0:2], ACT.Exp).then_inc(sem("lam_exp"), 1)
            for g in range(10):
                evacuate(g)
                if g:
                    copy_turned(g - 1)
            prev = 9
            def heads_std(t):
                act.wait_ge(sem("ss_ready"), t + 1)
                nc.scalar.activation(ors[:, t, :], ss[:, t, :], ACT.Sqrt).then_inc(sem("ostd_ready"), 1)

            def copy_heads(t):
                for b in range(2):
                    act.wait_ge(sem("oT_done"), 2 * t + b + 1)
                    nc.scalar.copy(oT[t][:, 4 * b:4 * b + 4, :],
                                   bank((6, 4)[t] + b).rearrange("p (k t) -> p k t", k=4)).then_inc(sem("oT_copied"), 1)

            for s in range(NS + 3):
                for kind, i in FILL[s]:
                    if kind == "g":
                        evacuate(i)
                        copy_turned(prev)
                        prev = i
                if s < NS:
                    act.wait_ge(sem("nb_ready"), s + 1)
                    for n in range(2):
                        nc.scalar.activation(pr[s % 2][:, n, :], bank(score_bank(s) + n), ACT.Exp,
                                             bias=nb[:, s % 2, n:n + 1], scale=SCALE,
                                             accum_out=sm[:, s % 2, n:n + 1]).then_inc(sem("exp_done"), 1)
                    if s == NS - 1:
                        load_ln(0)
                if 2 <= s < NS + 2:
                    act.wait_ge(sem("aT_done"), s - 1)
                    nc.scalar.copy(aT[s % 2], bank(4)).then_inc(sem("aT_copied"), 1)
                if s >= 3:
                    j, t, h = STEPS[s - 3]
                    hh = HPJ * j + h
                    act.wait_ge(sem("pv_done"), s - 2)
                    nc.scalar.activation(bank(5, P, 2 * P), bank(5, 0, P), ACT.Square,
                                         accum_out=ss[:, t, hh:hh + 1]).then_inc(sem("o_squared"), 1)
                    nc.scalar.copy(osb[:, t, hh * P:hh * P + P], bank(5, 0, P)).then_inc(sem("o_copied"), 1)
                if s == NS - 1:
                    heads_std(0)
                if s == NS:
                    copy_heads(0)
            heads_std(1)
            copy_heads(1)

            def std(n):
                for t in range(TT):
                    act.wait_ge(sem("var_ready"), TT * n + t + 1)
                    nc.scalar.activation(mv[:, 4 * t + 3:4 * t + 4], mv[:, 4 * t + 2:4 * t + 3], ACT.Sqrt).then_inc(sem("std_ready"), 1)

            def load_norms():
                act.wait_ge(sem("rows_cleared"), 1)
                two = lambda a: a.rearrange("(m n) -> m n", n=NB)
                for row, n in ((2 * SC1, 1), (2 * SC2, 2)):
                    load(row_g[row:row + 2, :], two(ln_g[n // 2, n % 2]), "joins_loaded")
                    load(row_b[row:row + 2, :], two(ln_b[n // 2, n % 2]), "joins_loaded")
                load(row_g[2 * G1:2 * G1 + 2, :], two(pool_scale[0]), "joins_loaded")
                act.wait_ge(sem("xl_done"), TT)
                load_ln(1)

            std(0)
            for layer in range(DEPTH):
                q0 = NE * layer
                for part in range(2 * TT):
                    t, b = part // 2, part % 2
                    act.wait_ge(sem("h2T_done"), 4 * layer + part + 1)
                    nc.scalar.copy(h2T[:, 4 * b:4 * b + 4, t * P:t * P + P],
                                   bank((4, 6, 5, 7)[part]).rearrange("p (k t) -> p k t", k=4))\
                        .then_inc(sem("h2T_copied"), 1)
                act.wait_ge(sem("parts_done"), layer + 1)
                nc.scalar.copy(lparts, bank(4, 0, TOK)).then_inc(sem("parts_copied"), 1)
                act.wait_ge(sem("rmax_ready"), layer + 1)
                for t in range(TT):
                    nc.scalar.activation(prob[:, t, :], prob[:, t, :], ACT.Exp, bias=col[:, t:t + 1],
                                         accum_out=col[:, 2 + t:3 + t]).then_inc(sem("rexp_done"), 1)
                act.wait_ge(sem("gather_done"), q0 + 1)
                nc.scalar.copy(xrows, bank(6)).then_inc(sem("xrows_copied"), 1)
                act.wait_ge(sem("x_turned"), q0 + 1)
                nc.scalar.copy(work[:, 0:NB], bank(6)).then_inc(sem("xT_copied"), 1)
                if layer == 0:
                    load_norms()

                def expert(e, j, v, turns, last_one):
                    q = e + q0
                    used(act, v + 1, turns)
                    nc.scalar.activation(sig, bank(4), ACT.Sigmoid).then_inc(sem("sig_ready"), 1)
                    if not last_one:
                        act.wait_ge(sem("gather_done"), q + 2)
                        nc.scalar.copy(xrows, bank(6)).then_inc(sem("xrows_copied"), 1)
                        act.wait_ge(sem("x_turned"), q + 2)
                        b = (j + 1) % 2
                        nc.scalar.copy(work[:, b * NB:(b + 1) * NB], bank(6)).then_inc(sem("xT_copied"), 1)
                    used(act, v + 5, turns)
                    nc.scalar.copy(ysb, bank(6)).then_inc(sem("ys_copied"), 1)

                def pool_unit(v):
                    std(1)
                    for g in range(4):
                        act.wait_ge(sem("poolT_done"), g + 1)
                        nc.scalar.copy(work[:, g * NB:(g + 1) * NB], bank((4, 6, 5, 7)[g]))\
                            .then_inc(sem("poolT_copied"), 1)
                    act.wait_ge(sem("xl_done"), 2 * TT)
                    load_ln(2)
                    std(2)

                def further_experts():
                    def body(n, e):
                        act.wait_ge(sem(f"x{layer}_up"), n + 1)
                        nc.scalar.activation(sig, bank(4), ACT.Sigmoid).then_inc(sem(f"x{layer}_sig"), 1)
                    further(act, layer, None, body)

                def broadcasts(what):
                    if layer == 1:
                        act.wait_ge(sem("xl_done"), 3 * TT)
                        load_ln(3)

                walk(act, layer, expert, broadcasts, pool_unit, further_experts)
            std(3)

        @block.vector
        def _(dve):
            v_ = nc.vector
            chain = [0]

            def link(ins):
                chain[0] += 1
                ins.then_inc(sem("dve_chain"), 1)
                dve.wait_ge(sem("dve_chain"), chain[0])

            def bank(b, n0=0, n1=NB):
                return ps[:, b, n0:n1]

            for q_ in qT:
                v_.memset(q_[HD:P, 0, :, :], 0.0)
                v_.memset(q_[0:HD, 1, :, :], 0.0).then_inc(sem("q_cleared"), 1)
            v_.memset(rw[:, :].rearrange("p (k n) -> p k n", k=KT)[:, :, NE:32], 0.0).then_inc(sem("rw_padded"), 1)
            dve.wait_ge(sem("csig_ready"), 1)
            v_.tensor_tensor(crow, crow, csig, ALU.mult).then_inc(sem("crow_ready"), 1)
            dve.wait_ge(sem("ccol_done"), 1)
            csv = cs[:, :].rearrange("p (k n) -> p k n", k=KT)
            for b in range(2):
                v_.tensor_copy(csv[:, :, 16 * b:16 * b + 16],
                               bank(7, KT * b, KT * b + KT).unsqueeze(2).to_broadcast([P, KT, 16]))\
                    .then_inc(sem("cs_ready"), 1)

            def picker(b, row):
                if b >= 2:
                    dve.wait_ge(sem("bc_done"), min(b, len(BC)) - 1)
                return v_.tensor_copy(pick[:, (b % 2) * P:(b % 2 + 1) * P],
                                      cst[0:NMOD, C_ID + row:C_ID + row + 1].to_broadcast([NMOD, P]))

            def broadcast_out(b, bk):
                layer, m = BC[b]
                dve.wait_ge(sem("bc_done"), b + 1)
                one = 0.0 if layer == 1 or m // 2 in (SH1, SH2) else 1.0
                v_.tensor_scalar(mod[:, m * NB:(m + 1) * NB], bank(bk), one, None, ALU.add).then_inc(sem("mod_ready"), 1)

            dve.wait_ge(sem("consts_loaded"), 16)
            for m in range(4 + 1):
                if m < 4:
                    if m >= 2:
                        dve.wait_ge(sem("modc_done"), m - 1)
                    picker(m, m).then_inc(sem("pick_ready"), 1)
                    early_used(dve, ("mod", m))
                    v_.tensor_copy(modp[:, (m % 2) * NB:(m % 2 + 1) * NB], bank(3 * (m % 2)))\
                        .then_inc(sem("modp_copied"), 1)
                if m:
                    broadcast_out(m - 1, 1 + 4 * ((m - 1) % 2))

            def unit_sum(n):
                dve.wait_ge(sem(f"sum_loaded_{n % 2}"), 16 * (n // 2 + 1))
                if n >= 2:
                    dve.wait_ge(sem("row_done"), n - 1)
                w = slot(2 + n % 2).rearrange("p (k n) -> p k n", k=KT)
                acc = modp[:, (n % 2) * NB:(n % 2 + 1) * NB]
                for k in range(KT):
                    ck = cs[:, 32 * k:32 * k + 1]
                    if k == 0:
                        ins = v_.tensor_scalar(acc, w[:, 0, :], ck, None, ALU.mult)
                    else:
                        ins = v_.scalar_tensor_tensor(out=acc, in0=w[:, k, :], scalar=ck, in1=acc, op0=ALU.mult,
                                                      op1=ALU.add)
                    if k < KT - 1:
                        link(ins)
                ins.then_inc(sem("summed"), 1)

            def rows_sum(layer):
                dve.wait_ge(sem("row_done"), (SUMS0, NSUM)[layer])
                dve.wait_ge(sem(f"rows_loaded_{layer}"), 16)
                r_ = rows[layer][0:NMOD, :]
                v_.tensor_tensor(r_, r_, ps[0:NMOD, 7, :], ALU.add).then_inc(sem("rows_ready"), 1)

            dve.wait_ge(sem("mod_ready"), 4)
            dve.wait_ge(sem("x_loaded"), 16)
            dve.wait_ge(sem("ctx_loaded"), 16)
            for i in range(KEYT):
                if i < TT:
                    link(v_.tensor_tensor(hnat[:, i, :], xl[:, i * D:(i + 1) * D], mod[:, D:2 * D], ALU.mult))
                else:
                    dve.wait_ge(sem("modc_ready"), 4)
                    link(v_.scalar_tensor_tensor(out=hnat[:, i, :], in0=modc[:, D:2 * D], scalar=1.0,
                                                 in1=cin[:, i - TT, :], op0=ALU.add, op1=ALU.mult))
                v_.tensor_tensor(hnat[:, i, :], hnat[:, i, :], (mod if i < TT else modc)[:, 0:D], ALU.add)\
                    .then_inc(sem("hnat_ready"), 1)
            dve.wait_ge(sem("attn_small_loaded"), 48)
            lv = lamb.rearrange("p (a b n) -> p a b n", a=2, b=2)
            link(v_.tensor_tensor(ltmp.rearrange("p (a n) -> p a n", a=2), lv[:, :, 0, :], lv[:, :, 1, :], ALU.mult))
            v_.tensor_reduce(lam[:, 0:2], ltmp.rearrange("p (a n) -> p a n", a=2), AX, ALU.add)\
                .then_inc(sem("lam_sums"), 1)
            link(v_.tensor_scalar(subln, subln, 1.0 - LAM_INIT, None, ALU.mult))
            dve.wait_ge(sem("hnat_ready"), KEYT)

            def evacuate(g):
                if EVAC[g][0] != "dve":
                    return
                kind, j, t = GROUPS[g]
                n = QK_N[g]
                group_done(dve, g)
                if n >= 2:
                    dve.wait_ge(sem("qkT_done"), n - 1)
                if EVAC[g][1]:
                    dve.wait_ge(sem("qkv_out_dve"), EVAC[g][1])
                heads = 2 * HPJ
                src = bank(g % 2)
                c_ = ropes[:, t, 0, :].unsqueeze(1).to_broadcast([P, heads, HD])
                v_.tensor_tensor(rtmp[0].rearrange("p (h n) -> p h n", h=heads), src.rearrange("p (h n) -> p h n", h=heads),
                                 c_, ALU.mult)
                q4 = HD // 4
                view = src.rearrange("p (h a b n) -> p h a b n", h=heads, a=2, b=2)
                dst = rtmp[1].rearrange("p (h a b n) -> p h a b n", h=heads, a=2, b=2)
                sn = ropes[:, t, 1, :].rearrange("p (a b n) -> p a b n", a=2, b=2)
                for a in range(2):
                    for b in range(2):
                        last = v_.tensor_tensor(dst[:, :, a, b, :], view[:, :, a, 1 - b, :],
                                                sn[:, a, b, :].unsqueeze(1).to_broadcast([P, heads, q4]), ALU.mult)
                link(last)
                v_.tensor_tensor(nat[n % 2], rtmp[0], rtmp[1], ALU.add).then_inc(sem("qkv_out_dve"), 1)

            for g in range(10):
                evacuate(g)
                unit_sum(g)
            def norm_heads(t):
                dve.wait_ge(sem("o_copied"), NS - (TT - 1 - t) * HPJ)
                dve.wait_ge(sem("o_squared"), NS - (TT - 1 - t) * HPJ)
                v_.tensor_scalar(ss[:, t, :], ss[:, t, :], 1.0 / P, EPS, ALU.mult, ALU.add).then_inc(sem("ss_ready"), 1)
                dve.wait_ge(sem("ostd_ready"), t + 1)
                link(v_.reciprocal(ors[:, t, :], ors[:, t, :]))
                o3 = osb[:, t, :].rearrange("p (h n) -> p h n", h=HEADS)
                link(v_.tensor_tensor(o3, o3, ors[:, t, :].unsqueeze(2).to_broadcast([P, HEADS, P]), ALU.mult))
                v_.tensor_tensor(o3, o3, subln.unsqueeze(1).to_broadcast([P, HEADS, P]), ALU.mult)\
                    .then_inc(sem("o_normed"), 1)

            rows_sum(0)
            dve.wait_ge(sem("lam_exp"), 1)
            link(v_.tensor_tensor(lam[:, 4:5], lam[:, 3:4], lam[:, 2:3], ALU.subtract))
            link(v_.tensor_scalar(lam[:, 5:6], lam[:, 4:5], -LAM_INIT, None, ALU.add))
            for s in range(NS + 1):
                for kind, i in FILL[s]:
                    if kind == "g":
                        evacuate(i)
                if s < NS:
                    b = s % 2
                    dve.wait_ge(sem("scores_done"), s + 1)
                    link(v_.tensor_reduce(mx[:, b, :], ps[:, score_bank(s):score_bank(s) + 2, :], AX, ALU.max))
                    v_.tensor_scalar(nb[:, b, :], mx[:, b, :], -SCALE, None, ALU.mult).then_inc(sem("nb_ready"), 1)
                if s:
                    b = (s - 1) % 2
                    dve.wait_ge(sem("exp_done"), 2 * s)
                    link(v_.reciprocal(rs[:, b, :], sm[:, b, :]))
                    link(v_.tensor_tensor(rl[:, b:b + 1], rs[:, b, 1:2], lam[:, 5:6], ALU.mult))
                    link(v_.tensor_scalar(pr[b][:, 1, :], pr[b][:, 1, :], rl[:, b:b + 1], None, ALU.mult))
                    if s >= 3:
                        dve.wait_ge(sem("aT_done"), s - 2)
                    v_.scalar_tensor_tensor(out=att[b], in0=pr[b][:, 0, :], scalar=rs[:, b, 0:1], in1=pr[b][:, 1, :],
                                            op0=ALU.mult, op1=ALU.add).then_inc(sem("att_ready"), 1)
                if 10 + s < NSUM:
                    unit_sum(10 + s)
                if s == 11:
                    rows_sum(1)
                if s in PICK_AT:
                    picker(PICK_AT[s], BC[PICK_AT[s]][1]).then_inc(sem("pick_ready"), 1)
                for i in OUT_AT.get(s, ()):
                    broadcast_out(i, BC_BANK[i])
                if s == NS - 1:
                    norm_heads(0)
            v_.memset(row_b, 0.0)
            v_.memset(row_g, 1.0).then_inc(sem("rows_cleared"), 1)
            norm_heads(1)

            def fuse(shift, scale):
                dve.wait_ge(sem("ln_loaded"), 32)
                sc_, sh_ = mod[:, scale * D:(scale + 1) * D], mod[:, shift * D:(shift + 1) * D]
                z = h2[:, D:2 * D]
                link(v_.tensor_tensor(z, sc_, lnb, ALU.mult))
                link(v_.tensor_tensor(sh_, sh_, z, ALU.add))
                link(v_.tensor_tensor(sc_, sc_, lng, ALU.mult))

            def join_rows():
                dve.wait_ge(sem("joins_loaded"), 5 * 16)
                r_ = rows[1][:, :]
                link(v_.tensor_scalar(r_, r_, cst[0:NMOD, C_PLUS:C_PLUS + 1], None, ALU.add))
                v_.tensor_tensor(row_b, row_b, r_, ALU.mult).then_inc(sem("terms_ready"), 1)
                dve.wait_ge(sem("terms_ready"), 1)
                link(v_.tensor_tensor(r_, r_, row_g, ALU.mult))
                dve.wait_ge(sem("terms_moved"), 1)
                v_.tensor_tensor(r_, r_, ps[0:NMOD, 7, :], ALU.add).then_inc(sem("rows_ready"), 1)

            def deepnorm(n, ready, gate, shift=None, scale=None):
                def tokens(t):
                    z = xl[:, t * D:(t + 1) * D]
                    for h in range(2):
                        c0, c1 = h * NB, (h + 1) * NB
                        ready(t, h)
                        y = h2[:, t * D + c0:t * D + c1]
                        link(v_.tensor_tensor(y, bank(2 * t + h), mod[:, gate * D + c0:gate * D + c1], ALU.mult))
                        link(v_.scalar_tensor_tensor(out=z[:, c0:c1], in0=z[:, c0:c1], scalar=ALPHA, in1=y,
                                                     op0=ALU.mult, op1=ALU.add))
                        link(v_.bn_stats(stat[:, 6 * h:6 * h + 6], z[:, c0:c1]))
                    m_ = mv[:, 4 * t:4 * t + 4]
                    link(v_.bn_aggr(m_[:, 0:2], stat[:, 0:12]))
                    v_.tensor_scalar(m_[:, 2:3], m_[:, 1:2], EPS, None, ALU.add).then_inc(sem("var_ready"), 1)
                    if scale is not None:
                        hh = h2[:, t * D:(t + 1) * D]
                        link(v_.scalar_tensor_tensor(out=hh, in0=z, scalar=m_[:, 0:1],
                                                     in1=mod[:, scale * D:(scale + 1) * D], op0=ALU.subtract, op1=ALU.mult))
                    dve.wait_ge(sem("std_ready"), TT * n + t + 1)
                    link(v_.reciprocal(m_[:, 2:3], m_[:, 3:4]))
                    if scale is not None:
                        v_.scalar_tensor_tensor(out=hh, in0=hh, scalar=m_[:, 2:3], in1=mod[:, shift * D:(shift + 1) * D],
                                                op0=ALU.mult, op1=ALU.add).then_inc(sem("tokens_ready"), 1)

                for t in range(TT):
                    tokens(t)
                    if scale is None:
                        stream(n, t)

            def stream(n, t):
                dve.wait_ge(sem("ln_loaded"), 32 * (n + 1))
                z, m_ = xl[:, t * D:(t + 1) * D], mv[:, 4 * t:4 * t + 4]
                link(v_.scalar_tensor_tensor(out=z, in0=z, scalar=m_[:, 0:1], in1=lng, op0=ALU.subtract, op1=ALU.mult))
                v_.scalar_tensor_tensor(out=z, in0=z, scalar=m_[:, 2:3], in1=lnb, op0=ALU.mult, op1=ALU.add)\
                    .then_inc(sem("xl_done"), 1)

            def slots_of(e, io, s_gat, s_sc, n_gat=None):
                for t in range(TT):
                    last = v_.tensor_scalar(sgat[:, t, :], io[:, 0:SLOTS], small[:, bass.ds(e + (128 + NE * t), 1)], None,
                                            ALU.is_equal)
                if s_gat is not None:
                    last.then_inc(s_gat, 1)
                if n_gat is not None:
                    n_gat()
                for t in range(TT):
                    last = v_.tensor_scalar(ssc[:, t, :], io[:, 0:P], small[:, bass.ds(e + (128 + NE * t), 1)],
                                            small[:, bass.ds(e + (64 + NE * t), 1)], ALU.is_equal, ALU.mult)
                last.then_inc(s_sc, 1)

            iota = cst[:, C_IOTA:C_IOTA + P]

            def route(layer):
                dve.wait_ge(sem("logits_done"), layer + 1)
                dve.wait_ge(sem("router_loaded"), 32)
                g8 = [P, TT * NG, EG, EG]
                link(v_.tensor_tensor(prob, bank(5, 0, TT * NE).rearrange("p (t e) -> p t e", t=TT),
                                      rb[:, :].unsqueeze(1).to_broadcast([P, TT, NE]), ALU.add))
                link(v_.tensor_reduce(col[:, 0:2], prob, AX, ALU.max))
                v_.tensor_scalar(col[:, 0:2], col[:, 0:2], -1.0, None, ALU.mult).then_inc(sem("rmax_ready"), 1)
                dve.wait_ge(sem("rexp_done"), TT * (layer + 1))
                link(v_.reciprocal(col[:, 2:4], col[:, 2:4]))
                link(v_.tensor_tensor(prob, prob, col[:, 2:4].unsqueeze(2).to_broadcast([P, TT, NE]), ALU.mult))
                pg = small[:, 0:32].rearrange("p (g j) -> p g j", j=EG)
                over_k, over_j = pg.unsqueeze(2).to_broadcast(g8), pg.unsqueeze(3).to_broadcast(g8)
                pa = pair_a.rearrange("p (g j k) -> p g j k", j=EG, k=EG)
                pb = pair_b.rearrange("p (g j k) -> p g j k", j=EG, k=EG)
                lt = cst[:, C_LT:C_SUM].rearrange("p (j k) -> p j k", j=EG)
                v_.tensor_tensor(pa, over_k, over_j, ALU.is_gt)
                link(v_.tensor_tensor(pb, over_k, over_j, ALU.is_equal))
                link(v_.tensor_tensor(pb, pb, lt.unsqueeze(1).to_broadcast(g8), ALU.mult))
                link(v_.tensor_tensor(pa, pa, pb, ALU.add))
                link(v_.tensor_reduce(rt, pa, AX, ALU.add))
                link(v_.tensor_scalar(sel, rt, float(2), None, ALU.is_lt))
                link(v_.tensor_tensor(wgt, sel, prob, ALU.mult))
                link(v_.tensor_reduce(gs, small[:, 64:96].rearrange("p (g j) -> p g j", j=EG), AX, ALU.add))
                link(v_.tensor_reduce(col[:, 4:6], gs, AX, ALU.max))
                link(v_.tensor_tensor(gs, gs, col[:, 4:6].unsqueeze(2).to_broadcast([P, TT, NG]), ALU.is_equal))
                g2_ = [P, TT, NG, NG]
                pc = pair[:, 0:TT * NG * NG].rearrange("p (t g k) -> p t g k", t=TT, g=NG)
                link(v_.tensor_tensor(pc, gs.unsqueeze(2).to_broadcast(g2_), lt.unsqueeze(1).to_broadcast(g2_), ALU.mult))
                link(v_.tensor_reduce(gt2, pc, AX, ALU.add))
                link(v_.scalar_tensor_tensor(out=gs, in0=gt2, scalar=0.0, in1=gs, op0=ALU.is_equal, op1=ALU.mult))
                ge = small[:, 160:168].unsqueeze(2).to_broadcast([P, TT * NG, EG])
                sg, wg_ = (small[:, a:a + 32].rearrange("p (g j) -> p g j", j=EG) for a in (32, 64))
                v_.tensor_tensor(sg, sg, ge, ALU.mult).then_inc(sem("sel_ready"), 1)
                link(v_.tensor_tensor(wg_, wg_, ge, ALU.mult))
                link(v_.tensor_reduce(col[:, 6:8], wgt, AX, ALU.add))
                link(v_.reciprocal(col[:, 6:8], col[:, 6:8]))
                link(v_.tensor_tensor(wgt, wgt, col[:, 6:8].unsqueeze(2).to_broadcast([P, TT, NE]), ALU.mult))
                v_.memset(tra[:, 128:128 + TT * P], 0.0).then_inc(sem("ssc_zeroed"), 1)
                dve.wait_ge(sem("rank_done"), layer + 1)
                link(v_.scalar_tensor_tensor(out=rt, in0=bank(6, 0, TT * NE).rearrange("p (t e) -> p t e", t=TT), scalar=1.0,
                                             in1=sel, op0=ALU.add, op1=ALU.mult))
                link(v_.tensor_scalar(rt, rt, -1.0, None, ALU.add))
                link(v_.tensor_reduce(col[:, 8:9], bank(6, TT * NE, (TT + 1) * NE), AX, ALU.max))
                for n in range(1, TOK // SLOTS):
                    last = v_.tensor_scalar(col[:, 3 + n:4 + n], col[:, 8:9], float(n * SLOTS), None, ALU.is_gt)
                link(last)
                link(v_.tensor_tensor(col[:, 4:5], col[:, 4:5], col[:, 5:6], ALU.add))
                link(v_.tensor_tensor(nchunk[:, :], col[:, 4:5], col[:, 6:7], ALU.add))
                v_.tensor_copy(iota_x[:, :], iota).then_inc(sem("routed"), 1)
                dve.wait_ge(sem("acc_open"), 4 * (layer + 1))

            fuse(SH2, SC2)
            deepnorm(0, lambda t, h: mixed(dve, 0, t, h), G1, SH2, SC2)
            for layer in range(DEPTH):
                q0 = NE * layer
                route(layer)
                slots_of(0, iota, sem("sgat_ready"), sem("ssc_ready"))
                dve.wait_ge(sem("sw_turned"), q0 + 1)
                v_.tensor_copy(swT[0], bank(4, 0, TT * P)).then_inc(sem("swT_copied"), 1)
                if layer == 0:
                    for t in range(TT):
                        stream(0, t)

                def expert(e, j, v, turns, last_one):
                    q = e + q0
                    if not last_one:
                        dve.wait_ge(sem("gather_done"), q + 1)
                        slots_of(e + 1, iota, sem("sgat_ready"), sem("ssc_ready"),
                                 lambda: dve.wait_ge(sem("sw_turned"), q + 1))
                    dve.wait_ge(sem("sig_ready"), q + 1)
                    v_.tensor_tensor(hmid, bank(4), sig, ALU.mult).then_inc(sem("silu_ready"), 1)
                    dve.wait_ge(sem("silu_ready"), q + 1)
                    used(dve, v + 3, turns)
                    v_.tensor_tensor(hmid, hmid, bank(5), ALU.mult).then_inc(sem("h_ready"), 1)
                    dve.wait_ge(sem("hT_turned"), q + 1)
                    v_.tensor_copy(work[:, 3 * NB:4 * NB], bank(7)).then_inc(sem("hTt_copied"), 1)
                    if not last_one:
                        dve.wait_ge(sem("sw_turned"), q + 2)
                        v_.tensor_copy(swT[(j + 1) % 2], bank(4, 0, TT * P)).then_inc(sem("swT_copied"), 1)

                def broadcasts(what):
                    first, end = BC.index(what[0]), BC.index(what[-1]) + 1
                    if (1, 0) in what:
                        join_rows()
                    for b in range(first, end, 2):
                        for b2 in (b, b + 1):
                            picker(b2, BC[b2][1]).then_inc(sem("pick_ready"), 1)
                        for b2 in (b, b + 1):
                            broadcast_out(b2, 5 if b2 % 2 else 7)
                    if layer == 1:
                        for t in range(TT):
                            stream(2, t)

                def pool_unit(v):
                    deepnorm(2, lambda t, h: mixed(dve, 1, t, h), G1, SH2, SC2)

                def further_experts():
                    ci_now = [0]

                    def chunk(ci):
                        ci_now[0] = ci
                        v_.tensor_scalar(iota_x[:, :], iota_x[:, :], float(SLOTS), None, ALU.add)\
                            .then_inc(sem(f"x{layer}_iota"), 1)

                    def body(n, e):
                        x_ = f"x{layer}_"
                        dve.wait_ge(sem(x_ + "iota"), ci_now[0] + 1)
                        dve.wait_ge(sem(x_ + "scattered"), n + 1)
                        slots_of(e, iota_x, None, sem(x_ + "sel"))
                        dve.wait_ge(sem(x_ + "gathered"), n + 1)
                        v_.tensor_copy(xrows, bank(6)).then_inc(sem(x_ + "rows"), 1)
                        v_.tensor_copy(swT[0], bank(4, 0, TT * P))
                        dve.wait_ge(sem(x_ + "xturned"), n + 1)
                        v_.tensor_copy(work[:, 0:NB], bank(6)).then_inc(sem(x_ + "in"), 1)
                        dve.wait_ge(sem(x_ + "sig"), n + 1)
                        v_.tensor_tensor(hmid, bank(4), sig, ALU.mult).then_inc(sem(x_ + "silu"), 1)
                        dve.wait_ge(sem(x_ + "silu"), n + 1)
                        v_.tensor_tensor(hmid, hmid, bank(5), ALU.mult).then_inc(sem(x_ + "h"), 1)
                        dve.wait_ge(sem(x_ + "turned"), n + 1)
                        v_.tensor_copy(work[:, 3 * NB:4 * NB], bank(7)).then_inc(sem(x_ + "hT"), 1)
                        dve.wait_ge(sem(x_ + "down"), n + 2)
                        v_.tensor_copy(ysb, bank(6)).then_inc(sem(x_ + "ys"), 1)
                    dve.wait_ge(sem("scattered"), NE * (layer + 1))
                    further(dve, layer, chunk, body,
                            end=lambda: dve.wait_ge(sem("further_done"), layer + 1))
                    if layer == 0:
                        deepnorm(1, lambda t, h: None, G2, SH1, SC1)
                        for t in range(TT):
                            stream(1, t)

                walk(dve, layer, expert, broadcasts, pool_unit, further_experts)
            deepnorm(3, lambda t, h: None, G2)


_INS = ["x", "c", "ctx", "c_ctx", "mod_w", "mod_b", "ln_g", "ln_b", "attn_wqkv", "attn_wo", "attn_lam", "attn_subln",
        "pool_w", "pool_scale", "router_w", "router_b", "moe_wg", "moe_wu", "moe_wd"]


def kernel(**inputs):
    import concourse.bacc as bacc
    import numpy as np
    from concourse.bass_utils import run_bass_kernel_spmd

    nc = bacc.Bacc("TRN2", target_bir_lowering=False, num_devices=1)
    given = {name: np.ascontiguousarray(inputs[name]) for name in _INS}
    given.update(constants())
    arrays, args = {}, []
    for name, a in given.items():
        arrays[f"in_{name}"] = a
        args.append(nc.dram_tensor(f"in_{name}", a.shape, mybir.dt.from_np(a.dtype), kind="ExternalInput").ap())
    args.append(nc.dram_tensor("out_latent", (1, TOK, D), F32, kind="ExternalOutput").ap())
    trunk(nc, *args)
    r = run_bass_kernel_spmd(nc, [arrays], core_ids=[0])
    return r.results[0]["out_latent"]
```
